# Optimizing a Trainium2 kernel written in Bass

```python
import math
import jax
import jax.numpy as jnp
from jax import lax
import numpy as np
import jax, jax.numpy as jnp

D_MODEL = 1024
BATCH = 1
SEQ = 256
DEPTH = 2

HG_HEADS = 4
HG_DK = 128
HG_DV = 128
HG_F = HG_HEADS * HG_DK
HG_V = HG_HEADS * HG_DV
HG_CHUNK = 64
SB_HEADS = 8
SB_DH = 64
SB_W = SB_HEADS * SB_DH
SB_BLOCK = 128
PEER_HEADS = 8
PEER_NKEYS = 128
PEER_N = PEER_NKEYS * PEER_NKEYS
PEER_DKEY = 128
PEER_TOPK = 16
PEER_TOK_BLOCK = 16
DN_ALPHA = (2.0 * DEPTH) ** 0.25
DN_BETA = (8.0 * DEPTH) ** -0.25
LN_EPS = 1e-5
RMS_EPS = 1e-6
IN_SIZES = (HG_F, HG_F, HG_V, HG_V, SB_W, SB_W, SB_W, D_MODEL, D_MODEL)
IN_WIDTH = sum(IN_SIZES)
IN_SPLITS = tuple(int(s) for s in np.cumsum(IN_SIZES)[:-1])


def layer_norm(x, g, b):
    xf = x.astype(jnp.float32)
    mu = jnp.mean(xf, axis=-1, keepdims=True)
    var = jnp.mean(jnp.square(xf - mu), axis=-1, keepdims=True)
    return (xf - mu) * lax.rsqrt(var + LN_EPS) * g + b

def head_rms_norm(o, g):
    of = o.astype(jnp.float32)
    return of * lax.rsqrt(jnp.mean(jnp.square(of), axis=-1, keepdims=True) + RMS_EPS) * g

def hgrn2_chunkwise(q, f_logit, v, lb):
    B, S, H, DK = q.shape
    DV = v.shape[-1]
    C = HG_CHUNK
    NC = S // C
    q = q.astype(jnp.float32)
    z = f_logit.astype(jnp.float32)
    v = v.astype(jnp.float32)
    lb = lb.reshape(H, DK)
    log_f = jnp.log(lb + (1.0 - lb) * jax.nn.sigmoid(z))
    k = (1.0 - lb) * jax.nn.sigmoid(-z)

    def chunks(a):
        return a.reshape(B, NC, C, H, a.shape[-1]).transpose(1, 0, 3, 2, 4)

    qc, kc, vc, gc = chunks(q), chunks(k), chunks(v), chunks(log_f)
    bc = jnp.cumsum(gc, axis=3)
    tri = jnp.tril(jnp.ones((C, C), dtype=bool))[:, :, None]

    def step(state, inp):
        q_, k_, v_, b_ = inp
        b_end = b_[:, :, -1:, :]
        inter = jnp.einsum('bhtd,bhde->bhte', q_ * jnp.exp(b_), state)
        diff = b_[:, :, :, None, :] - b_[:, :, None, :, :]
        decay = jnp.where(tri, jnp.exp(jnp.where(tri, diff, 0.0)), 0.0)
        scores = jnp.einsum('bhtd,bhsd,bhtsd->bhts', q_, k_, decay)
        intra = jnp.einsum('bhts,bhse->bhte', scores, v_)
        new_state = (jnp.exp(b_end[:, :, 0, :])[..., None] * state
                     + jnp.einsum('bhsd,bhse->bhde', k_ * jnp.exp(b_end - b_), v_))
        return new_state, inter + intra

    state0 = jnp.zeros((B, H, DK, DV), jnp.float32)
    _, o = lax.scan(step, state0, (qc, kc, vc, bc))
    return o.transpose(1, 0, 3, 2, 4).reshape(B, S, H, DV)

def stick_breaking_attention(q, k, v):
    B, S, H, d = q.shape
    scale = 1.0 / math.sqrt(d)
    qh = q.astype(jnp.float32).transpose(0, 2, 1, 3)
    kh = k.astype(jnp.float32).transpose(0, 2, 1, 3)
    vh = v.astype(jnp.float32).transpose(0, 2, 1, 3)
    outs = []
    for blk in range(S // SB_BLOCK):
        t0 = blk * SB_BLOCK
        t1 = t0 + SB_BLOCK
        z = jnp.einsum('bhtd,bhsd->bhts', qh[:, :, t0:t1], kh[:, :, :t1]) * scale
        tpos = t0 + jnp.arange(SB_BLOCK)[:, None]
        spos = jnp.arange(t1)[None, :]
        causal = spos < tpos
        log_1mb = jnp.where(causal, jax.nn.log_sigmoid(-z), 0.0)
        after = lax.cumsum(log_1mb, axis=3, reverse=True) - log_1mb
        w = jnp.where(causal, jnp.exp(jax.nn.log_sigmoid(z) + after), 0.0)
        outs.append(jnp.einsum('bhts,bhsd->bhtd', w, vh[:, :, :t1]))
    o = jnp.concatenate(outs, axis=2)
    return o.transpose(0, 2, 1, 3)

def peer_ffn(h, w_pq, sub_keys, peer_u, peer_v):
    B, S, D = h.shape
    half = PEER_DKEY // 2
    q = (h @ w_pq).reshape(B, S, PEER_HEADS, 2, half).astype(jnp.float32)
    s1 = jnp.einsum('bshd,hnd->bshn', q[..., 0, :], sub_keys[0].astype(jnp.float32))
    s2 = jnp.einsum('bshd,hnd->bshn', q[..., 1, :], sub_keys[1].astype(jnp.float32))
    v1, i1 = lax.top_k(s1, PEER_TOPK)
    v2, i2 = lax.top_k(s2, PEER_TOPK)
    cand = (v1[..., :, None] + v2[..., None, :]).reshape(B, S, PEER_HEADS, PEER_TOPK * PEER_TOPK)
    cand_idx = (i1[..., :, None] * PEER_NKEYS + i2[..., None, :]).reshape(B, S, PEER_HEADS, PEER_TOPK * PEER_TOPK)
    top, pos = lax.top_k(cand, PEER_TOPK)
    idx = jnp.take_along_axis(cand_idx, pos, axis=-1)
    gates = jax.nn.softmax(top, axis=-1)

    T = PEER_TOK_BLOCK
    nb = S // T

    def blockify(a):
        return a.reshape((B, nb, T) + a.shape[2:]).swapaxes(0, 1)

    def expert_block(args):
        hb, ib, gb = args
        u = peer_u[ib]
        act = jax.nn.gelu(jnp.einsum('btd,bthkd->bthk', hb, u), approximate=False)
        return jnp.einsum('bthk,bthkd->btd', gb * act, peer_v[ib])

    out = lax.map(expert_block, (blockify(h), blockify(idx), blockify(gates)))
    return out.swapaxes(0, 1).reshape(B, S, D)

def first_inputs(seed: int = 0) -> dict:
    key = jax.random.key(seed)
    ks = jax.random.split(key, 16)
    nrm = jax.random.normal
    f32 = jnp.float32
    D = D_MODEL
    return {
        "x": nrm(ks[0], (BATCH, SEQ, D), f32),
        "c": nrm(ks[1], (BATCH, D), f32),
        "w_ada": nrm(ks[2], (DEPTH, D, 6 * D), f32) * (0.5 * D ** -0.5),
        "b_ada": nrm(ks[3], (DEPTH, 6 * D), f32) * 0.01,
        "w_in": nrm(ks[4], (DEPTH, D, IN_WIDTH), f32) * D ** -0.5,
        "lb_logits": nrm(ks[5], (DEPTH, HG_F), f32) * 0.1,
        "hg_norm_g": 1.0 + 0.02 * nrm(ks[6], (DEPTH, HG_V), f32),
        "w_up_a": nrm(ks[7], (DEPTH, HG_V, D), f32) * HG_V ** -0.5,
        "w_up_b": nrm(ks[8], (DEPTH, SB_W, D), f32) * SB_W ** -0.5,
        "w_o": nrm(ks[9], (DEPTH, D, D), f32) * (DN_BETA * D ** -0.5),
        "w_pq": nrm(ks[10], (DEPTH, D, PEER_HEADS * PEER_DKEY), f32) * D ** -0.5,
        "sub_keys": nrm(ks[11], (DEPTH, 2, PEER_HEADS, PEER_NKEYS, PEER_DKEY // 2), f32) * (PEER_DKEY // 2) ** -0.5,
        "peer_u": nrm(ks[12], (DEPTH, PEER_N, D), f32) * D ** -0.5,
        "peer_v": nrm(ks[13], (DEPTH, PEER_N, D), f32) * DN_BETA,
        "ln_g": 1.0 + 0.02 * nrm(ks[14], (DEPTH, 2, D), f32),
        "ln_b": 0.02 * nrm(ks[15], (DEPTH, 2, D), f32),
    }

def first_block(x, c, w_ada, b_ada, w_in, lb_logits, hg_norm_g, w_up_a, w_up_b, w_o,
              w_pq, sub_keys, peer_u, peer_v, ln_g, ln_b):
    B, S, _ = x.shape
    p = jax.nn.softmax(lb_logits.astype(jnp.float32), axis=0)
    lower_bounds = jnp.cumsum(p, axis=0) - p[0:1]
    cond = jax.nn.silu(c)
    for l in range(DEPTH):
        mod = cond @ w_ada[l] + b_ada[l]
        sh1, sc1, gt1, sh2, sc2, gt2 = jnp.split(mod, 6, axis=-1)

        hm = x * (1.0 + sc1[:, None]) + sh1[:, None]
        proj = hm @ w_in[l]
        qa, fa, ia, ga, qb, kb, vb, gate_a, gate_b = jnp.split(proj, IN_SPLITS, axis=-1)
        oa = hgrn2_chunkwise(qa.reshape(B, S, HG_HEADS, HG_DK),
                             fa.reshape(B, S, HG_HEADS, HG_DK),
                             ia.reshape(B, S, HG_HEADS, HG_DV),
                             lower_bounds[l])
        oa = head_rms_norm(oa, hg_norm_g[l].reshape(HG_HEADS, HG_DV)).reshape(B, S, HG_V) * jax.nn.silu(ga)
        ob = stick_breaking_attention(qb.reshape(B, S, SB_HEADS, SB_DH),
                                      kb.reshape(B, S, SB_HEADS, SB_DH),
                                      vb.reshape(B, S, SB_HEADS, SB_DH)).reshape(B, S, SB_W)
        merged = jax.nn.sigmoid(gate_a) * (oa @ w_up_a[l]) + jax.nn.sigmoid(gate_b) * (ob @ w_up_b[l])
        y = (merged @ w_o[l]) * gt1[:, None]
        x = layer_norm(DN_ALPHA * x + y, ln_g[l, 0], ln_b[l, 0])

        hf = x * (1.0 + sc2[:, None]) + sh2[:, None]
        y = peer_ffn(hf, w_pq[l], sub_keys[l], peer_u[l], peer_v[l]) * gt2[:, None]
        x = layer_norm(DN_ALPHA * x + y, ln_g[l, 1], ln_b[l, 1])
    return x


GRID_W = 64
CTX_LEN = 256
N_MIXERS = 2
N_HEADS = 16
N_KV_HEADS = 4
HEAD_DIM = D_MODEL // N_HEADS
GROUP = N_HEADS // N_KV_HEADS
Q_DIM = N_HEADS * HEAD_DIM
KV_DIM = N_KV_HEADS * HEAD_DIM
WINDOW = 128
BLOCK = 128
ROPE_THETA = 10000.0
ROPE_QUARTER = HEAD_DIM // 4
CONV_WIDTH = 3
D_FF = 2816
N_MOD = 9
NEG_INF = -1e30
HALF_STEP = 0.5


def rmsnorm(x, g):
    xf = x.astype(jnp.float32)
    y = xf * lax.rsqrt(jnp.mean(xf * xf, axis=-1, keepdims=True) + RMS_EPS)
    return (y * g.astype(jnp.float32)).astype(x.dtype)

def adaln_in(x, g, shift, scale):
    return rmsnorm(x, g) * (1 + scale) + shift

def adaln_out(x, y, g, gate, weight):
    return x + weight * gate * rmsnorm(y, g)

def swiglu(h, w_gu, w_down):
    gu = h @ w_gu
    return (jax.nn.silu(gu[..., :D_FF]) * gu[..., D_FF:]) @ w_down

def ffn_sublayer(x, mod, k, g_pre, g_post, w_gu, w_down):
    h = adaln_in(x, g_pre, mod[k], mod[k + 1])
    return adaln_out(x, swiglu(h, w_gu, w_down), g_post, mod[k + 2], HALF_STEP)

def short_conv_mixer(h, w_in, w_conv, w_out):
    bcu = h @ w_in
    b, cg, u = bcu[..., :D_MODEL], bcu[..., D_MODEL:2 * D_MODEL], bcu[..., 2 * D_MODEL:]
    up = jnp.pad(cg * u, ((0, 0), (1, 1), (0, 0)))
    y = w_conv[0] * up[:, :-2] + w_conv[1] * up[:, 1:-1] + w_conv[2] * up[:, 2:]
    return (b * y) @ w_out

def axial_rope_tables(n_tokens, dtype):
    rows = n_tokens // GRID_W
    row = jnp.broadcast_to(jnp.arange(rows)[:, None], (rows, GRID_W)).reshape(-1).astype(jnp.float32)
    col = jnp.broadcast_to(jnp.arange(GRID_W)[None, :], (rows, GRID_W)).reshape(-1).astype(jnp.float32)
    inv_freq = ROPE_THETA ** (-jnp.arange(ROPE_QUARTER, dtype=jnp.float32) / ROPE_QUARTER)
    ang = jnp.stack([row[:, None] * inv_freq, col[:, None] * inv_freq], axis=1)
    return jnp.cos(ang)[:, None].astype(dtype), jnp.sin(ang)[:, None].astype(dtype)

def apply_rope(t, cos, sin):
    t4 = t.reshape(t.shape[:-1] + (2, 2, ROPE_QUARTER))
    x1, x2 = t4[..., 0, :], t4[..., 1, :]
    out = jnp.stack([x1 * cos - x2 * sin, x2 * cos + x1 * sin], axis=-2)
    return out.reshape(t.shape)

def banded_blocks(t, nb):
    B = t.shape[0]
    tp = jnp.pad(t, ((0, 0), (BLOCK, BLOCK), (0, 0), (0, 0)))
    tp = tp.reshape(B, nb + 2, BLOCK, N_KV_HEADS, HEAD_DIM)
    return jnp.concatenate([tp[:, :-2], tp[:, 1:-1], tp[:, 2:]], axis=2)

def band_mask(nb, n_tokens):
    a = jnp.arange(BLOCK)[:, None]
    b = jnp.arange(3 * BLOCK)[None, :]
    off = b - a
    in_win = (off >= BLOCK - WINDOW) & (off <= BLOCK + WINDOW)
    key_pos = (jnp.arange(nb)[:, None] - 1) * BLOCK + b
    valid = (key_pos >= 0) & (key_pos < n_tokens)
    return in_win[None] & valid[:, None, :]

def window_attention_mixer(hx, hz, w_qkv, w_o, sink, cos, sin, ctx_queries):
    B, S, _ = hx.shape
    C = hz.shape[1]
    nb = S // BLOCK
    nk = 3 * BLOCK
    scale = HEAD_DIM ** -0.5
    qkv = hx @ w_qkv
    q = apply_rope(qkv[..., :Q_DIM].reshape(B, S, N_HEADS, HEAD_DIM), cos, sin) * scale
    k = apply_rope(qkv[..., Q_DIM:Q_DIM + KV_DIM].reshape(B, S, N_KV_HEADS, HEAD_DIM), cos, sin)
    v = qkv[..., Q_DIM + KV_DIM:].reshape(B, S, N_KV_HEADS, HEAD_DIM)
    kvz = hz @ w_qkv[:, Q_DIM:]
    kz = kvz[..., :KV_DIM].reshape(B, C, N_KV_HEADS, HEAD_DIM)
    vz = kvz[..., KV_DIM:].reshape(B, C, N_KV_HEADS, HEAD_DIM)
    sink_l = sink.reshape(N_KV_HEADS, GROUP).astype(jnp.float32)

    qb = q.reshape(B, nb, BLOCK, N_KV_HEADS, GROUP, HEAD_DIM)
    kb = banded_blocks(k, nb)
    vb = banded_blocks(v, nb)
    s_win = jnp.einsum('bnqhgd,bnkhd->bnhgqk', qb, kb).astype(jnp.float32)
    s_win = jnp.where(band_mask(nb, S)[None, :, None, None], s_win, NEG_INF)
    s_ctx = jnp.einsum('bnqhgd,bchd->bnhgqc', qb, kz).astype(jnp.float32)
    s_sink = jnp.broadcast_to(sink_l[None, None, :, :, None, None], s_win.shape[:-1] + (1,))
    p = jax.nn.softmax(jnp.concatenate([s_win, s_ctx, s_sink], axis=-1), axis=-1).astype(v.dtype)
    o = (jnp.einsum('bnhgqk,bnkhd->bnqhgd', p[..., :nk], vb)
         + jnp.einsum('bnhgqc,bchd->bnqhgd', p[..., nk:nk + C], vz))
    yx = o.reshape(B, S, Q_DIM) @ w_o

    yz = None
    if ctx_queries:
        qz = (hz @ w_qkv[:, :Q_DIM]).reshape(B, C, N_KV_HEADS, GROUP, HEAD_DIM) * scale
        sz = jnp.einsum('bqhgd,bkhd->bhgqk', qz, kz).astype(jnp.float32)
        sz_sink = jnp.broadcast_to(sink_l[None, :, :, None, None], sz.shape[:-1] + (1,))
        pz = jax.nn.softmax(jnp.concatenate([sz, sz_sink], axis=-1), axis=-1).astype(vz.dtype)
        oz = jnp.einsum('bhgqk,bkhd->bqhgd', pz[..., :C], vz)
        yz = oz.reshape(B, C, Q_DIM) @ w_o
    return yx, yz

def second_inputs(seed: int = 0) -> dict:
    key = jax.random.key(seed)
    ks = jax.random.split(key, 16)
    n_conv = (DEPTH + 1) // N_MIXERS
    n_attn = DEPTH // N_MIXERS

    def w(k, shape, fan_in, gain=1.0):
        return gain * fan_in ** -0.5 * jax.random.normal(k, shape, jnp.float32)

    return {
        'x': jax.random.normal(ks[0], (BATCH, SEQ, D_MODEL), jnp.float32),
        'c': jax.random.normal(ks[1], (BATCH, D_MODEL), jnp.float32),
        'ctx': jax.random.normal(ks[2], (BATCH, CTX_LEN, D_MODEL), jnp.float32),
        'c_ctx': jax.random.normal(ks[3], (D_MODEL,), jnp.float32),
        'w_mod': w(ks[4], (DEPTH, D_MODEL, N_MOD * D_MODEL), D_MODEL, 0.5),
        'b_mod': 0.02 * jax.random.normal(ks[5], (DEPTH, N_MOD * D_MODEL), jnp.float32),
        'norm_g': 1.0 + 0.05 * jax.random.normal(ks[6], (DEPTH, 6, D_MODEL), jnp.float32),
        'ffn_w_gu': w(ks[7], (DEPTH, 2, D_MODEL, 2 * D_FF), D_MODEL),
        'ffn_w_down': w(ks[8], (DEPTH, 2, D_FF, D_MODEL), D_FF),
        'conv_w_in': w(ks[9], (n_conv, D_MODEL, 3 * D_MODEL), D_MODEL),
        'conv_w': w(ks[10], (n_conv, CONV_WIDTH, D_MODEL), CONV_WIDTH),
        'conv_w_out': w(ks[11], (n_conv, D_MODEL, D_MODEL), D_MODEL),
        'attn_w_qkv': w(ks[12], (n_attn, D_MODEL, Q_DIM + 2 * KV_DIM), D_MODEL),
        'attn_w_o': w(ks[13], (n_attn, Q_DIM, D_MODEL), Q_DIM),
        'attn_sink': 0.5 * jax.random.normal(ks[14], (n_attn, N_HEADS), jnp.float32),
    }

def second_block(x, c, ctx, c_ctx, w_mod, b_mod, norm_g, ffn_w_gu, ffn_w_down,
              conv_w_in, conv_w, conv_w_out, attn_w_qkv, attn_w_o, attn_sink):
    B, S, D = x.shape
    cos, sin = axial_rope_tables(S, x.dtype)
    z = ctx
    for i in range(DEPTH):
        last = i == DEPTH - 1
        use_attn = (i % N_MIXERS) == 1
        j = i // N_MIXERS
        g = norm_g[i]
        mx = (jax.nn.silu(c) @ w_mod[i] + b_mod[i]).reshape(B, N_MOD, 1, D).transpose(1, 0, 2, 3)
        mz = (jax.nn.silu(c_ctx) @ w_mod[i] + b_mod[i]).reshape(N_MOD, D)
        ctx_needed = (not last) or use_attn

        x = ffn_sublayer(x, mx, 0, g[0], g[1], ffn_w_gu[i, 0], ffn_w_down[i, 0])
        if ctx_needed:
            z = ffn_sublayer(z, mz, 0, g[0], g[1], ffn_w_gu[i, 0], ffn_w_down[i, 0])

        hx = adaln_in(x, g[2], mx[3], mx[4])
        if use_attn:
            hz = adaln_in(z, g[2], mz[3], mz[4])
            yx, yz = window_attention_mixer(hx, hz, attn_w_qkv[j], attn_w_o[j], attn_sink[j],
                                            cos, sin, not last)
        else:
            yx = short_conv_mixer(hx, conv_w_in[j], conv_w[j], conv_w_out[j])
            yz = None
            if not last:
                hz = adaln_in(z, g[2], mz[3], mz[4])
                yz = short_conv_mixer(hz, conv_w_in[j], conv_w[j], conv_w_out[j])
        x = adaln_out(x, yx, g[3], mx[5], 1.0)

        x = ffn_sublayer(x, mx, 6, g[4], g[5], ffn_w_gu[i, 1], ffn_w_down[i, 1])
        if not last:
            z = adaln_out(z, yz, g[3], mz[5], 1.0)
            z = ffn_sublayer(z, mz, 6, g[4], g[5], ffn_w_gu[i, 1], ffn_w_down[i, 1])
    return x


def setup_inputs(seed=0):
    out = dict(first_inputs(seed))
    for name, value in second_inputs(seed + 1).items():
        if name != "x":
            out[name + "_2"] = value
    return out


def reference(
    x, c, w_ada, b_ada, w_in, lb_logits, hg_norm_g, w_up_a, w_up_b, w_o, w_pq, sub_keys, peer_u,
    peer_v, ln_g, ln_b, c_2, ctx_2, c_ctx_2, w_mod_2, b_mod_2, norm_g_2, ffn_w_gu_2,
    ffn_w_down_2, conv_w_in_2, conv_w_2, conv_w_out_2, attn_w_qkv_2, attn_w_o_2, attn_sink_2,
):
    x = first_block(
        x, c, w_ada, b_ada, w_in, lb_logits, hg_norm_g, w_up_a, w_up_b, w_o, w_pq, sub_keys,
        peer_u, peer_v, ln_g, ln_b,
    )
    return second_block(
        x, c_2, ctx_2, c_ctx_2, w_mod_2, b_mod_2, norm_g_2, ffn_w_gu_2, ffn_w_down_2,
        conv_w_in_2, conv_w_2, conv_w_out_2, attn_w_qkv_2, attn_w_o_2, attn_sink_2,
    )


_drawn_inputs = setup_inputs


def setup_inputs(seed=0):
    import zlib

    import numpy as np

    out = dict(_drawn_inputs(seed))
    spreads = {}
    factors = {'b_ada': 4.563, 'lb_logits': 8.0, 'hg_norm_g': 32.316, 'attn_sink_2': 8.0}
    for name, (base, spread) in spreads.items():
        noise = np.random.default_rng([zlib.crc32(name.encode()), seed]).standard_normal(out[name].shape)
        drawn = base * np.exp(spread * noise) if base else spread * noise
        out[name] = jnp.asarray(drawn.astype(out[name].dtype))
    for name, factor in factors.items():
        out[name] = (out[name] * factor).astype(out[name].dtype)
    return out
```

```python
import math
from contextlib import ExitStack

import numpy as np

import concourse.bass as bass
from concourse import mybir

F32 = mybir.dt.float32
U32 = mybir.dt.uint32
ALU = mybir.AluOpType
ACT = mybir.ActivationFunctionType
AX_X = mybir.AxisListType.X

P = 128
D = 1024
KC = D // P
SEQ = 256
TT = SEQ // P
DEPTH = 2
DN_ALPHA = (2.0 * DEPTH) ** 0.25
LN_EPS = 1e-5
RMS_EPS = 1e-6

HG_HEADS = 4
SB_HEADS = 8
SB_DH = 64
PEER_HEADS = 8
TOPK = 16
NKEYS = 128
HALF_KEY = 64
SLOTS = PEER_HEADS * TOPK

D_FF = 2816
FC = D_FF // P
HD = 64
NQ = 16
NKV = 4
NEG = -1e30

RING = 4
TILE = 4096
LEVELS = (64, 32, 16, 8, 4, 2, 1)


class Signal:

    def __init__(self, sem):
        self.sem = sem
        self.base = 0

    def at(self, k):
        return self.base + k


class Steps:

    def __init__(self, eng, count):
        self.eng, self.count, self.n = eng, count, count.base

    def tick(self, ins):
        ins.then_inc(self.count.sem, 1)
        self.n += 1
        self.count.base = self.n

    def wait(self):
        self.eng.wait_ge(self.count.sem, self.n)

    def link(self, ins):
        self.tick(ins)
        self.wait()

    def loop(self, turns, per_turn, body):
        start = self.n
        with self.eng.Fori(0, turns) as i:
            self.n = start + i * per_turn
            body(i)
        self.n = self.count.base = start + turns * per_turn


def in_turns(eng, n, period, body):
    turns = n // period
    if turns > 1:
        with eng.Fori(0, turns) as i:
            for j in range(period):
                body(i * period + j, j, i)
    elif turns:
        for j in range(period):
            body(j, j, 0)
    for j in range(n - turns * period):
        body(turns * period + j, j, turns)


class WeightStream:

    def __init__(self, ring, ready, used):
        self.ring, self.ready, self.used = ring, ready, used
        self.groups = []
        self.at_group = 0

    def add(self, name, n, width, shape, source):
        first = sum(g[1] for g in self.groups)
        self.groups.append((name, n, width, shape, source, first))

    def begin(self, name):
        group = self.groups[self.at_group]
        assert group[0] == name, (name, group[0])

    def end(self):
        self.used.base += self.groups[self.at_group][1]
        self.at_group += 1

    def view(self, j):
        _, _, width, shape, _, first = self.groups[self.at_group]
        return self.ring[:, (first + j) % RING, 0:width].rearrange(shape[0], **shape[1])

    def landed(self, pe, j, turn, period):
        first = self.groups[self.at_group][5]
        pe.wait_ge(self.ready[(first + j) % RING],
                   32 * ((first + j) // RING + 1) + turn * (32 * period // RING))

    def _load(self, sp, group, t, j):
        _, _, width, shape, source, first = group
        slot = (first + j) % RING
        if not (isinstance(t, int) and first + t < RING):
            sp.wait_ge(self.used.sem, first + t - RING + 1)
        dst = self.ring[:, slot, 0:width].rearrange(shape[0], **shape[1])
        parts = source(t)
        if isinstance(parts, list):
            for k, part in enumerate(parts):
                sp.dma_start(dst[:, :, k, :], part).then_inc(self.ready[slot], 16)
        else:
            sp.dma_start(dst, parts).then_inc(self.ready[slot], 32)

    def prime(self, sp):
        for t in range(min(RING, self.groups[0][1])):
            self._load(sp, self.groups[0], t, t)

    def feed(self, sp):
        group = self.groups[self.at_group]
        n, left = group[1], max(group[1] - RING, 0)
        turns = left // RING
        if turns > 1:
            with sp.Fori(1, turns + 1) as i:
                for j in range(RING):
                    self._load(sp, group, i * RING + j, j)
        else:
            for t in range(RING, RING + turns * RING):
                self._load(sp, group, t, t)
        for t in range(RING + turns * RING, n):
            self._load(sp, group, t, t)
        if self.at_group + 1 < len(self.groups):
            after = self.groups[self.at_group + 1]
            for t in range(min(RING, after[1])):
                self._load(sp, after, t, t)


def columns(w, cols, width=512):
    v = w.rearrange("(c p) n -> p c n", p=P)
    if isinstance(cols, range):
        return lambda t: v[:, :, bass.ds(t * cols.step + cols.start, width)]
    return lambda t: v[:, :, cols[t]:cols[t] + width]


WIDE = ("p (c n) -> p c n", {"c": KC})


def build(nc, a, out):
    ctx = ExitStack()
    with ctx:
        _build(nc, ctx, a, out)


def _build(nc, ctx, a, out):
    def sb(name, shape, dt=F32):
        return ctx.enter_context(nc.sbuf_tensor(name, shape, dt))

    def signal(name):
        return Signal(ctx.enter_context(nc.semaphore(name)))

    ring = sb("ring", [P, RING, TILE])
    x_tok = sb("x_tok", [P, TT, D])
    z_tok = sb("z_tok", [P, TT, D])
    y_tok = sb("y_tok", [P, TT, D])
    hT = sb("hT", [P, KC, SEQ])
    ident = sb("ident", [P, P])
    tri = sb("tri", [P, P])
    before = sb("before", [P, P])
    before_neg = sb("before_neg", [P, P])
    ones = sb("ones", [P, P])
    level_mask = sb("level_mask", [P, len(LEVELS) + 1, P], U32)
    iota16 = sb("iota16", [P, TOPK])
    vcol = sb("vcol", [P, 4, P])
    condT = sb("condT", [P, KC, 1])
    cond2T = sb("cond2T", [P, KC, 2])
    adacol = sb("adacol", [P, DEPTH, 48])
    modcol = sb("modcol", [P, DEPTH, 72, 2])
    scol = sb("scol", [P, KC])
    bcol = sb("bcol", [P, KC])
    lbcol = sb("lbcol", [P, DEPTH, 2, HG_HEADS])
    stat = sb("stat", [P, 64])
    rows = sb("rows", [P, 3, D])
    context_kT = sb("context_kT", [P, 4, SEQ])
    context_v = sb("context_v", [P, TT, NKV * HD])
    arena_size = 20480
    arena = sb("arena", [P, arena_size])
    ps = ctx.enter_context(nc.psum_tensor("ps", [P, 4, 1024], F32))

    def carve(*shapes):
        at, out_ = 0, []
        for shape in shapes:
            n = math.prod(shape)
            v = arena[:, at:at + n]
            if len(shape) > 1:
                names = [f"d{i}" for i in range(len(shape))]
                v = v.rearrange(f"p ({' '.join(names)}) -> p {' '.join(names)}",
                                **{m: s for m, s in zip(names[1:], shape[1:])})
            out_.append(v)
            at += n
        assert at <= arena_size, at
        return out_

    tile_done = signal("tile_done")
    unit_free = [signal(f"unit_free_{u}") for u in range(2)]
    vec_step = signal("vec_step")
    act_step = signal("act_step")
    pool_step = signal("pool_step")
    loaded = signal("loaded")
    stored = signal("stored")
    pe_done = signal("pe_done")
    vec_ready = signal("vec_ready")
    act_ready = signal("act_ready")
    cols_ready = signal("cols_ready")
    ready = [ctx.enter_context(nc.semaphore(f"tile_landed_{s}")) for s in range(RING)]
    GR = 8
    row_landed = [signal(f"rows_landed_{s}") for s in range(GR)]
    row_used = signal("row_used")
    turned = signal("turned")
    summed = signal("summed")
    diag_ready = signal("diag_ready")

    weights = WeightStream(ring, ready, tile_done)

    def w(name, l):
        return a[name][l]

    CHUNK_KV = 2 * 512
    for l in range(DEPTH):
        weights.add(f"ada{l}", 12, TILE, WIDE, columns(w("w_ada", l), range(0, 6144, 512)))
    for l in range(DEPTH):
        weights.add(f"mod{l}", 18, TILE, WIDE, columns(w("w_mod_2", l), range(0, 9216, 512)))
    for l in range(DEPTH):
        weights.add(f"in{l}", 11, TILE, WIDE, columns(
            w("w_in", l), [0, 512, 2048, 2560, 1024, 1536, 3072, 3584, 4096, 4608, 5120]))
        up = [w("w_up_a", l), w("w_up_b", l)]
        weights.add(f"up{l}", 2, TILE, ("p (c n) -> p c n", {"c": 4}),
                    lambda t, up=up: up[t].rearrange("(c p) n -> p c n", p=P))
        weights.add(f"o{l}", 2, TILE, WIDE, columns(w("w_o", l), range(0, 1024, 512)))
        weights.add(f"pq{l}", 2, TILE, WIDE, columns(w("w_pq", l), range(0, 1024, 512)))

    def add_ffn(name, l, k):
        gu = a["ffn_w_gu_2"][l, k].rearrange("(c p) (two f) -> p c two f", p=P, two=2)
        down = a["ffn_w_down_2"][l, k].rearrange("(h c p) n -> p h c n", p=P, h=2)
        weights.add(f"gu_{name}", 11, TILE, ("p (c two f) -> p c two f", {"c": KC, "two": 2}),
                    lambda t: [gu[:, :, two, bass.ds(t * 256, 256)] for two in range(2)])
        weights.add(f"down_{name}", 8, 11 * 256, ("p (c n) -> p c n", {"c": 11}),
                    lambda t: down[:, t % 2, :, (t // 2) * 256:(t // 2) * 256 + 256])

    def add_conv(name):
        weights.add(f"conv_{name}", 6, TILE, WIDE,
                    columns(a["conv_w_in_2"][0], range(0, 3072, 512)))
        weights.add(f"convout_{name}", 2, TILE, WIDE,
                    columns(a["conv_w_out_2"][0], range(0, 1024, 512)))

    for s in "zx":
        add_ffn(f"{s}00", 0, 0)
        add_conv(s)
        add_ffn(f"{s}01", 0, 1)
        add_ffn(f"{s}10", 1, 0)
        if s == "z":
            weights.add("kv_z", 1, TILE, WIDE, columns(a["attn_w_qkv_2"][0], [CHUNK_KV]))
    weights.add("qkv", 3, TILE, WIDE, columns(a["attn_w_qkv_2"][0], range(0, 1536, 512)))
    weights.add("attn_o", 2, TILE, WIDE, columns(a["attn_w_o_2"][0], range(0, 1024, 512)))
    add_ffn("x11", 1, 1)

    vrows = carve((4, P))[0]
    V_C, V_C2, V_CCTX, V_BADA = 0, 8, 16, 24
    V_BMOD = 0
    V_LB, V_HGG = 0, 8
    V_NG, V_CW = 16, 112
    with nc.Block() as block:
        @block.sync
        def _(sp):
            def small(dst, src):
                sp.dma_start(dst, src).then_inc(loaded.sem, 16)
                loaded.base += 16
            small(vrows[V_C:V_C + 8, 0, :], a["c"].rearrange("a (r p) -> (a r) p", p=P))
            small(vrows[V_C2:V_C2 + 8, 0, :], a["c_2"].rearrange("a (r p) -> (a r) p", p=P))
            small(vrows[V_CCTX:V_CCTX + 8, 0, :], a["c_ctx_2"].rearrange("(r p) -> r p", p=P))
            small(vrows[V_BADA:V_BADA + 96, 0, :], a["b_ada"].rearrange("l (r p) -> (l r) p", p=P))
            for l in range(DEPTH):
                small(vrows[0:72, 1 + l, :], a["b_mod_2"][l].rearrange("(r p) -> r p", p=P))
            small(vrows[V_LB:V_LB + 8, 3, :], a["lb_logits"].rearrange("l (r p) -> (l r) p", p=P))
            small(vrows[V_HGG:V_HGG + 8, 3, :], a["hg_norm_g"].rearrange("l (r p) -> (l r) p", p=P))
            small(vrows[V_NG:V_NG + 96, 3, :], a["norm_g_2"].rearrange("l k (r p) -> (l k r) p", p=P))
            cw = a["conv_w_2"][0].rearrange("k (r p) -> (k r) p", p=P)
            small(vrows[V_CW:V_CW + 16, 3, :], cw[0:16, :])
            small(vrows[72:80, 1, :], cw[16:24, :])
            small(ident[:], a["k_ident"])
            small(tri[:], a["k_tri"])
            small(before[:], a["k_before"])
            small(before_neg[:], a["k_before_neg"])
            small(level_mask[:], a["k_levels"])
            small(iota16[:], a["k_iota16"])
            small(x_tok[:], a["x"][0].rearrange("(t p) d -> p t d", p=P))
            small(z_tok[:], a["ctx_2"][0].rearrange("(t p) d -> p t d", p=P))
            weights.prime(sp)

        group_rows = (120, 80, 72, 128)

        @block.tensor
        def _(pe):
            pe.wait_ge(loaded.sem, loaded.base)
            for g, n in enumerate(group_rows):
                pe.transpose(ps[:, 0, g * P:g * P + n], vrows[0:n, g, :], ident[0:n, 0:n]) \
                    .then_inc(pe_done.sem, 1)

        @block.scalar
        def _(act):
            act.wait_ge(vec_ready.sem, vec_ready.at(1))
            act.activation(condT[:, :, 0], vcol[:, 0, V_C:V_C + 8], ACT.Silu)
            for k, at in enumerate((V_C2, V_CCTX)):
                act.activation(cond2T[:, :, k], vcol[:, 0, at:at + 8], ACT.Silu)

        @block.vector
        def _(dve):
            v = Steps(dve, vec_step)
            v.tick(dve.memset(ones[:], 1.0))
            dve.wait_ge(pe_done.sem, pe_done.at(4))
            for g, n in enumerate(group_rows):
                ins = dve.tensor_copy(vcol[:, g, 0:n], ps[:, 0, g * P:g * P + n])
                if g < 3:
                    v.tick(ins)
            ins.then_inc(vec_ready.sem, 1)
            dve.wait_ge(vec_ready.sem, vec_ready.at(1))
            v.tick(dve.memset(lbcol[:, 0, 0, :], 0.0))
            v.link(dve.tensor_tensor(lbcol[:, 1, 0, :], vcol[:, 3, V_LB:V_LB + 4],
                                     vcol[:, 3, V_LB + 4:V_LB + 8], ALU.subtract))
            for u in range(2):
                dve.memset(stat[:, u:u + 1], 0.0).then_inc(unit_free[u].sem, 1)
            dve.memset(stat[:, 2:3], 0.0).then_inc(row_used.sem, GR)

    pe_done.base += 4
    vec_ready.base += 1

    with nc.Block() as block:
        @block.scalar
        def _(act):
            s = Steps(act, act_step)
            s.link(act.activation(lbcol[:, 1, 0, :], lbcol[:, 1, 0, :], ACT.Sigmoid, scale=-1.0))

        @block.vector
        def _(dve):
            dve.wait_ge(act_step.sem, act_step.base)
            for l in range(DEPTH):
                dve.tensor_scalar(lbcol[:, l, 1, :], lbcol[:, l, 0, :], -1.0, 1.0,
                                  ALU.mult, ALU.add)

    def unit_wait(eng, j, turn=0):
        u = unit_free[j % 2]
        eng.wait_ge(u.sem, turn * (RING // 2) + u.at(j // 2 + 1))

    def units_used(n):
        for u in range(2):
            unit_free[u].base += (n + 1 - u) // 2

    def modulation(name, n, cond, dst, bias):
        nc_ = cond.shape[2]
        row = arena[0:nc_, 0:1024].rearrange("k (u n) -> k u n", u=2)
        weights.begin(name)
        with nc.Block() as block:
            @block.sync
            def _(sp):
                weights.feed(sp)

            @block.tensor
            def _(pe):
                def turn_row(t, j):
                    pe.wait_ge(act_ready.sem, t + act_ready.at(1))
                    for b in range(4):
                        mm = pe.matmul(ps[:, j % 2, 512 + b * nc_:512 + (b + 1) * nc_],
                                       row[:, j % 2, b * P:(b + 1) * P], ident[0:nc_, 0:nc_],
                                       start=True, stop=True)
                    mm.then_inc(pe_done.sem, 1)

                def tile(t, j, turn):
                    weights.landed(pe, j, turn, RING)
                    unit_wait(pe, j, turn)
                    wt = weights.view(j)
                    for c in range(KC):
                        mm = pe.matmul(ps[0:nc_, j % 2, 0:512], cond[:, c, :], wt[:, c, :],
                                       start=(c == 0), stop=(c == KC - 1))
                    mm.then_inc(tile_done.sem, 1)
                    turn_row(t, j)
                in_turns(pe, n, RING, tile)

            @block.scalar
            def _(act):
                def tile(t, j, turn):
                    act.wait_ge(tile_done.sem, t + tile_done.at(1))
                    act.copy(row[:, j % 2, :], ps[0:nc_, j % 2, 0:512]).then_inc(act_ready.sem, 1)
                in_turns(act, n, RING, tile)

            @block.vector
            def _(dve):
                def tile(t, j, turn):
                    dve.wait_ge(pe_done.sem, t + pe_done.at(1))
                    src = ps[:, j % 2, 512:512 + 4 * nc_].rearrange("p (b k) -> p b k", k=nc_)
                    add = bias[:, bass.ds(t * 4, 4)].unsqueeze(2).to_broadcast([P, 4, nc_])
                    dve.tensor_tensor(dst[:, bass.ds(t * 4, 4), :], src, add, ALU.add) \
                       .then_inc(unit_free[j % 2].sem, 1)
                in_turns(dve, n, RING, tile)
        units_used(n)
        act_ready.base += n
        pe_done.base += n
        weights.end()

    def modulated_features(src, scale, shift, gain=None):
        normed = y_tok
        with nc.Block() as block:
            @block.tensor
            def _(pe):
                if gain is None:
                    tokens = src
                else:
                    tokens = normed
                for t in range(TT):
                    if gain is not None:
                        pe.wait_ge(vec_ready.sem, vec_ready.at(2 + t))
                    for c in range(KC):
                        mm = pe.transpose(ps[:, t, c * P:(c + 1) * P],
                                          tokens[:, t, c * P:(c + 1) * P], ident[:])
                    mm.then_inc(pe_done.sem, 1)

            @block.scalar
            def _(act):
                if gain is not None:
                    act.wait_ge(vec_ready.sem, vec_ready.at(1))
                    act.activation(stat[:, 2:4], stat[:, 0:2], ACT.Sqrt).then_inc(act_ready.sem, 1)
                act.wait_ge(cols_ready.sem, cols_ready.at(1))
                act.wait_ge(pe_done.sem, pe_done.at(1))
                for c in range(KC):
                    act.activation(hT[:, c, 0:P], ps[:, 0, c * P:(c + 1) * P], ACT.Identity,
                                   bias=shift(c), scale=scol[:, c:c + 1])

            @block.vector
            def _(dve):
                v = Steps(dve, vec_step)
                if gain is None:
                    dve.tensor_scalar(scol[:], scale, 1.0, None, ALU.add).then_inc(cols_ready.sem, 1)
                else:
                    dve.scalar_tensor_tensor(out=scol[:], in0=scale, scalar=1.0, in1=gain,
                                             op0=ALU.add, op1=ALU.mult).then_inc(cols_ready.sem, 1)
                    for t in range(TT):
                        v.tick(dve.tensor_tensor_reduce(normed[:, t, :], src[:, t, :], src[:, t, :],
                                                        1.0, 0.0, ALU.mult, ALU.add,
                                                        stat[:, t:t + 1]))
                    v.wait()
                    dve.tensor_scalar(stat[:, 0:2], stat[:, 0:2], 1.0 / D, RMS_EPS,
                                      ALU.mult, ALU.add).then_inc(vec_ready.sem, 1)
                    dve.wait_ge(act_ready.sem, act_ready.at(1))
                    v.link(dve.reciprocal(stat[:, 4:6], stat[:, 2:4]))
                    for t in range(TT):
                        dve.tensor_scalar(normed[:, t, :], src[:, t, :], stat[:, 4 + t:5 + t], None,
                                          ALU.mult).then_inc(vec_ready.sem, 1)
                dve.wait_ge(cols_ready.sem, cols_ready.at(1))
                dve.wait_ge(pe_done.sem, pe_done.at(2))
                for c in range(KC):
                    dve.tensor_scalar(hT[:, c, P:SEQ], ps[:, 1, c * P:(c + 1) * P],
                                      scol[:, c:c + 1], shift(c), ALU.mult, ALU.add)
        cols_ready.base += 1
        pe_done.base += 2
        if gain is not None:
            vec_ready.base += 3
            act_ready.base += 1

    def project_features(pe, wt, j, unit, hT_=None, kc=KC):
        for b in range(4):
            for c in range(kc):
                mm = pe.matmul(ps[:, unit, b * SEQ:(b + 1) * SEQ], wt[:, c, b * P:(b + 1) * P],
                               (hT if hT_ is None else hT_)[:, c, :],
                               start=(c == 0), stop=(c == kc - 1))
        return mm

    def project_tokens(pe, wt, unit, hT_=None):
        for t in range(TT):
            for c in range(KC):
                mm = pe.matmul(ps[:, unit, t * 512:(t + 1) * 512],
                               (hT if hT_ is None else hT_)[:, c, t * P:(t + 1) * P], wt[:, c, :],
                               start=(c == 0), stop=(c == KC - 1))
        return mm

    def broadcast_row(pe, column, unit):
        for c in range(KC):
            mm = pe.matmul(ps[:, unit, c * P:(c + 1) * P], column(c).to_broadcast([P, P]), ident[:],
                           start=True, stop=True)
        return mm

    def input_projection(l, qa, sg, km, ia, ga, qb, kb, vb, gates):
        weights.begin(f"in{l}")
        flat = {0: qa, 2: qb, 3: kb}
        tokens = {4: ia, 6: vb}
        with nc.Block() as block:
            @block.sync
            def _(sp):
                weights.feed(sp)

            @block.tensor
            def _(pe):
                for t in range(11):
                    weights.landed(pe, t, 0, RING)
                    unit_wait(pe, t)
                    wt = weights.view(t)
                    mm = project_tokens(pe, wt, t % 2) if t in (4, 5, 6) else \
                        project_features(pe, wt, t, t % 2)
                    mm.then_inc(tile_done.sem, 1)

            @block.scalar
            def _(act):
                for t in (1, 5, 7, 8, 9, 10):
                    act.wait_ge(tile_done.sem, tile_done.at(t + 1))
                    if t == 1:
                        act.activation(sg.rearrange("p h t -> p (h t)"), ps[:, t % 2, :], ACT.Sigmoid)
                        act.activation(km.rearrange("p h t -> p (h t)"), ps[:, t % 2, :],
                                       ACT.Sigmoid, scale=-1.0).then_inc(unit_free[t % 2].sem, 1)
                    elif t == 5:
                        act.activation(ga.rearrange("p t n -> p (t n)"), ps[:, t % 2, :],
                                       ACT.Sigmoid).then_inc(act_ready.sem, 1)
                    else:
                        g = gates[:, (t - 7) * 4:(t - 6) * 4, :].rearrange("p b t -> p (b t)")
                        act.activation(g, ps[:, t % 2, :], ACT.Sigmoid).then_inc(unit_free[t % 2].sem, 1)

            @block.vector
            def _(dve):
                for t in (0, 2, 3, 4, 5, 6):
                    dve.wait_ge(tile_done.sem, tile_done.at(t + 1))
                    if t == 5:
                        dve.wait_ge(act_ready.sem, act_ready.at(1))
                        g = ga.rearrange("p t n -> p (t n)")
                        dve.tensor_tensor(g, ps[:, t % 2, :], g, ALU.mult).then_inc(unit_free[t % 2].sem, 1)
                    else:
                        dst = flat.get(t, tokens.get(t)).rearrange("p h t -> p (h t)")
                        dve.tensor_copy(dst, ps[:, t % 2, :]).then_inc(unit_free[t % 2].sem, 1)
        act_ready.base += 1
        units_used(11)
        weights.end()

    def hgrn(l, qa, sg, km, ia, ga, oaT, tmp):
        B, E, qe, ke, scores, cross, o, sq = tmp
        blocks = HG_HEADS * TT
        NL = len(LEVELS)
        with nc.Block() as block:
            @block.tensor
            def _(pe):
                pe.wait_ge(vec_ready.sem, vec_ready.at(1))
                for h in range(HG_HEADS):
                    for t in range(TT):
                        b = h * TT + t
                        mm = pe.matmul(ps[:, 0, b * P:(b + 1) * P], km[:, h, t * P:(t + 1) * P],
                                       qa[:, h, t * P:(t + 1) * P], start=True, stop=True)
                mm.then_inc(pe_done.sem, 1)
                for n in range(NL):
                    pe.wait_ge(vec_ready.sem, vec_ready.at(2 + n))
                    for b in range(blocks):
                        mm = pe.matmul(ps[:, (n + 1) % 2, b * P:(b + 1) * P],
                                       ke[:, b * P:(b + 1) * P], qe[:, b * P:(b + 1) * P],
                                       start=True, stop=True)
                    mm.then_inc(pe_done.sem, 1)
                pe.wait_ge(vec_ready.sem, vec_ready.at(2 + NL))
                for h in range(HG_HEADS):
                    mm = pe.matmul(ps[:, 2, h * P:(h + 1) * P], ke[:, 2 * h * P:(2 * h + 1) * P],
                                   qe[:, (2 * h + 1) * P:(2 * h + 2) * P], start=True, stop=True)
                mm.then_inc(pe_done.sem, 1)
                pe.wait_ge(vec_ready.sem, vec_ready.at(3 + NL))
                for t in range(TT):
                    for h in range(HG_HEADS):
                        b = h * TT + t
                        dst = ps[:, 3, t * 512 + h * P:t * 512 + (h + 1) * P]
                        mm = pe.matmul(dst, scores[:, b * P:(b + 1) * P], ia[:, t, h * P:(h + 1) * P],
                                       start=True, stop=(t == 0))
                        if t == 1:
                            mm = pe.matmul(dst, cross[:, h * P:(h + 1) * P],
                                           ia[:, 0, h * P:(h + 1) * P], start=False, stop=True)
                mm.then_inc(pe_done.sem, 1)
                pe.wait_ge(vec_ready.sem, vec_ready.at(5 + NL))
                for h in range(HG_HEADS):
                    for t in range(TT):
                        mm = pe.transpose(ps[:, 0, h * SEQ + t * P:h * SEQ + (t + 1) * P],
                                          o[:, t, h * P:(h + 1) * P], ident[:])
                mm.then_inc(pe_done.sem, 1)

            @block.scalar
            def _(act):
                act.wait_ge(cols_ready.sem, cols_ready.at(1))
                act.activation(sg.rearrange("p h t -> p (h t)"), sg.rearrange("p h t -> p (h t)"),
                               ACT.Ln).then_inc(act_ready.sem, 1)
                for n in range(NL + 1):
                    act.wait_ge(cols_ready.sem, cols_ready.at(2 + n))
                    act.activation(E[:], E[:], ACT.Exp).then_inc(act_ready.sem, 1)
                act.wait_ge(vec_ready.sem, vec_ready.at(4 + NL))
                act.activation(stat[:, 8:16], stat[:, 0:8], ACT.Sqrt).then_inc(act_ready.sem, 1)
                act.wait_ge(pe_done.sem, pe_done.at(4 + NL))
                for h in range(HG_HEADS):
                    act.activation(oaT[:, h, :], ps[:, 0, h * SEQ:(h + 1) * SEQ], ACT.Identity,
                                   scale=vcol[:, 3, V_HGG + 4 * l + h:V_HGG + 4 * l + h + 1])

            @block.vector
            def _(dve):
                v = Steps(dve, vec_step)
                v.tick(dve.memset(qe[:], 0.0))
                v.tick(dve.memset(ke[:], 0.0))
                v.tick(dve.memset(scores[:], 0.0))
                for h in range(HG_HEADS):
                    ins = dve.tensor_scalar(sg[:, h, :], sg[:, h, :], lbcol[:, l, 1, h:h + 1],
                                            lbcol[:, l, 0, h:h + 1], ALU.mult, ALU.add)
                    if h < HG_HEADS - 1:
                        v.tick(ins)
                v.wait()
                ins.then_inc(cols_ready.sem, 1)
                for h in range(HG_HEADS):
                    ins = dve.tensor_scalar(km[:, h, :], km[:, h, :], lbcol[:, l, 1, h:h + 1], None,
                                            ALU.mult)
                    if h < HG_HEADS - 1:
                        v.tick(ins)
                v.wait()
                ins.then_inc(vec_ready.sem, 1)
                dve.wait_ge(act_ready.sem, act_ready.at(1))
                for h in range(HG_HEADS):
                    for t in range(TT):
                        b = h * TT + t
                        v.tick(dve.tensor_tensor_scan(
                            B[:, b * P:(b + 1) * P], ones[:], sg[:, h, t * P:(t + 1) * P], 0.0,
                            ALU.mult, ALU.add))
                v.wait()
                q_all = qa.rearrange("p h t -> p (h t)")
                k_all = km.rearrange("p h t -> p (h t)")

                def take(n):
                    dve.wait_ge(pe_done.sem, pe_done.at(n + 1))
                    mask = level_mask[:, n, :].unsqueeze(1).to_broadcast([P, blocks, P])
                    v.link(dve.copy_predicated(
                        scores.rearrange("p (b t) -> p b t", t=P), mask,
                        ps[:, n % 2, :].rearrange("p (b t) -> p b t", t=P)))

                for n, m in enumerate(LEVELS):
                    nb = 1024 // (2 * m)

                    def halves(ap):
                        r = ap.rearrange("p (b two m) -> p b two m", two=2, m=m)
                        return r[:, :, 0, :], r[:, :, 1, :]
                    b_lo, b_hi = halves(B)
                    e_lo, e_hi = halves(E)
                    mid = b_lo[:, :, m - 1:m].to_broadcast([P, nb, m])
                    v.tick(dve.tensor_tensor(e_hi, b_hi, mid, ALU.subtract))
                    v.wait()
                    dve.tensor_tensor(e_lo, mid, b_lo, ALU.subtract).then_inc(cols_ready.sem, 1)
                    if n >= 1:
                        take(n - 1)
                    dve.wait_ge(act_ready.sem, act_ready.at(2 + n))
                    if n >= 1:
                        dve.wait_ge(pe_done.sem, pe_done.at(n + 1))
                    v.link(dve.tensor_tensor(halves(qe)[1], halves(q_all)[1], e_hi, ALU.mult))
                    dve.tensor_tensor(halves(ke)[0], halves(k_all)[0], e_lo, ALU.mult) \
                       .then_inc(vec_ready.sem, 1)
                    dve.wait_ge(vec_ready.sem, vec_ready.at(2 + n))
                tiles = [ap.rearrange("p (h t m) -> p h t m", t=TT, m=P) for ap in (B, E, qe, ke, q_all, k_all)]
                tb, te, tq, tk, tqa, tka = tiles
                v.link(dve.tensor_copy(te[:, :, 1, :], tb[:, :, 1, :]))
                dve.tensor_tensor(te[:, :, 0, :], tb[:, :, 0, P - 1:P].to_broadcast([P, HG_HEADS, P]),
                                  tb[:, :, 0, :], ALU.subtract).then_inc(cols_ready.sem, 1)
                take(NL - 1)
                dve.wait_ge(act_ready.sem, act_ready.at(2 + NL))
                dve.wait_ge(pe_done.sem, pe_done.at(NL + 1))
                v.link(dve.tensor_tensor(tq[:, :, 1, :], tqa[:, :, 1, :], te[:, :, 1, :], ALU.mult))
                dve.tensor_tensor(tk[:, :, 0, :], tka[:, :, 0, :], te[:, :, 0, :], ALU.mult) \
                   .then_inc(vec_ready.sem, 1)
                take(NL)
                dve.wait_ge(pe_done.sem, pe_done.at(NL + 2))
                dve.tensor_copy(cross[:], ps[:, 2, 0:512]).then_inc(vec_ready.sem, 1)
                dve.wait_ge(pe_done.sem, pe_done.at(NL + 3))
                o_flat = o.rearrange("p t n -> p (t n)")
                v.link(dve.tensor_copy(o_flat, ps[:, 3, :]))
                v.link(dve.tensor_tensor(sq[:], o_flat, o_flat, ALU.mult))
                v.link(dve.tensor_reduce(stat[:, 0:8], sq.rearrange("p (b e) -> p b e", e=P), AX_X,
                                         ALU.add))
                dve.tensor_scalar(stat[:, 0:8], stat[:, 0:8], 1.0 / P, RMS_EPS, ALU.mult, ALU.add) \
                   .then_inc(vec_ready.sem, 1)
                v.link(dve.tensor_tensor(o_flat, o_flat, ga.rearrange("p t n -> p (t n)"), ALU.mult))
                dve.wait_ge(act_ready.sem, act_ready.at(3 + NL))
                v.link(dve.reciprocal(stat[:, 16:24], stat[:, 8:16]))
                o_heads = o_flat.rearrange("p (b e) -> p b e", e=P)
                dve.tensor_tensor(o_heads, o_heads,
                                  stat[:, 16:24].unsqueeze(2).to_broadcast([P, 8, P]), ALU.mult) \
                   .then_inc(vec_ready.sem, 1)
        cols_ready.base += 2 + NL
        vec_ready.base += 5 + NL
        act_ready.base += 3 + NL
        pe_done.base += 4 + NL

    def stick_breaking(qb, kb, vb, obT, tmp):
        Y, L, S = tmp
        scale = 1.0 / math.sqrt(SB_DH)
        groups = SB_HEADS // 4
        W_ = SEQ + P

        def unit(base, n):
            return ps[:, base + n // 2, (n % 2) * 512:(n % 2) * 512 + W_]

        def both(base):
            return ps[:, base:base + 2, :].rearrange("p u (h n) -> p u h n", h=2)[:, :, :, 0:W_]

        def by_unit(ap):
            return ap.rearrange("p (u h) n -> p u h n", h=2)

        with nc.Block() as block:
            @block.tensor
            def _(pe):
                for g in range(groups):
                    if g:
                        pe.wait_ge(vec_ready.sem, vec_ready.at(3 * g))
                    for n in range(4):
                        h = 4 * g + n
                        at = slice(64 * (h % 2), 64 * (h % 2) + 64)
                        u = unit(0, n)
                        pe.matmul(u[:, 0:SEQ], kb[at, h // 2, 0:P], qb[at, h // 2, :],
                                  start=True, stop=True)
                        mm = pe.matmul(u[:, SEQ:W_], kb[at, h // 2, P:SEQ], qb[at, h // 2, P:SEQ],
                                       start=True, stop=True)
                    mm.then_inc(pe_done.sem, 1)
                    pe.wait_ge(vec_ready.sem, vec_ready.at(3 * g + 1))
                    for n in range(4):
                        u = unit(2, n)
                        pe.matmul(u[:, 0:SEQ], tri[:], L[:, n, 0:SEQ], start=True, stop=False)
                        pe.matmul(u[:, P:SEQ], ones[:], L[:, n, SEQ:W_], start=False, stop=True)
                        mm = pe.matmul(u[:, SEQ:W_], tri[:], L[:, n, SEQ:W_], start=True, stop=True)
                    mm.then_inc(pe_done.sem, 1)
                    pe.wait_ge(act_ready.sem, act_ready.at(4 * g + 4))
                    for n in range(4):
                        h = 4 * g + n
                        dst = ps[64 * (h % 2):64 * (h % 2) + 64, 0, (n // 2) * SEQ:(n // 2 + 1) * SEQ]
                        pe.matmul(dst, vb[:, 0, h * 64:(h + 1) * 64], S[:, n, 0:SEQ],
                                  start=True, stop=False, skip_group_check=True)
                        mm = pe.matmul(dst[:, P:SEQ], vb[:, 1, h * 64:(h + 1) * 64], S[:, n, SEQ:W_],
                                       start=False, stop=True, skip_group_check=True)
                    mm.then_inc(pe_done.sem, 1)

            @block.scalar
            def _(act):
                s = Steps(act, act_step)
                for g in range(groups):
                    act.wait_ge(pe_done.sem, pe_done.at(3 * g + 1))
                    act.activation(by_unit(Y), both(0), ACT.Copy, scale=scale) \
                       .then_inc(act_ready.sem, 1)
                    act.wait_ge(act_ready.sem, act_ready.at(4 * g + 1))
                    if g:
                        act.wait_ge(vec_ready.sem, vec_ready.at(3 * g))
                    s.link(act.activation(L[:], Y[:], ACT.Abs))
                    s.link(act.activation(L[:], L[:], ACT.Exp, scale=-1.0))
                    act.activation(L[:], L[:], ACT.Ln, bias=1.0).then_inc(act_ready.sem, 1)
                    act.wait_ge(vec_ready.sem, vec_ready.at(3 * g + 2))
                    act.activation(S[:], S[:], ACT.Exp).then_inc(act_ready.sem, 2)

            @block.vector
            def _(dve):
                v = Steps(dve, vec_step)
                for g in range(groups):
                    dve.wait_ge(act_ready.sem, act_ready.at(4 * g + 2))
                    v.link(dve.scalar_tensor_tensor(out=L[:], in0=Y[:], scalar=0.0, in1=L[:],
                                                    op0=ALU.max, op1=ALU.add))
                    mask = before[:].unsqueeze(1).to_broadcast([P, 4, P])
                    v.link(dve.tensor_tensor(L[:, :, 0:P], L[:, :, 0:P], mask, ALU.mult))
                    dve.tensor_tensor(L[:, :, SEQ:W_], L[:, :, SEQ:W_], mask, ALU.mult) \
                       .then_inc(vec_ready.sem, 1)
                    dve.wait_ge(pe_done.sem, pe_done.at(3 * g + 2))
                    v.link(dve.tensor_tensor(by_unit(S), by_unit(Y), both(2), ALU.subtract))
                    neg = before_neg[:].unsqueeze(1).to_broadcast([P, 4, P])
                    v.link(dve.tensor_tensor(S[:, :, 0:P], S[:, :, 0:P], neg, ALU.add))
                    dve.tensor_tensor(S[:, :, SEQ:W_], S[:, :, SEQ:W_], neg, ALU.add) \
                       .then_inc(vec_ready.sem, 1)
                    dve.wait_ge(pe_done.sem, pe_done.at(3 * g + 3))
                    dve.tensor_copy(obT[:, 2 * g:2 * g + 2, :].rearrange("p c t -> p (c t)"),
                                    ps[:, 0, 0:512]).then_inc(vec_ready.sem, 1)
        vec_ready.base += 3 * groups
        act_ready.base += 4 * groups
        pe_done.base += 3 * groups

    def merge(l, oaT, obT, gates):
        weights.begin(f"up{l}")
        with nc.Block() as block:
            @block.sync
            def _(sp):
                weights.feed(sp)

            @block.tensor
            def _(pe):
                for k, src in enumerate((oaT, obT)):
                    weights.landed(pe, k, 0, RING)
                    wt = weights.view(k)
                    for b in range(KC):
                        for c in range(4):
                            mm = pe.matmul(ps[:, 2 * k + b // 4, (b % 4) * SEQ:(b % 4 + 1) * SEQ],
                                           wt[:, c, b * P:(b + 1) * P], src[:, c, :],
                                           start=(c == 0), stop=(c == 3))
                    mm.then_inc(tile_done.sem, 1)

            @block.vector
            def _(dve):
                v = Steps(dve, vec_step)
                for k in range(2):
                    dve.wait_ge(tile_done.sem, tile_done.at(k + 1))
                    g = gates[:, k * KC:(k + 1) * KC, :].rearrange("p (u b) t -> p u (b t)", u=2)
                    v.link(dve.tensor_tensor(g, g, ps[:, 2 * k:2 * k + 2, :], ALU.mult))
                dve.tensor_tensor(hT[:], gates[:, 0:KC, :], gates[:, KC:2 * KC, :], ALU.add)
        weights.end()

    def residual_norm(dve, act_, v, pieces, gate, gain, shift):
        for t, c0, part in pieces:
            cols = slice(c0, c0 + 512)
            v.link(dve.tensor_tensor(y_tok[:, t, cols], part, gate[:, cols], ALU.mult))
            v.link(dve.scalar_tensor_tensor(out=x_tok[:, t, cols], in0=x_tok[:, t, cols],
                                            scalar=DN_ALPHA, in1=y_tok[:, t, cols],
                                            op0=ALU.mult, op1=ALU.add))
        for t in range(TT):
            for k in range(2):
                v.link(dve.bn_stats(stat[:, 16 + 12 * t + 6 * k:22 + 12 * t + 6 * k],
                                    x_tok[:, t, k * 512:(k + 1) * 512]))
            v.link(dve.bn_aggr(stat[:, 2 * t:2 * t + 2], stat[:, 16 + 12 * t:28 + 12 * t]))
        mean_var = stat[:, 0:4].rearrange("p (t k) -> p t k", k=2)
        dve.tensor_scalar(stat[:, 4:6], mean_var[:, :, 1], LN_EPS, None, ALU.add) \
           .then_inc(vec_ready.sem, 1)
        dve.wait_ge(act_ready.sem, act_ready.at(act_))
        v.link(dve.reciprocal(stat[:, 8:10], stat[:, 6:8]))
        for t in range(TT):
            v.link(dve.tensor_scalar(x_tok[:, t, :], x_tok[:, t, :], stat[:, 2 * t:2 * t + 1],
                                     stat[:, 8 + t:9 + t], ALU.subtract, ALU.mult))
            v.link(dve.tensor_tensor(x_tok[:, t, :], x_tok[:, t, :], gain, ALU.mult))
            v.tick(dve.tensor_tensor(x_tok[:, t, :], x_tok[:, t, :], shift, ALU.add))

    def load_rows(sp, l, k):
        sp.dma_start(rows[:, 1, :], a["ln_g"][l, k:k + 1, :].to_broadcast([P, D])) \
          .then_inc(loaded.sem, 16)
        sp.dma_start(rows[:, 2, :], a["ln_b"][l, k:k + 1, :].to_broadcast([P, D])) \
          .then_inc(loaded.sem, 16)

    def output_projection(l):
        weights.begin(f"o{l}")
        with nc.Block() as block:
            @block.sync
            def _(sp):
                load_rows(sp, l, 0)
                weights.feed(sp)

            @block.tensor
            def _(pe):
                broadcast_row(pe, lambda c: adacol[:, l, 16 + c:17 + c], 2).then_inc(pe_done.sem, 1)
                for t in range(2):
                    weights.landed(pe, t, 0, RING)
                    project_tokens(pe, weights.view(t), t).then_inc(tile_done.sem, 1)

            @block.scalar
            def _(act):
                act.wait_ge(pe_done.sem, pe_done.at(1))
                act.copy(rows[:, 0, :], ps[:, 2, :]).then_inc(act_ready.sem, 1)
                act.wait_ge(vec_ready.sem, vec_ready.at(1))
                act.activation(stat[:, 6:8], stat[:, 4:6], ACT.Sqrt).then_inc(act_ready.sem, 1)

            @block.vector
            def _(dve):
                v = Steps(dve, vec_step)
                dve.wait_ge(act_ready.sem, act_ready.at(1))
                dve.wait_ge(loaded.sem, loaded.at(32))
                dve.wait_ge(tile_done.sem, tile_done.at(2))
                pieces = [(t, k * 512, ps[:, k, t * 512:(t + 1) * 512])
                          for k in range(2) for t in range(TT)]
                residual_norm(dve, 2, v, pieces, rows[:, 0, :], rows[:, 1, :], rows[:, 2, :])
        loaded.base += 32
        pe_done.base += 1
        act_ready.base += 2
        vec_ready.base += 1
        weights.end()

    def peer_queries(l, hf_tok, pqT, keys, keysT, sc):
        weights.begin(f"pq{l}")
        with nc.Block() as block:
            @block.sync
            def _(sp):
                for half in range(2):
                    sp.dma_start(keys[:, :, half * 64:(half + 1) * 64],
                                 a["sub_keys"][l, half].rearrange("h n d -> n h d")) \
                      .then_inc(loaded.sem, 16)
                weights.feed(sp)

            @block.tensor
            def _(pe):
                for t in range(2):
                    weights.landed(pe, t, 0, RING)
                    project_features(pe, weights.view(t), t, t).then_inc(tile_done.sem, 1)
                broadcast_row(pe, lambda c: scol[:, c:c + 1], 2).then_inc(pe_done.sem, 1)
                broadcast_row(pe, lambda c: adacol[:, l, 24 + c:25 + c], 3).then_inc(pe_done.sem, 1)
                pe.wait_ge(loaded.sem, loaded.at(32))
                pe.wait_ge(act_ready.sem, act_ready.at(1))
                for h in range(PEER_HEADS):
                    mm = pe.transpose(ps[:, 2, h * P:(h + 1) * P], keys[:, h, :], ident[:])
                mm.then_inc(pe_done.sem, 1)
                pe.wait_ge(act_ready.sem, act_ready.at(4))
                for t in range(TT):
                    if t:
                        pe.wait_ge(act_ready.sem, act_ready.at(5))
                    for h in range(PEER_HEADS):
                        for half in range(2):
                            at = slice(64 * half, 64 * half + 64)
                            mm = pe.matmul(ps[:, half, h * P:(h + 1) * P],
                                           pqT[at, h, t * P:(t + 1) * P], keysT[at, h, :],
                                           start=True, stop=True)
                    mm.then_inc(pe_done.sem, 1)

            @block.scalar
            def _(act):
                act.wait_ge(pe_done.sem, pe_done.at(1))
                act.copy(rows[:, 0, :], ps[:, 2, :]).then_inc(act_ready.sem, 1)
                act.wait_ge(tile_done.sem, tile_done.at(2))
                for t in range(2):
                    ins = act.copy(pqT[:, 4 * t:4 * t + 4, :].rearrange("p b t -> p (b t)"),
                                   ps[:, t, :])
                    if t:
                        ins.then_inc(act_ready.sem, 1)
                act.wait_ge(pe_done.sem, pe_done.at(2))
                act.copy(rows[:, 1, :], ps[:, 3, :]).then_inc(act_ready.sem, 1)
                act.wait_ge(pe_done.sem, pe_done.at(3))
                act.copy(keysT.rearrange("p h n -> p (h n)"), ps[:, 2, :]).then_inc(act_ready.sem, 1)
                for t in range(TT):
                    act.wait_ge(pe_done.sem, pe_done.at(4 + t))
                    act.copy(sc[:, t], ps[:, 0:2, :]) \
                       .then_inc(act_ready.sem, 1)

            @block.vector
            def _(dve):
                v = Steps(dve, vec_step)
                dve.wait_ge(act_ready.sem, act_ready.at(3))
                for t in range(TT):
                    v.link(dve.tensor_tensor(hf_tok[:, t, :], x_tok[:, t, :], rows[:, 0, :], ALU.mult))
                    v.link(dve.tensor_tensor(hf_tok[:, t, :], hf_tok[:, t, :], rows[:, 1, :], ALU.add))
        loaded.base += 32
        pe_done.base += 5
        act_ready.base += 6
        weights.end()

    def peer_select(l, sc, best, bestf, cand, pos, p12, eq, sel, index, gate):
        def top16(dve, v, values, idx, scores):
            v.link(dve.max(values[:, 0:8], scores))
            v.link(dve.max_index(idx[:, 0:8], values[:, 0:8], scores))
            v.link(dve.match_replace(scores, values[:, 0:8], scores, -3.0e38))
            v.link(dve.max(values[:, 8:16], scores))
            v.tick(dve.max_index(idx[:, 8:16], values[:, 8:16], scores))

        with nc.Block() as block:
            @block.scalar
            def _(act):
                for t in range(TT):
                    act.wait_ge(vec_ready.sem, vec_ready.at(t + 1))
                    act.activation(gate[:, t], gate[:, t], ACT.Exp).then_inc(act_ready.sem, 1)

            @block.vector
            def _(dve):
                v = Steps(dve, vec_step)
                for t in range(TT):
                    for h in range(PEER_HEADS):
                        for half in range(2):
                            n = h * 2 + half
                            top16(dve, v, best[:, n, :], pos[:, n, :], sc[:, t, half, h * P:(h + 1) * P])
                    v.wait()
                    v.link(dve.tensor_copy(bestf, pos))
                    b = best.rearrange("p (h two) k -> p h two k", two=2)
                    v.link(dve.tensor_tensor(
                        cand.rearrange("p h (i j) -> p h i j", j=TOPK),
                        b[:, :, 0, :].unsqueeze(3).to_broadcast([P, PEER_HEADS, TOPK, TOPK]),
                        b[:, :, 1, :].unsqueeze(2).to_broadcast([P, PEER_HEADS, TOPK, TOPK]),
                        ALU.add))
                    top = gate[:, t]
                    for h in range(PEER_HEADS):
                        top16(dve, v, top[:, h, :], pos[:, h, :], cand[:, h, :])
                    v.wait()
                    at = pos[:, 0:PEER_HEADS, :]
                    v.link(dve.tensor_scalar(p12[:, 0], at, 4, None, ALU.logical_shift_right))
                    v.link(dve.tensor_scalar(p12[:, 1], at, 15, None, ALU.bitwise_and))
                    v.link(dve.tensor_copy(sel, p12))
                    bf = bestf.rearrange("p (h two) k -> p h two k", two=2)
                    shape = [P, PEER_HEADS, TOPK, TOPK]
                    e4 = eq.rearrange("p h (k j) -> p h k j", j=TOPK)
                    steps16 = iota16[:].unsqueeze(1).unsqueeze(1).to_broadcast(shape)
                    for k in range(2):
                        v.link(dve.tensor_tensor(e4, sel[:, k].unsqueeze(3).to_broadcast(shape),
                                                 steps16, ALU.is_equal))
                        v.link(dve.tensor_tensor(e4, e4, bf[:, :, k, :].unsqueeze(2).to_broadcast(shape),
                                                 ALU.mult))
                        v.link(dve.tensor_reduce(sel[:, k], e4, AX_X, ALU.add))
                    v.link(dve.tensor_scalar(sel[:, 1], sel[:, 1], float(l * NKEYS * NKEYS), None,
                                             ALU.add))
                    v.link(dve.scalar_tensor_tensor(out=index[:, t], in0=sel[:, 0],
                                                    scalar=float(NKEYS), in1=sel[:, 1],
                                                    op0=ALU.mult, op1=ALU.add))
                    v.link(dve.tensor_copy(stat[:, 0:8], top[:, :, 0]))
                    m = stat[:, 0:8].unsqueeze(2).to_broadcast([P, PEER_HEADS, TOPK])
                    dve.tensor_tensor(top, top, m, ALU.subtract).then_inc(vec_ready.sem, 1)
                    dve.wait_ge(act_ready.sem, act_ready.at(t + 1))
                    v.link(dve.tensor_reduce(stat[:, 8:16], top, AX_X, ALU.add))
                    v.link(dve.reciprocal(stat[:, 16:24], stat[:, 8:16]))
                    r = stat[:, 16:24].unsqueeze(2).to_broadcast([P, PEER_HEADS, TOPK])
                    v.link(dve.tensor_tensor(top, top, r, ALU.mult))
        vec_ready.base += TT
        act_ready.base += TT

    TURNS = TT * PEER_HEADS // 2

    def gather(gp, table, index, cells, grow, zero, tick):
        p_ = Steps(gp, pool_step)
        p_.tick(gp.memset(tick, 0))
        p_.link(gp.memset(zero, 0))

        def turn(i):
            for half in range(2):
                p_.tick(gp.tensor_copy(cells[:, half, :], index[:, bass.ds(i * 32 + half * TOPK, TOPK)]))
                for k in range(TOPK):
                    slot = half * TOPK + k
                    if k % 2 == 0:
                        p_.wait()
                        gp.wait_ge(row_used.sem, row_used.at(i * 32 + slot + 2))
                        p_.tick(gp.tensor_tensor(tick, tick, zero, ALU.add))
                    gp.indirect_dma_start(
                        grow[:, slot % GR, :], None, table,
                        bass.IndirectOffsetOnAxis(ap=cells[:, half, k:k + 1], axis=0)) \
                      .then_inc(row_landed[slot % GR].sem, 16)
        p_.loop(TURNS, 2 + TOPK, turn)

    def landed(eng, i, slot):
        eng.wait_ge(row_landed[slot % GR].sem,
                    i * (16 * 32 // GR) + row_landed[slot % GR].at(16 * (slot // GR + 1)))

    PER_TILE = TURNS // TT

    def peer_down(l, hf_tok, index, cells, grow, tick, zero, act_cell, acts):
        with nc.Block() as block:
            @block.gpsimd
            def _(gp):
                gather(gp, a["peer_u"].rearrange("l n d -> (l n) d"), index, cells, grow, zero, tick)

            @block.vector
            def _(dve):
                v = Steps(dve, vec_step)
                for t in range(TT):
                    def turn(i):
                        q = i + t * PER_TILE
                        v.wait()
                        for slot in range(32):
                            landed(dve, q, slot)
                            dve.tensor_tensor_reduce(
                                grow[:, slot % GR, :], grow[:, slot % GR, :], hf_tok[:, t, :],
                                1.0, 0.0, ALU.mult, ALU.add, act_cell[:, slot:slot + 1]) \
                               .then_inc(row_used.sem, 1)
                        dve.wait_ge(row_used.sem, q * 32 + row_used.at(32 + GR))
                        v.tick(dve.tensor_copy(acts[:, bass.ds(q * 32, 32)], act_cell))
                    v.loop(PER_TILE, 1, turn)
        row_used.base += TT * SLOTS
        for s in range(GR):
            row_landed[s].base += 16 * TT * SLOTS // GR

    def peer_up(l, index, cells, grow, tick, zero, acts, gate, w_cell, diag, zeros_w):
        with nc.Block() as block:
            @block.sync
            def _(sp):
                load_rows(sp, l, 1)

            @block.gpsimd
            def _(gp):
                gather(gp, a["peer_v"].rearrange("l n d -> (l n) d"), index, cells, grow, zero, tick)

            @block.tensor
            def _(pe):
                broadcast_row(pe, lambda c: adacol[:, l, 40 + c:41 + c], 3).then_inc(pe_done.sem, 1)
                pe.wait_ge(diag_ready.sem, diag_ready.at(1))
                for t in range(TT):
                    for half in range(2):
                        pe.matmul(ps[:, t, half * 512:(half + 1) * 512], zeros_w, hT[:, 0:2, :],
                                  start=True, stop=False, skip_group_check=True)
                    with pe.Fori(t * PER_TILE, (t + 1) * PER_TILE) as q:
                        for slot in range(32):
                            landed(pe, q, slot)
                            pe.wait_ge(diag_ready.sem, q * 32 + diag_ready.at(2 + slot))
                            for half in range(2):
                                mm = pe.matmul(ps[:, t, half * 512:(half + 1) * 512],
                                               diag[:, slot % 4, :],
                                               grow[:, slot % GR, half * 512:(half + 1) * 512],
                                               start=False, stop=False, skip_group_check=True)
                            mm.then_inc(row_used.sem, 1)
                    for half in range(2):
                        mm = pe.matmul(ps[:, t, half * 512:(half + 1) * 512], zeros_w, hT[:, 0:2, :],
                                       start=False, stop=True, skip_group_check=True)
                    mm.then_inc(pe_done.sem, 1)

            @block.scalar
            def _(act):
                act.activation(acts, acts, ACT.Gelu).then_inc(act_ready.sem, 1)
                act.wait_ge(pe_done.sem, pe_done.at(1))
                act.copy(rows[:, 0, :], ps[:, 3, :]).then_inc(act_ready.sem, 1)
                act.wait_ge(vec_ready.sem, vec_ready.at(1))
                act.activation(stat[:, 6:8], stat[:, 4:6], ACT.Sqrt).then_inc(act_ready.sem, 1)

            @block.vector
            def _(dve):
                v = Steps(dve, vec_step)
                dve.memset(zeros_w, 0.0).then_inc(diag_ready.sem, 1)
                dve.wait_ge(act_ready.sem, act_ready.at(1))
                v.link(dve.tensor_tensor(acts, acts, gate.rearrange("p t h k -> p (t h k)"), ALU.mult))

                def turn(i):
                    dve.wait_ge(diag_ready.sem, i * 32 + diag_ready.at(1))
                    v.link(dve.tensor_copy(w_cell, acts[:, bass.ds(i * 32, 32)]))
                    for slot in range(32):
                        dve.wait_ge(row_used.sem, i * 32 + row_used.at(GR + slot - 3))
                        dve.tensor_scalar(diag[:, slot % 4, :], ident[:], w_cell[:, slot:slot + 1],
                                          None, ALU.mult).then_inc(diag_ready.sem, 1)
                v.loop(TURNS, 1, turn)
                dve.wait_ge(act_ready.sem, act_ready.at(2))
                dve.wait_ge(loaded.sem, loaded.at(32))
                dve.wait_ge(pe_done.sem, pe_done.at(3))
                pieces = [(t, k * 512, ps[:, t, k * 512:(k + 1) * 512])
                          for k in range(2) for t in range(TT)]
                residual_norm(dve, 3, v, pieces, rows[:, 0, :], rows[:, 1, :], rows[:, 2, :])
        row_used.base += TT * SLOTS
        for s in range(GR):
            row_landed[s].base += 16 * TT * SLOTS // GR
        diag_ready.base += 1 + TT * SLOTS
        loaded.base += 32
        pe_done.base += 3
        act_ready.base += 3
        vec_ready.base += 1

    def gate_up(name, hff, silu):
        weights.begin(f"gu_{name}")
        with nc.Block() as block:
            @block.sync
            def _(sp):
                weights.feed(sp)

            @block.tensor
            def _(pe):
                def tile(t, j, turn):
                    weights.landed(pe, j, turn, RING)
                    unit_wait(pe, j, turn)
                    wt = weights.view(j)
                    for two in range(2):
                        for b in range(2):
                            at = two * 512 + b * SEQ
                            for c in range(KC):
                                mm = pe.matmul(ps[:, j % 2, at:at + SEQ],
                                               wt[:, c, two, b * P:(b + 1) * P], hT[:, c, :],
                                               start=(c == 0), stop=(c == KC - 1))
                    mm.then_inc(tile_done.sem, 1)
                in_turns(pe, 11, RING, tile)

            @block.scalar
            def _(act):
                def tile(t, j, turn):
                    unit_wait(act, j, turn)
                    act.wait_ge(tile_done.sem, tile_done.at(1) + t)
                    act.activation(silu[:, j % 2, :], ps[:, j % 2, 0:512], ACT.Silu) \
                       .then_inc(act_ready.sem, 1)
                in_turns(act, 11, RING, tile)

            @block.vector
            def _(dve):
                def tile(t, j, turn):
                    dve.wait_ge(act_ready.sem, act_ready.at(1) + t)
                    dve.tensor_tensor(hff[:, bass.ds(t * 512, 512)], silu[:, j % 2, :],
                                      ps[:, j % 2, 512:1024], ALU.mult).then_inc(unit_free[j % 2].sem, 1)
                in_turns(dve, 11, RING, tile)
        act_ready.base += 11
        units_used(11)
        weights.end()

    def down(name, hff):
        weights.begin(f"down_{name}")
        width = 256
        hv = hff.rearrange("p (c t) -> p c t", t=SEQ)
        with nc.Block() as block:
            @block.sync
            def _(sp):
                weights.feed(sp)

            @block.tensor
            def _(pe):
                for t in range(8):
                    g, half = t // 2, t % 2
                    weights.landed(pe, t, 0, RING)
                    if half == 0:
                        unit_wait(pe, g)
                    wt = weights.view(t)
                    for m in range(TT):
                        for c in range(11):
                            mm = pe.matmul(ps[:, g % 2, m * 512:m * 512 + width],
                                           hv[:, half * 11 + c, m * P:(m + 1) * P], wt[:, c, :],
                                           start=(half == 0 and c == 0),
                                           stop=(half == 1 and c == 10))
                    mm.then_inc(tile_done.sem, 1)

            @block.vector
            def _(dve):
                for g in range(4):
                    dve.wait_ge(tile_done.sem, tile_done.at(2 * g + 2))
                    src = ps[:, g % 2, :].rearrange("p (t n) -> p t n", t=TT)[:, :, 0:width]
                    dve.tensor_copy(y_tok[:, :, g * width:(g + 1) * width], src) \
                       .then_inc(unit_free[g % 2].sem, 1)
        units_used(4)
        weights.end()

    def project_out(name):
        weights.begin(name)
        with nc.Block() as block:
            @block.sync
            def _(sp):
                weights.feed(sp)

            @block.tensor
            def _(pe):
                for t in range(2):
                    weights.landed(pe, t, 0, RING)
                    unit_wait(pe, t)
                    project_tokens(pe, weights.view(t), t).then_inc(tile_done.sem, 1)

            @block.vector
            def _(dve):
                for t in range(2):
                    dve.wait_ge(tile_done.sem, tile_done.at(t + 1))
                    dve.tensor_copy(y_tok[:, :, t * 512:(t + 1) * 512],
                                    ps[:, t, :].rearrange("p (t n) -> p t n", t=TT)) \
                       .then_inc(unit_free[t].sem, 1)
        units_used(2)
        weights.end()

    def add_normed(tok, gate, gain, weight):
        junk = hT.rearrange("p c t -> p (c t)").rearrange("p (t n) -> p t n", t=TT)
        with nc.Block() as block:
            @block.vector
            def _(dve):
                v = Steps(dve, vec_step)
                dve.scalar_tensor_tensor(out=scol[:], in0=gate, scalar=weight, in1=gain,
                                         op0=ALU.mult, op1=ALU.mult).then_inc(cols_ready.sem, 1)
                for t in range(TT):
                    v.tick(dve.tensor_tensor_reduce(junk[:, t, :], y_tok[:, t, :], y_tok[:, t, :],
                                                    1.0, 0.0, ALU.mult, ALU.add, stat[:, t:t + 1]))
                v.wait()
                dve.tensor_scalar(stat[:, 0:2], stat[:, 0:2], 1.0 / D, RMS_EPS, ALU.mult, ALU.add) \
                   .then_inc(vec_ready.sem, 1)
                dve.wait_ge(act_ready.sem, act_ready.at(1))
                v.link(dve.reciprocal(stat[:, 4:6], stat[:, 2:4]))
                dve.wait_ge(pe_done.sem, pe_done.at(1))
                for t in range(TT):
                    v.link(dve.scalar_tensor_tensor(out=y_tok[:, t, :], in0=y_tok[:, t, :],
                                                    scalar=stat[:, 4 + t:5 + t], in1=ps[:, 3, :],
                                                    op0=ALU.mult, op1=ALU.mult))
                    v.link(dve.tensor_tensor(tok[:, t, :], tok[:, t, :], y_tok[:, t, :], ALU.add))

            @block.tensor
            def _(pe):
                pe.wait_ge(cols_ready.sem, cols_ready.at(1))
                broadcast_row(pe, lambda c: scol[:, c:c + 1], 3).then_inc(pe_done.sem, 1)

            @block.scalar
            def _(act):
                act.wait_ge(vec_ready.sem, vec_ready.at(1))
                act.activation(stat[:, 2:4], stat[:, 0:2], ACT.Sqrt).then_inc(act_ready.sem, 1)
        cols_ready.base += 1
        vec_ready.base += 1
        act_ready.base += 1
        pe_done.base += 1

    def mod_cols(l, k, s):
        return modcol[:, l, k * KC:(k + 1) * KC, s]

    def gain_cols(l, k):
        at = V_NG + (l * 6 + k) * KC
        return vcol[:, 3, at:at + KC]

    def norm_in(tok, s, l, k, gain):
        modulated_features(tok, mod_cols(l, k + 1, s),
                           lambda c: modcol[:, l, k * KC + c, s:s + 1], gain_cols(l, gain))

    def ffn(name, tok, s, l, k, gain):
        hff, silu = carve((D_FF * TT,), (2, 512))
        norm_in(tok, s, l, k, gain)
        gate_up(name, hff, silu)
        down(name, hff)
        add_normed(tok, mod_cols(l, k + 2, s), gain_cols(l, gain + 1), 0.5)

    def conv_projection(name, b_gate, u, up):
        weights.begin(f"conv_{name}")
        with nc.Block() as block:
            @block.sync
            def _(sp):
                weights.feed(sp)

            @block.tensor
            def _(pe):
                for t in range(6):
                    weights.landed(pe, t, 0, RING)
                    unit_wait(pe, t)
                    project_features(pe, weights.view(t), t, t % 2).then_inc(tile_done.sem, 1)

            @block.scalar
            def _(act):
                for t in (2, 3):
                    act.wait_ge(tile_done.sem, tile_done.at(t + 1))
                    act.copy(u[:, 4 * (t - 2):4 * (t - 1), :],
                             ps[:, t % 2, :].rearrange("p (b t) -> p b t", t=SEQ)) \
                       .then_inc(unit_free[t % 2].sem, 1)

            @block.vector
            def _(dve):
                v = Steps(dve, vec_step)
                v.tick(dve.memset(up[:, :, 0:1], 0.0))
                v.tick(dve.memset(up[:, :, SEQ + 1:SEQ + 2], 0.0))
                for t in (0, 1, 4, 5):
                    dve.wait_ge(tile_done.sem, tile_done.at(t + 1))
                    src = ps[:, t % 2, :].rearrange("p (b t) -> p b t", t=SEQ)
                    if t < 2:
                        dve.tensor_copy(b_gate[:, 4 * t:4 * t + 4, :], src).then_inc(unit_free[t % 2].sem, 1)
                    else:
                        at = slice(4 * (t - 4), 4 * (t - 3))
                        dve.tensor_tensor(up[:, at, 1:SEQ + 1], u[:, at, :], src, ALU.mult) \
                           .then_inc(unit_free[t % 2].sem, 1)
        units_used(6)
        weights.end()

    def conv_taps(b_gate, up, y):
        with nc.Block() as block:
            @block.vector
            def _(dve):
                v = Steps(dve, vec_step)

                def tap(k, c):
                    if k == 2:
                        return vcol[:, 1, 72 + c:73 + c]
                    at = V_CW + k * KC + c
                    return vcol[:, 3, at:at + 1]
                for c in range(KC):
                    v.tick(dve.tensor_scalar(y[:, c, :], up[:, c, 0:SEQ], tap(0, c), None, ALU.mult))
                for k in (1, 2):
                    v.wait()
                    for c in range(KC):
                        v.tick(dve.scalar_tensor_tensor(
                            out=y[:, c, :], in0=up[:, c, k:k + SEQ], scalar=tap(k, c), in1=y[:, c, :],
                            op0=ALU.mult, op1=ALU.add))
                v.wait()
                v.tick(dve.tensor_tensor(hT[:], y, b_gate, ALU.mult))

    def conv(name, tok, s):
        b_gate, u, up, y = carve((KC, SEQ), (KC, SEQ), (KC, SEQ + 2), (KC, SEQ))
        norm_in(tok, s, 0, 3, 2)
        conv_projection(name, b_gate, u, up)
        conv_taps(b_gate, up, y)
        project_out(f"convout_{name}")
        add_normed(tok, mod_cols(0, 5, s), gain_cols(0, 3), 1.0)

    def rotate(dve, v, t, heads, out_, src, cos, sin, tmp):
        s5 = src.rearrange("p h (a two q) -> p h a two q", a=2, two=2)
        o5 = out_.rearrange("p h (a two q) -> p h a two q", a=2, two=2)
        t4 = tmp.rearrange("p (h a q) -> p h a q", a=2, q=16)
        shape = [P, heads, 2, 16]
        c4 = cos[:, t].unsqueeze(1).to_broadcast(shape)
        n4 = sin[:, t].unsqueeze(1).to_broadcast(shape)
        for half, op in ((0, ALU.subtract), (1, ALU.add)):
            mine, other = s5[:, :, :, half, :], s5[:, :, :, 1 - half, :]
            v.link(dve.tensor_tensor(t4, other, n4, ALU.mult))
            v.link(dve.tensor_tensor(o5[:, :, :, half, :], mine, c4, ALU.mult))
            v.link(dve.tensor_tensor(o5[:, :, :, half, :], o5[:, :, :, half, :], t4, op))

    def context_keys(kz, vz, kzT):
        weights.begin("kv_z")
        with nc.Block() as block:
            @block.sync
            def _(sp):
                weights.feed(sp)

            @block.tensor
            def _(pe):
                weights.landed(pe, 0, 0, RING)
                project_tokens(pe, weights.view(0), 0).then_inc(tile_done.sem, 1)
                pe.wait_ge(vec_ready.sem, vec_ready.at(1))
                for c in range(4):
                    for t in range(TT):
                        mm = pe.transpose(ps[:, 1, c * SEQ + t * P:c * SEQ + (t + 1) * P],
                                          kz[:, t, 2 * c:2 * c + 2, :], ident[:])
                mm.then_inc(pe_done.sem, 1)

            @block.vector
            def _(dve):
                v = Steps(dve, vec_step)
                dve.wait_ge(tile_done.sem, tile_done.at(1))
                src = ps[:, 0, :].rearrange("p (t n) -> p t n", t=TT)
                copy_keys(dve, v, kz, 0, src)
                dve.tensor_copy(vz, src[:, :, 256:512]).then_inc(vec_ready.sem, 1)
                dve.wait_ge(pe_done.sem, pe_done.at(1))
                dve.tensor_copy(kzT.rearrange("p c t -> p (c t)"), ps[:, 1, :])
        vec_ready.base += 1
        pe_done.base += 1
        weights.end()

    def copy_keys(dve, v, dst, head0, src):
        for t in range(TT):
            k4 = src[:, t, 0:256].rearrange("p (h d) -> p h d", d=HD)
            v.tick(dve.tensor_copy(dst[:, t, head0:head0 + 4, :], k4))
            pairs = src[:, t, 0:256].rearrange("p (c two d) -> p c two d", two=2, d=HD)
            out4 = dst[:, t, head0 + 4:head0 + 8, :].rearrange("p (c two) d -> p c two d", two=2)
            for e in range(2):
                v.tick(dve.tensor_copy(out4[:, :, e, :], pairs[:, :, 1 - e, :]))
        v.wait()

    def queries_and_keys(qk, rot, vx, qkT, cos, sin, tmp):
        heads = NQ + 2 * NKV
        weights.begin("qkv")
        with nc.Block() as block:
            @block.sync
            def _(sp):
                sp.dma_start(cos, a["k_cos"]).then_inc(loaded.sem, 16)
                sp.dma_start(sin, a["k_sin"]).then_inc(loaded.sem, 16)
                weights.feed(sp)

            @block.tensor
            def _(pe):
                for t in range(3):
                    weights.landed(pe, t, 0, RING)
                    project_tokens(pe, weights.view(t), t).then_inc(tile_done.sem, 1)
                pe.wait_ge(vec_ready.sem, vec_ready.at(1))
                for u in range(3):
                    for c in range(4):
                        for t in range(TT):
                            h = 8 * u + 2 * c
                            mm = pe.transpose(ps[:, u, c * SEQ + t * P:c * SEQ + (t + 1) * P],
                                              rot[:, t, h:h + 2, :], ident[:])
                    mm.then_inc(pe_done.sem, 1)

            @block.scalar
            def _(act):
                for k in range(2):
                    act.wait_ge(tile_done.sem, tile_done.at(k + 1))
                    for t in range(TT):
                        ins = act.activation(qk[:, t, 8 * k:8 * k + 8, :],
                                             ps[:, k, t * 512:(t + 1) * 512].rearrange(
                                                 "p (h d) -> p h d", d=HD),
                                             ACT.Copy, scale=HD ** -0.5)
                ins.then_inc(act_ready.sem, 1)
                for u in range(3):
                    act.wait_ge(pe_done.sem, pe_done.at(u + 1))
                    act.copy(qkT[:, 4 * u:4 * u + 4, :].rearrange("p c t -> p (c t)"), ps[:, u, :])

            @block.vector
            def _(dve):
                v = Steps(dve, vec_step)
                dve.wait_ge(tile_done.sem, tile_done.at(3))
                src = ps[:, 2, :].rearrange("p (t n) -> p t n", t=TT)
                copy_keys(dve, v, qk, NQ, src)
                v.tick(dve.tensor_copy(vx, src[:, :, 256:512]))
                dve.wait_ge(act_ready.sem, act_ready.at(1))
                dve.wait_ge(loaded.sem, loaded.at(32))
                for t in range(TT):
                    rotate(dve, v, t, heads, rot[:, t], qk[:, t], cos, sin, tmp)
                dve.memset(stat[:, 0:1], 0.0).then_inc(vec_ready.sem, 1)
        loaded.base += 32
        vec_ready.base += 1
        act_ready.base += 1
        pe_done.base += 3
        weights.end()

    def window_attention(qkT, kzT, vx, vz, s, pT, band, sink):
        with nc.Block() as block:
            @block.sync
            def _(sp):
                sp.dma_start(band, a["k_band"]).then_inc(loaded.sem, 16)
                sp.dma_start(sink, a["attn_sink_2"].to_broadcast([P, NQ])).then_inc(loaded.sem, 16)

            @block.tensor
            def _(pe):
                def scores(h):
                    if h >= 2:
                        pe.wait_ge(vec_ready.sem, vec_ready.at(3 * (h - 2) + 1))
                    kv = h // (NQ // NKV)
                    same = h % 2 == kv % 2
                    at = slice(64 * (h % 2), 64 * (h % 2) + 64)
                    kx = qkT[at, 8 + kv // 2 + (0 if same else 2), :]
                    kz = kzT[at, kv // 2 + (0 if same else 2), :]
                    for t in range(TT):
                        q = qkT[at, h // 2, t * P:(t + 1) * P]
                        pe.matmul(ps[:, h % 2, t * 512:t * 512 + 256], q, kx, start=True, stop=True)
                        mm = pe.matmul(ps[:, h % 2, t * 512 + 256:(t + 1) * 512], q, kz,
                                       start=True, stop=True)
                    mm.then_inc(pe_done.sem, 1)

                scores(0)
                for h in range(NQ):
                    if h + 1 < NQ:
                        scores(h + 1)
                    pe.wait_ge(vec_ready.sem, vec_ready.at(3 * h + 3))
                    for c in range(4):
                        for t in range(TT):
                            mm = pe.transpose(ps[:, 2, c * SEQ + t * P:c * SEQ + (t + 1) * P],
                                              s[:, h % 2, t, c * P:(c + 1) * P], ident[:])
                    mm.then_inc(turned.sem, 1)
                    pe.wait_ge(act_ready.sem, act_ready.at(2 * h + 2))
                    if h == 8:
                        pe.wait_ge(cols_ready.sem, cols_ready.at(1))
                    kv = h // (NQ // NKV)
                    dst = ps[64 * (h % 2):64 * (h % 2) + 64, 3,
                             (h % 8 // 2) * SEQ:(h % 8 // 2 + 1) * SEQ]
                    for c in range(4):
                        values = (vx if c < 2 else vz)[:, c % 2, kv * HD:(kv + 1) * HD]
                        mm = pe.matmul(dst, values, pT[:, c, :], start=(c == 0), stop=(c == 3),
                                       skip_group_check=True)
                    mm.then_inc(summed.sem, 1)

            @block.scalar
            def _(act):
                def turn_out(h):
                    act.wait_ge(turned.sem, turned.at(h + 1))
                    if h >= 1:
                        act.wait_ge(summed.sem, summed.at(h))
                    act.copy(pT.rearrange("p c t -> p (c t)"), ps[:, 2, :]) \
                       .then_inc(act_ready.sem, 1)

                for h in range(NQ):
                    act.wait_ge(vec_ready.sem, vec_ready.at(3 * h + 2))
                    b = 8 * (h % 2)
                    for t in range(TT):
                        act.activation(s[:, h % 2, t, :], s[:, h % 2, t, :], ACT.Exp,
                                       bias=stat[:, b + t:b + t + 1],
                                       accum_out=stat[:, b + 2 + t:b + 3 + t])
                    act.activation(stat[:, b + 4:b + 6], stat[:, b:b + 2], ACT.Exp,
                                   bias=sink[:, h:h + 1]).then_inc(act_ready.sem, 1)
                    turn_out(h)

            @block.vector
            def _(dve):
                v = Steps(dve, vec_step)
                dve.wait_ge(loaded.sem, loaded.at(32))
                for h in range(NQ):
                    b = 8 * (h % 2)
                    dve.wait_ge(pe_done.sem, pe_done.at(h + 1))
                    if h >= 2:
                        dve.wait_ge(turned.sem, turned.at(h - 1))
                    dve.tensor_tensor(s[:, h % 2], ps[:, h % 2, :].rearrange("p (t n) -> p t n", t=TT),
                                      band, ALU.add).then_inc(vec_ready.sem, 1)
                    dve.wait_ge(vec_ready.sem, vec_ready.at(3 * h + 1))
                    v.link(dve.tensor_reduce(stat[:, b:b + 2], s[:, h % 2], AX_X, ALU.max))
                    dve.tensor_scalar(stat[:, b:b + 2], stat[:, b:b + 2], sink[:, h:h + 1], -1.0,
                                      ALU.max, ALU.mult).then_inc(vec_ready.sem, 1)
                    dve.wait_ge(act_ready.sem, act_ready.at(2 * h + 1))
                    v.link(dve.tensor_tensor(stat[:, b + 6:b + 8], stat[:, b + 2:b + 4],
                                             stat[:, b + 4:b + 6], ALU.add))
                    v.link(dve.reciprocal(stat[:, b + 6:b + 8], stat[:, b + 6:b + 8]))
                    dve.tensor_tensor(s[:, h % 2], s[:, h % 2],
                                      stat[:, b + 6:b + 8].unsqueeze(2).to_broadcast([P, TT, 512]),
                                      ALU.mult).then_inc(vec_ready.sem, 1)
                    if h % 8 == 7:
                        dve.wait_ge(summed.sem, summed.at(h + 1))
                        dve.tensor_copy(hT[:, h // 8 * 4:h // 8 * 4 + 4, :].rearrange(
                            "p c t -> p (c t)"), ps[:, 3, :]).then_inc(cols_ready.sem, 1)
        loaded.base += 32
        pe_done.base += NQ
        turned.base += NQ
        summed.base += NQ
        vec_ready.base += 3 * NQ
        act_ready.base += 2 * NQ
        cols_ready.base += 2

    for l in range(DEPTH):
        modulation(f"ada{l}", 12, condT, adacol[:, l, :].unsqueeze(2),
                   vcol[:, 0, V_BADA + 48 * l:V_BADA + 48 * (l + 1)])
    for l in range(DEPTH):
        modulation(f"mod{l}", 18, cond2T, modcol[:, l], vcol[:, 1 + l, V_BMOD:V_BMOD + 72])

    for l in range(DEPTH):
        modulated_features(x_tok, adacol[:, l, 8:16], lambda c: adacol[:, l, c:c + 1])
        (qa, sg, km, ia, ga, qb, kb, vb, gates, oaT, obT, work) = carve(
            (4, SEQ), (4, SEQ), (4, SEQ), (TT, 512), (TT, 512), (4, SEQ), (4, SEQ), (TT, 512),
            (2 * KC, SEQ), (4, SEQ), (4, SEQ), (5632,))
        input_projection(l, qa, sg, km, ia, ga, qb, kb, vb, gates)
        hg = [work[:, k * 1024:(k + 1) * 1024] for k in range(5)]
        cross = work[:, 5120:5632]
        o, sq = y_tok[:, 0, :].rearrange("p (t n) -> p t n", t=TT), y_tok[:, 1, :]
        hgrn(l, qa, sg, km, ia, ga, oaT,
             (hg[0], hg[1], hg[2], hg[3], hg[4], cross, o, sq))
        sbt = [work[:, k * 1536:(k + 1) * 1536].rearrange("p (n w) -> p n w", n=4) for k in range(3)]
        stick_breaking(qb, kb, vb, obT, sbt)
        merge(l, oaT, obT, gates)
        output_projection(l)

        modulated_features(x_tok, adacol[:, l, 32:40], lambda c: adacol[:, l, 24 + c:25 + c])
        hf_tok, index, gate, small, rest = carve((TT, D), (TT, PEER_HEADS, TOPK),
                                                 (TT, PEER_HEADS, TOPK), (512,), (13568,))
        index = index.bitcast(U32)
        pqT = rest[:, 0:2048].rearrange("p (h t) -> p h t", h=PEER_HEADS)
        keys = rest[:, 2048:3072].rearrange("p (h t) -> p h t", h=PEER_HEADS)
        keysT = rest[:, 3072:4096].rearrange("p (h t) -> p h t", h=PEER_HEADS)
        sc = rest[:, 4096:8192].rearrange("p (t half n) -> p t half n", t=TT, half=2)
        best = rest[:, 8192:8448].rearrange("p (n k) -> p n k", k=TOPK)
        bestf = rest[:, 8448:8704].rearrange("p (n k) -> p n k", k=TOPK)
        pos = rest[:, 8704:8960].rearrange("p (n k) -> p n k", k=TOPK).bitcast(U32)
        p12 = rest[:, 8960:9216].rearrange("p (z h k) -> p z h k", z=2, k=TOPK).bitcast(U32)
        sel = rest[:, 9216:9472].rearrange("p (z h k) -> p z h k", z=2, k=TOPK)
        cand = rest[:, 9472:11520].rearrange("p (h n) -> p h n", h=PEER_HEADS)
        eq = rest[:, 11520:13568].rearrange("p (h n) -> p h n", h=PEER_HEADS)
        peer_queries(l, hf_tok, pqT, keys, keysT, sc)
        peer_select(l, sc, best, bestf, cand, pos, p12, eq, sel, index, gate)
        grow = rest[:, 0:GR * D].rearrange("p (r n) -> p r n", r=GR)
        diag = rest[:, GR * D:GR * D + 512].rearrange("p (r n) -> p r n", r=4)
        zeros_w = rest[:, GR * D + 512:GR * D + 640]
        acts = rest[:, GR * D + 640:GR * D + 896]
        cells = small[:, 0:32].rearrange("p (a k) -> p a k", a=2).bitcast(U32)
        act_cell, tick, zero = small[:, 32:64], small[:, 64:65].bitcast(U32), small[:, 65:66].bitcast(U32)
        flat_index = index.rearrange("p t h k -> p (t h k)")
        peer_down(l, hf_tok, flat_index, cells, grow, tick, zero, act_cell, acts)
        peer_up(l, flat_index, cells, grow, tick, zero, acts, gate, act_cell, diag, zeros_w)

    kz, vz, kzT, late = None, None, None, None
    for tok, s, name in ((z_tok, 1, "z"), (x_tok, 0, "x")):
        ffn(f"{name}00", tok, s, 0, 0, 0)
        conv(name, tok, s)
        ffn(f"{name}01", tok, s, 0, 6, 4)
        ffn(f"{name}10", tok, s, 1, 0, 0)
        norm_in(tok, s, 1, 3, 2)
        if s == 1:
            (kz,) = carve((TT, 2 * NKV, HD))
            kzT, vz = context_kT[:], context_v[:]
            context_keys(kz, vz, kzT)
    qk, rot, vx, qkT, cos, sin, tmp = carve((TT, 24, HD), (TT, 24, HD), (TT, 256), (12, SEQ),
                                            (TT, 2, 16), (TT, 2, 16), (24 * 32,))
    queries_and_keys(qk, rot, vx, qkT, cos, sin, tmp)
    scores, pT, band, sink = carve((2, TT, 512), (4, SEQ), (TT, 512), (NQ,))
    window_attention(qkT, kzT, vx, vz, scores, pT, band, sink)
    project_out("attn_o")
    add_normed(x_tok, mod_cols(1, 5, 0), gain_cols(1, 3), 1.0)
    ffn("x11", x_tok, 0, 1, 6, 4)

    with nc.Block() as block:
        @block.sync
        def _(sp):
            sp.dma_start(out[0].rearrange("(t p) d -> p t d", p=P), x_tok[:]).then_inc(stored.sem, 16)
            sp.wait_ge(stored.sem, 16)


def constants():
    i = np.arange(P)
    s, t = i[:, None], i[None, :]
    levels = [s == t] + [(s // (2 * m) == t // (2 * m)) & (s % (2 * m) < m) & (t % (2 * m) >= m)
                         for m in LEVELS]
    tok = np.arange(SEQ)
    grid_w, quarter = 64, HD // 4
    freq = (np.float32(10000.0) ** (-np.arange(quarter, dtype=np.float32) / np.float32(quarter)))
    ang = np.stack([(tok // grid_w).astype(np.float32)[:, None] * freq,
                    (tok % grid_w).astype(np.float32)[:, None] * freq], axis=1)
    table = lambda f: np.ascontiguousarray(
        f(ang).astype(np.float32).reshape(TT, P, 2, quarter).transpose(1, 0, 2, 3))
    band = np.zeros((P, TT, 512), np.float32)
    q = tok.reshape(TT, P).T
    band[:, :, 0:SEQ] = np.where(np.abs(tok[None, None, :] - q[:, :, None]) <= 128, 0.0, NEG)
    f = np.float32
    return {
        "k_ident": (s == t).astype(f),
        "k_tri": (s >= t).astype(f),
        "k_before": (s < t).astype(f),
        "k_before_neg": np.where(s < t, 0.0, NEG).astype(f),
        "k_levels": np.ascontiguousarray(np.stack(levels, 1).astype(np.uint32)),
        "k_iota16": np.tile(np.arange(TOPK, dtype=f), (P, 1)),
        "k_cos": table(np.cos),
        "k_sin": table(np.sin),
        "k_band": band,
    }


_INS = ["x", "c", "w_ada", "b_ada", "w_in", "lb_logits", "hg_norm_g", "w_up_a", "w_up_b", "w_o",
        "w_pq", "sub_keys", "peer_u", "peer_v", "ln_g", "ln_b", "c_2", "ctx_2", "c_ctx_2",
        "w_mod_2", "b_mod_2", "norm_g_2", "ffn_w_gu_2", "ffn_w_down_2", "conv_w_in_2", "conv_w_2",
        "conv_w_out_2", "attn_w_qkv_2", "attn_w_o_2", "attn_sink_2"]


def kernel(**inputs):
    import concourse.bacc as bacc
    from concourse.bass_utils import run_bass_kernel_spmd

    nc = bacc.Bacc("TRN2", target_bir_lowering=False, num_devices=1)
    arrays, aps = {}, {}
    for name, value in [(n, inputs[n]) for n in _INS] + list(constants().items()):
        value = np.ascontiguousarray(value)
        arrays[f"in_{name}"] = value
        aps[name] = nc.dram_tensor(f"in_{name}", value.shape, mybir.dt.from_np(value.dtype),
                                   kind="ExternalInput").ap()
    out = nc.dram_tensor("out", (1, SEQ, D), F32, kind="ExternalOutput").ap()
    build(nc, aps, out)
    r = run_bass_kernel_spmd(nc, [arrays], core_ids=[0])
    return r.results[0]["out"]
```

```python
import math
from contextlib import ExitStack

import numpy as np

import concourse.bass as bass
from concourse import mybir

F32 = mybir.dt.float32
U32 = mybir.dt.uint32
F32R = mybir.dt.float32r
ALU = mybir.AluOpType
ACT = mybir.ActivationFunctionType
AX_X = mybir.AxisListType.X

P = 128
D = 1024
KC = D // P
SEQ = 256
TT = SEQ // P
DEPTH = 2
DN_ALPHA = (2.0 * DEPTH) ** 0.25
LN_EPS = 1e-5
RMS_EPS = 1e-6

HG_HEADS = 4
SB_HEADS = 8
SB_DH = 64
PEER_HEADS = 8
TOPK = 16
NKEYS = 128
HALF_KEY = 64
SLOTS = PEER_HEADS * TOPK

D_FF = 2816
FC = D_FF // P
HD = 64
NQ = 16
NKV = 4
NEG = -1e30

QUARTERS = 4
QUARTER = 1024
LEVELS = (64, 32, 16, 8, 4, 2, 1)


class Signal:

    def __init__(self, sem):
        self.sem = sem
        self.base = 0

    def at(self, k):
        return self.base + k


class Steps:

    def __init__(self, eng, count):
        self.eng, self.count, self.n = eng, count, count.base

    def tick(self, ins):
        ins.then_inc(self.count.sem, 1)
        self.n += 1
        self.count.base = self.n

    def wait(self):
        self.eng.wait_ge(self.count.sem, self.n)

    def link(self, ins):
        self.tick(ins)
        self.wait()

    def loop(self, turns, per_turn, body):
        start = self.n
        with self.eng.Fori(0, turns) as i:
            self.n = start + i * per_turn
            body(i)
        self.n = self.count.base = start + turns * per_turn


def in_pairs(n, eng, body):
    if n >= 4:
        with eng.Fori(0, n // 2) as i:
            for j in range(2):
                body(i * 2 + j, j, i)
    else:
        for t in range(n // 2 * 2):
            body(t, t % 2, t // 2)
    if n % 2:
        body(n - 1, 0, n // 2)


def with_last(n, eng, body):
    in_pairs(n - 1, eng, body)
    body(n - 1, (n - 1) % 2, (n - 1) // 2)


class Group:

    def __init__(self, name, n, chunks, cols, source, split, first, index):
        self.name, self.n, self.chunks, self.cols = name, n, chunks, cols
        self.source, self.split, self.first, self.index = source, split, first, index

    def starts(self, k):
        return sum(self.chunks[:k])

    def place(self, j, turn):
        return (self.first + j) % 2, turn + (self.first + j) // 2


class WeightStream:

    def __init__(self, raw, hi, lo, landed, hi_made, lo_made, used, whole_used):
        self.raw, self.hi, self.lo = raw, hi, lo
        self.landed, self.hi_made, self.lo_made = landed, hi_made, lo_made
        self.used, self.whole_used = used, whole_used
        self.groups = []
        self.now = 0

    def add(self, name, n, chunks, cols, source, split=True):
        assert n >= 2
        first = sum(g.n for g in self.groups)
        index = sum(g.n for g in self.groups if g.split == split)
        self.groups.append(Group(name, n, chunks, cols, source, split, first, index))

    def begin(self, name):
        assert self.group().name == name, (name, self.group().name)

    def end(self):
        self.now += 1

    def group(self, after=0):
        at = self.now + after
        return self.groups[at] if 0 <= at < len(self.groups) else None

    def wait_product(self, eng, t):
        g = self.group()
        if g.split:
            eng.wait_ge(self.used.sem, t * QUARTERS + (g.index * QUARTERS + 2 * QUARTERS))
        else:
            eng.wait_ge(self.whole_used.sem, t * 2 + (g.index * 2 + 2))

    def wait_raw_free(self, sp, g, t, half):
        if g.split:
            sp.wait_ge(self.lo_made.sem, t * QUARTERS + (g.index * QUARTERS + 2 * half + 2))
        else:
            sp.wait_ge(self.whole_used.sem, t * 2 + (g.index * 2 + half + 1))

    def raw_part(self, g, parity, half, c0, c1):
        at = g.starts(2 * half)
        return self.raw[:, 2 * parity + half, (c0 - at) * g.cols:(c1 - at) * g.cols]

    def load(self, sp, at, t, parity):
        g = self.groups[at]
        for half in range(2):
            c0, c1 = g.starts(2 * half), g.starts(2 * half + 2)
            if not isinstance(t, int) or t >= 2:
                self.wait_raw_free(sp, g, t - 2, half)
            elif at > 0:
                before = self.groups[at - 1]
                self.wait_raw_free(sp, before, before.n + t - 2, half)
            dst = self.raw_part(g, parity, half, c0, c1).rearrange("p (c n) -> p c n", n=g.cols)
            parts = g.source(t, c0, c1)
            done = self.landed[2 * parity + half]
            if isinstance(parts, list):
                wide = g.cols // 2
                for two, part in enumerate(parts):
                    sp.dma_start(dst[:, :, two * wide:(two + 1) * wide], part).then_inc(done, 16)
            else:
                sp.dma_start(dst, parts).then_inc(done, 32)

    def feed(self, sp):
        g = self.group()
        left = g.n - 2
        if left >= 8:
            with sp.Fori(1, left // 2 + 1) as i:
                for j in range(2):
                    self.load(sp, self.now, i * 2 + j, (g.first + j) % 2)
            done = 2 + left // 2 * 2
        else:
            done = 2
        for t in range(done, g.n):
            self.load(sp, self.now, t, (g.first + t) % 2)
        self.ahead_loads(sp, self.now + 1)

    def ahead_loads(self, sp, at):
        if at < len(self.groups):
            for t in range(2):
                self.load(sp, at, t, (self.groups[at].first + t) % 2)

    def next_tile(self, t, j, turn):
        g = self.group()
        if isinstance(t, int) and t == g.n - 1:
            return self.first_tile(self.group(1))
        return (g, t + 1) + g.place(j + 1, turn)

    def first_tile(self, g):
        return (g, 0) + g.place(0, 0) if g is not None and g.split else None

    def split_hi(self, act, tile):
        if tile is None:
            return
        g, t, parity, turn = tile
        for k in range(QUARTERS):
            if k % 2 == 0:
                act.wait_ge(self.landed[2 * parity + k // 2], turn * 32 + 32)
            act.wait_ge(self.used.sem, t * QUARTERS + (g.index * QUARTERS + k + 1))
            act.activation(self.hi[:, k, 0:g.chunks[k] * g.cols],
                           self.raw_part(g, parity, k // 2, g.starts(k), g.starts(k + 1)),
                           ACT.Copy).then_inc(self.hi_made.sem, 1)

    def split_lo(self, dve, tile):
        if tile is None:
            return
        g, t, parity, _ = tile
        for k in range(QUARTERS):
            n = g.chunks[k] * g.cols
            dve.wait_ge(self.hi_made.sem, t * QUARTERS + (g.index * QUARTERS + k + 1))
            dve.tensor_tensor(self.lo[:, k, 0:n],
                              self.raw_part(g, parity, k // 2, g.starts(k), g.starts(k + 1)),
                              self.hi[:, k, 0:n].bitcast(F32), ALU.subtract) \
               .then_inc(self.lo_made.sem, 1)

    def sections(self, pe, t, j, turn):
        g = self.group()
        parity, at = g.place(j, turn)
        if g.split:
            for k in range(QUARTERS):
                pe.wait_ge(self.lo_made.sem, t * QUARTERS + (g.index * QUARTERS + k + 1))
                yield g.starts(k), g.chunks[k], [
                    slots[:, k, 0:g.chunks[k] * g.cols].rearrange("p (c n) -> p c n", n=g.cols)
                    for slots in (self.hi, self.lo)]
        else:
            for half in range(2):
                pe.wait_ge(self.landed[2 * parity + half], at * 32 + 32)
                c0, c1 = g.starts(2 * half), g.starts(2 * half + 2)
                yield c0, c1 - c0, [self.raw_part(g, parity, half, c0, c1)
                                    .rearrange("p (c n) -> p c n", n=g.cols)]

    def section_done(self, mm):
        mm.then_inc(self.used.sem if self.group().split else self.whole_used.sem, 1)


def columns(w, cols):
    v = w.rearrange("(c p) n -> p c n", p=P)
    if isinstance(cols, range):
        return lambda t, c0, c1: v[:, c0:c1, bass.ds(t * cols.step + cols.start, 512)]
    return lambda t, c0, c1: v[:, c0:c1, cols[t]:cols[t] + 512]


EVEN = (2, 2, 2, 2)
DOWN = (3, 3, 3, 2)


def build(nc, a, out):
    ctx = ExitStack()
    with ctx:
        _build(nc, ctx, a, out)


def _build(nc, ctx, a, out):
    def sb(name, shape, dt=F32):
        return ctx.enter_context(nc.sbuf_tensor(name, shape, dt))

    def signal(name):
        return Signal(ctx.enter_context(nc.semaphore(name)))

    raw = sb("raw", [P, 4, 2 * QUARTER])
    w_hi = sb("w_hi", [P, QUARTERS, QUARTER], F32R)
    w_lo = sb("w_lo", [P, QUARTERS, QUARTER], F32R)
    x_tok = sb("x_tok", [P, TT, D])
    z_tok = sb("z_tok", [P, TT, D])
    y_tok = sb("y_tok", [P, TT, D])
    hT_hi = sb("hT_hi", [P, KC, SEQ], F32R)
    hT_lo = sb("hT_lo", [P, KC, SEQ], F32R)
    hT = (hT_hi, hT_lo)
    ident = sb("ident", [P, P])
    tri = sb("tri", [P, P])
    before = sb("before", [P, P])
    before_neg = sb("before_neg", [P, P])
    ones = sb("ones", [P, P])
    level_mask = sb("level_mask", [P, len(LEVELS) + 1, P], U32)
    iota16 = sb("iota16", [P, TOPK])
    vcol = sb("vcol", [P, 4, P])
    condT = sb("condT", [P, KC, 4])
    cond_parts = sb("cond_parts", [P, KC, 2], F32R)
    adacol = sb("adacol", [P, DEPTH, 48])
    modcol = sb("modcol", [P, DEPTH, 72, 2])
    scol = sb("scol", [P, KC])
    bcol = sb("bcol", [P, KC])
    lbcol = sb("lbcol", [P, DEPTH, 2, HG_HEADS])
    stat = sb("stat", [P, 64])
    rows = sb("rows", [P, 3, D])
    context_kT = sb("context_kT", [P, 4, SEQ])
    context_v = sb("context_v", [P, TT, NKV * HD])
    ps = ctx.enter_context(nc.psum_tensor("ps", [P, 4, 1024], F32))

    arena, parts = None, None
    outer, inner = ExitStack(), ExitStack()
    ctx.enter_context(outer)
    ctx.enter_context(inner)

    def begin_parts(name, size, dt=F32R):
        nonlocal parts
        inner.close()
        parts = None
        if size:
            parts = inner.enter_context(nc.sbuf_tensor(f"parts_{name}", [P, size], dt))

    def begin_stretch(name, arena_size, parts_size):
        nonlocal arena
        inner.close()
        outer.close()
        arena = outer.enter_context(nc.sbuf_tensor(f"arena_{name}", [P, arena_size], F32))
        begin_parts(name, parts_size)

    def carve(*shapes, of=None):
        whole = arena if of is None else of
        at, out_ = 0, []
        for shape in shapes:
            n = math.prod(shape)
            v = whole[:, at:at + n]
            if len(shape) > 1:
                names = [f"d{i}" for i in range(len(shape))]
                v = v.rearrange(f"p ({' '.join(names)}) -> p {' '.join(names)}",
                                **{m: s for m, s in zip(names[1:], shape[1:])})
            out_.append(v)
            at += n
        assert at <= whole.shape[1], (at, whole.shape)
        return out_

    used = signal("quarters_used")
    whole_used = signal("whole_halves_used")
    hi_made = signal("quarters_rounded")
    lo_made = signal("quarters_split")
    unit_free = [signal(f"unit_free_{u}") for u in range(2)]
    vec_step = signal("vec_step")
    act_step = signal("act_step")
    pool_step = signal("pool_step")
    loaded = signal("loaded")
    stored = signal("stored")
    pe_done = signal("pe_done")
    vec_ready = signal("vec_ready")
    act_ready = signal("act_ready")
    cols_ready = signal("cols_ready")
    halves_landed = [ctx.enter_context(nc.semaphore(f"half_landed_{k}")) for k in range(4)]
    GR = 8
    row_landed = [signal(f"rows_landed_{s}") for s in range(GR)]
    row_used = signal("row_used")
    turned = signal("turned")
    summed = signal("summed")
    zeros_made = signal("zeros_made")
    rows_rounded = signal("rows_rounded")
    rows_split = signal("rows_split")
    slot_summed = signal("slot_summed")
    dots_kept = signal("dots_kept")
    mod_rows = signal("mod_rows")
    mod_turned = signal("mod_turned")

    weights = WeightStream(raw, w_hi, w_lo, halves_landed, hi_made, lo_made, used, whole_used)

    def w(name, l):
        return a[name][l]

    CHUNK_KV = 2 * 512
    for l in range(DEPTH):
        weights.add(f"ada{l}", 12, EVEN, 512, columns(w("w_ada", l), range(0, 6144, 512)))

    def add_block_1(l):
        weights.add(f"in{l}", 7, EVEN, 512, columns(
            w("w_in", l), [0, 512, 2048, 2560, 1024, 1536, 3072]))
        weights.add(f"gates{l}", 4, EVEN, 512, columns(w("w_in", l), range(3584, 5632, 512)))
        up = [w("w_up_a", l), w("w_up_b", l)]
        weights.add(f"up{l}", 2, (1, 1, 1, 1), 1024, lambda t, c0, c1, up=up:
                    up[t].rearrange("(c p) n -> p c n", p=P)[:, c0:c1, :])
        weights.add(f"o{l}", 2, EVEN, 512, columns(w("w_o", l), range(0, 1024, 512)))
        weights.add(f"pq{l}", 2, EVEN, 512, columns(w("w_pq", l), range(0, 1024, 512)))

    def add_ffn(name, l, k, split=True):
        gu = a["ffn_w_gu_2"][l, k].rearrange("(c p) (two f) -> p c two f", p=P, two=2)
        down_ = a["ffn_w_down_2"][l, k].rearrange("(h c p) n -> p h c n", p=P, h=2)
        weights.add(f"gu_{name}", 11, EVEN, 512, lambda t, c0, c1:
                    [gu[:, c0:c1, two, bass.ds(t * 256, 256)] for two in range(2)], split)
        weights.add(f"down_{name}", 8, DOWN, 256, lambda t, c0, c1:
                    down_[:, t % 2, c0:c1, t // 2 * 256:t // 2 * 256 + 256], split)

    def add_conv(name, split=True):
        weights.add(f"conv_{name}", 6, EVEN, 512,
                    columns(a["conv_w_in_2"][0], range(0, 3072, 512)), split)
        weights.add(f"convout_{name}", 2, EVEN, 512,
                    columns(a["conv_w_out_2"][0], range(0, 1024, 512)), split)

    for l in range(DEPTH):
        add_block_1(l)
        weights.add(f"mod{l}", 18, EVEN, 512, columns(w("w_mod_2", l), range(0, 9216, 512)), False)
        if l == 0:
            add_ffn("z00", 0, 0, False)
            add_conv("z", False)
        else:
            add_ffn("z01", 0, 1, False)
            add_ffn("z10", 1, 0, False)
            kv = a["attn_w_qkv_2"][0].rearrange("(c p) n -> p c n", p=P)
            weights.add("kv_z", 2, EVEN, 256, lambda t, c0, c1:
                        kv[:, c0:c1, CHUNK_KV + t * 256:CHUNK_KV + (t + 1) * 256], False)
    add_ffn("x00", 0, 0)
    add_conv("x")
    add_ffn("x01", 0, 1)
    add_ffn("x10", 1, 0)
    weights.add("qkv", 3, EVEN, 512, columns(a["attn_w_qkv_2"][0], range(0, 1536, 512)))
    weights.add("attn_o", 2, EVEN, 512, columns(a["attn_w_o_2"][0], range(0, 1024, 512)))
    add_ffn("x11", 1, 1)

    begin_stretch("setup", 1024, 0)
    vrows = carve((4, P))[0]
    V_C, V_C2, V_CCTX, V_BADA = 0, 8, 16, 24
    V_BMOD = 0
    V_LB, V_HGG = 0, 8
    V_NG, V_CW = 16, 112
    with nc.Block() as block:
        @block.sync
        def _(sp):
            def small(dst, src):
                sp.dma_start(dst, src).then_inc(loaded.sem, 16)
                loaded.base += 16
            small(vrows[V_C:V_C + 8, 0, :], a["c"].rearrange("a (r p) -> (a r) p", p=P))
            small(vrows[V_C2:V_C2 + 8, 0, :], a["c_2"].rearrange("a (r p) -> (a r) p", p=P))
            small(vrows[V_CCTX:V_CCTX + 8, 0, :], a["c_ctx_2"].rearrange("(r p) -> r p", p=P))
            small(vrows[V_BADA:V_BADA + 96, 0, :], a["b_ada"].rearrange("l (r p) -> (l r) p", p=P))
            for l in range(DEPTH):
                small(vrows[0:72, 1 + l, :], a["b_mod_2"][l].rearrange("(r p) -> r p", p=P))
            small(vrows[V_LB:V_LB + 8, 3, :], a["lb_logits"].rearrange("l (r p) -> (l r) p", p=P))
            small(vrows[V_HGG:V_HGG + 8, 3, :], a["hg_norm_g"].rearrange("l (r p) -> (l r) p", p=P))
            small(vrows[V_NG:V_NG + 96, 3, :], a["norm_g_2"].rearrange("l k (r p) -> (l k r) p", p=P))
            cw = a["conv_w_2"][0].rearrange("k (r p) -> (k r) p", p=P)
            small(vrows[V_CW:V_CW + 16, 3, :], cw[0:16, :])
            small(vrows[72:80, 1, :], cw[16:24, :])
            small(ident[:], a["k_ident"])
            small(tri[:], a["k_tri"])
            small(before[:], a["k_before"])
            small(before_neg[:], a["k_before_neg"])
            small(level_mask[:], a["k_levels"])
            small(iota16[:], a["k_iota16"])
            small(x_tok[:], a["x"][0].rearrange("(t p) d -> p t d", p=P))
            small(z_tok[:], a["ctx_2"][0].rearrange("(t p) d -> p t d", p=P))
            weights.ahead_loads(sp, 0)

        group_rows = (120, 80, 72, 128)

        @block.tensor
        def _(pe):
            pe.wait_ge(loaded.sem, loaded.base)
            for g, n in enumerate(group_rows):
                pe.transpose(ps[:, 0, g * P:g * P + n], vrows[0:n, g, :], ident[0:n, 0:n]) \
                    .then_inc(pe_done.sem, 1)

        @block.scalar
        def _(act):
            act.wait_ge(vec_ready.sem, vec_ready.at(1))
            for k, at in enumerate((V_C, V_C2, V_CCTX)):
                ins = act.activation(condT[:, :, k], vcol[:, 0, at:at + 8], ACT.Silu)
            ins.then_inc(act_ready.sem, 1)
            act.wait_ge(act_ready.sem, act_ready.at(1))
            act.activation(stat[:, 8:9], condT[:, 0, 0:1], ACT.Copy).then_inc(rows_rounded.sem, 1)
            act.activation(cond_parts[:, :, 0], condT[:, :, 0], ACT.Copy).then_inc(act_ready.sem, 1)
            weights.split_hi(act, weights.first_tile(weights.group()))

        @block.vector
        def _(dve):
            v = Steps(dve, vec_step)
            v.tick(dve.memset(ones[:], 1.0))
            dve.wait_ge(pe_done.sem, pe_done.at(4))
            for g, n in enumerate(group_rows):
                ins = dve.tensor_copy(vcol[:, g, 0:n], ps[:, 0, g * P:g * P + n])
                if g < 3:
                    v.tick(ins)
            ins.then_inc(vec_ready.sem, 1)
            dve.wait_ge(vec_ready.sem, vec_ready.at(1))
            v.tick(dve.memset(lbcol[:, 0, 0, :], 0.0))
            v.link(dve.tensor_tensor(lbcol[:, 1, 0, :], vcol[:, 3, V_LB:V_LB + 4],
                                     vcol[:, 3, V_LB + 4:V_LB + 8], ALU.subtract))
            for u in range(2):
                dve.memset(stat[:, u:u + 1], 0.0).then_inc(unit_free[u].sem, 1)
            dve.memset(stat[:, 2:3], 0.0).then_inc(row_used.sem, GR)
            dve.memset(stat[:, 3:4], 0.0).then_inc(used.sem, QUARTERS)
            dve.memset(stat[:, 4:5], 0.0).then_inc(slot_summed.sem, 4)
            dve.memset(stat[:, 5:6], 0.0).then_inc(dots_kept.sem, 1)
            dve.memset(stat[:, 6:7], 0.0).then_inc(rows_split.sem, 1)
            dve.wait_ge(act_ready.sem, act_ready.at(2))
            v.tick(dve.tensor_tensor(cond_parts[:, :, 1], condT[:, :, 0],
                                     cond_parts[:, :, 0].bitcast(F32), ALU.subtract))
            weights.split_lo(dve, weights.first_tile(weights.group()))

    pe_done.base += 4
    vec_ready.base += 1
    act_ready.base += 2

    with nc.Block() as block:
        @block.scalar
        def _(act):
            s = Steps(act, act_step)
            s.link(act.activation(lbcol[:, 1, 0, :], lbcol[:, 1, 0, :], ACT.Sigmoid, scale=-1.0))

        @block.vector
        def _(dve):
            dve.wait_ge(act_step.sem, act_step.base)
            for l in range(DEPTH):
                dve.tensor_scalar(lbcol[:, l, 1, :], lbcol[:, l, 0, :], -1.0, 1.0,
                                  ALU.mult, ALU.add)

    def unit_wait(eng, j, turn):
        eng.wait_ge(unit_free[j].sem, turn + unit_free[j].at(1))

    def units_used(n):
        for u in range(2):
            unit_free[u].base += (n + 1 - u) // 2

    def passes(w_parts, x_parts):
        (wh, wl), (xh, xl) = w_parts, x_parts
        return ((wh, xh), (wh, xl), (wl, xh))

    def product(pe, out_, x_slices, w_slices, weights_stay, start, stop):
        combos = passes(w_slices, x_slices) if len(w_slices) == 2 else [w_slices + x_slices]
        for n, (wv, xv) in enumerate(combos):
            stay, move = (wv, xv) if weights_stay else (xv, wv)
            mm = pe.matmul(out_, stay, move, start=start and n == 0,
                           stop=stop and n == len(combos) - 1, skip_group_check=True)
        return mm

    def project_features(pe, t, bank, x_parts, j=None, turn=None):
        g = weights.group()
        last = sum(g.chunks) - 1
        if j is None:
            j, turn = t % 2, t // 2
        for start, n, parts in weights.sections(pe, t, j, turn):
            for b in range(g.cols // P):
                for c in range(n):
                    row = start + c
                    mm = product(pe, bank(b), [x[:, row, :] for x in x_parts],
                                 [w_[:, c, b * P:(b + 1) * P] for w_ in parts], True,
                                 row == 0 and b % 2 == 0, row == last)
            weights.section_done(mm)

    def project_tokens(pe, t, place, x_parts, chunk0=0, opens=True, closes=True):
        g = weights.group()
        last = sum(g.chunks) - 1
        for start, n, parts in weights.sections(pe, t, t % 2, t // 2):
            for m in range(TT):
                for c in range(n):
                    row = start + c
                    mm = product(pe, place(m),
                                 [x[:, chunk0 + row, m * P:(m + 1) * P] for x in x_parts],
                                 [w_[:, c, :] for w_ in parts], False,
                                 opens and row == 0, closes and row == last)
            weights.section_done(mm)

    def blocks_of(unit):
        return lambda b: ps[:, unit, b * SEQ:(b + 1) * SEQ]

    def tiles_of(unit, width=512):
        return lambda m: ps[:, unit, m * 512:m * 512 + width]

    def split_ahead(act=None, dve=None, tile=None):
        if not weights.group().split:
            return
        if act is not None:
            weights.split_hi(act, weights.next_tile(*tile))
        if dve is not None:
            weights.split_lo(dve, weights.next_tile(*tile))

    def product_wait(eng, t):
        weights.wait_product(eng, t)

    def ada_modulation(l):
        n = 12
        dst, bias = adacol[:, l, :], vcol[:, 0, V_BADA + 48 * l:V_BADA + 48 * (l + 1)]
        row = arena[0:2, 0:1024].rearrange("k (u n) -> k u n", u=2)
        weights.begin(f"ada{l}")
        with nc.Block() as block:
            @block.sync
            def _(sp):
                weights.feed(sp)

            @block.tensor
            def _(pe):
                def turn_row(t, j):
                    pe.wait_ge(mod_rows.sem, t + mod_rows.at(1))
                    for b in range(4):
                        mm = pe.matmul(ps[:, j, 512 + b:513 + b], row[:, j, b * P:(b + 1) * P],
                                       ones[0:2, 0:1], start=True, stop=True)
                    mm.then_inc(mod_turned.sem, 1)

                def tile(t, j, turn):
                    unit_wait(pe, j, turn)
                    for start, chunks, parts in weights.sections(pe, t, j, turn):
                        for c in range(chunks):
                            for k, part in enumerate(parts):
                                mm = pe.matmul(ps[0:2, j, 0:512], cond_parts[:, start + c, :],
                                               part[:, c, :], start=start + c == 0 and k == 0,
                                               stop=start + c == KC - 1 and k == 1)
                        weights.section_done(mm)
                    if j == 1:
                        turn_row(t - 1, 0)
                        turn_row(t, 1)
                in_pairs(n, pe, tile)

            @block.scalar
            def _(act):
                def tile(t, j, turn):
                    split_ahead(act=act, tile=(t, j, turn))
                    product_wait(act, t)
                    act.copy(row[:, j, :], ps[0:2, j, 0:512]).then_inc(mod_rows.sem, 1)
                with_last(n, act, tile)

            @block.vector
            def _(dve):
                def tile(t, j, turn):
                    split_ahead(dve=dve, tile=(t, j, turn))
                    if j == 1:
                        for back in (1, 0):
                            u = t - back
                            dve.wait_ge(mod_turned.sem, u + mod_turned.at(1))
                            at = bass.ds(u * 4, 4)
                            dve.tensor_tensor(dst[:, at], ps[:, 1 - back, 512:516], bias[:, at],
                                              ALU.add).then_inc(unit_free[1 - back].sem, 1)
                with_last(n, dve, tile)
        units_used(n)
        mod_rows.base += n
        mod_turned.base += n
        weights.end()

    def modulated_features(src, scale, shift, full, gain=None, whole=False):
        normed = y_tok
        with nc.Block() as block:
            @block.tensor
            def _(pe):
                tokens = src if gain is None else normed
                for t in range(TT):
                    if gain is not None:
                        pe.wait_ge(vec_ready.sem, vec_ready.at(2 + t))
                    for c in range(KC):
                        mm = pe.transpose(ps[:, t, c * P:(c + 1) * P],
                                          tokens[:, t, c * P:(c + 1) * P], ident[:])
                    mm.then_inc(pe_done.sem, 1)

            @block.scalar
            def _(act):
                s_ = Steps(act, act_step)
                if gain is not None:
                    act.wait_ge(vec_ready.sem, vec_ready.at(1))
                    act.activation(stat[:, 2:4], stat[:, 0:2], ACT.Sqrt).then_inc(turned.sem, 1)
                act.wait_ge(cols_ready.sem, cols_ready.at(1))
                act.wait_ge(pe_done.sem, pe_done.at(1))
                for c in range(KC):
                    s_.tick(act.activation(full[:, c, 0:P], ps[:, 0, c * P:(c + 1) * P], ACT.Identity,
                                           bias=shift(c), scale=scol[:, c:c + 1]))
                s_.wait()
                if whole:
                    return
                act.activation(hT_hi[:, :, 0:P], full[:, :, 0:P], ACT.Copy).then_inc(act_ready.sem, 1)

            @block.vector
            def _(dve):
                v = Steps(dve, vec_step)
                if gain is None:
                    dve.tensor_scalar(scol[:], scale, 1.0, None, ALU.add).then_inc(cols_ready.sem, 1)
                else:
                    dve.scalar_tensor_tensor(out=scol[:], in0=scale, scalar=1.0, in1=gain,
                                             op0=ALU.add, op1=ALU.mult).then_inc(cols_ready.sem, 1)
                    for t in range(TT):
                        v.tick(dve.tensor_tensor_reduce(normed[:, t, :], src[:, t, :], src[:, t, :],
                                                        1.0, 0.0, ALU.mult, ALU.add,
                                                        stat[:, t:t + 1]))
                    v.wait()
                    dve.tensor_scalar(stat[:, 0:2], stat[:, 0:2], 1.0 / D, RMS_EPS,
                                      ALU.mult, ALU.add).then_inc(vec_ready.sem, 1)
                    dve.wait_ge(turned.sem, turned.at(1))
                    v.link(dve.reciprocal(stat[:, 4:6], stat[:, 2:4]))
                    for t in range(TT):
                        dve.tensor_scalar(normed[:, t, :], src[:, t, :], stat[:, 4 + t:5 + t], None,
                                          ALU.mult).then_inc(vec_ready.sem, 1)
                dve.wait_ge(cols_ready.sem, cols_ready.at(1))
                dve.wait_ge(pe_done.sem, pe_done.at(2))
                for c in range(KC):
                    v.tick(dve.tensor_scalar(full[:, c, P:SEQ], ps[:, 1, c * P:(c + 1) * P],
                                             scol[:, c:c + 1], shift(c), ALU.mult, ALU.add))
                if whole:
                    return
                v.wait()
                v.link(dve.tensor_copy(hT_hi[:, :, P:SEQ], full[:, :, P:SEQ]))
                dve.wait_ge(act_ready.sem, act_ready.at(1))
                v.tick(dve.tensor_tensor(hT_lo[:], full, hT_hi[:].bitcast(F32), ALU.subtract))
        cols_ready.base += 1
        pe_done.base += 2
        if not whole:
            act_ready.base += 1
        if gain is not None:
            vec_ready.base += 3
            turned.base += 1

    def broadcast_row(pe, column, unit):
        for c in range(KC):
            mm = pe.matmul(ps[:, unit, c * P:(c + 1) * P], column(c).to_broadcast([P, P]), ident[:],
                           start=True, stop=True)
        return mm

    def input_projection(l, qa, sg, km, ia, ga, qb, kb, vb):
        weights.begin(f"in{l}")
        flat = {0: qa, 2: qb, 3: kb}
        tokens = {4: ia, 6: vb}
        n = 7
        with nc.Block() as block:
            @block.sync
            def _(sp):
                weights.feed(sp)

            @block.tensor
            def _(pe):
                for t in range(n):
                    unit_wait(pe, t % 2, t // 2)
                    if t in (4, 5, 6):
                        project_tokens(pe, t, tiles_of(t % 2), hT)
                    else:
                        project_features(pe, t, blocks_of(t % 2), hT)

            @block.scalar
            def _(act):
                for t in range(n):
                    split_ahead(act=act, tile=(t, t % 2, t // 2))
                    if t == 1:
                        product_wait(act, t)
                        act.activation(sg.rearrange("p h t -> p (h t)"), ps[:, t % 2, :], ACT.Sigmoid)
                        act.activation(km.rearrange("p h t -> p (h t)"), ps[:, t % 2, :],
                                       ACT.Sigmoid, scale=-1.0).then_inc(unit_free[t % 2].sem, 1)
                    elif t == 5:
                        product_wait(act, t)
                        act.activation(ga.rearrange("p t n -> p (t n)"), ps[:, t % 2, :],
                                       ACT.Sigmoid).then_inc(act_ready.sem, 1)

            @block.vector
            def _(dve):
                for t in range(n):
                    split_ahead(dve=dve, tile=(t, t % 2, t // 2))
                    if t == 1:
                        continue
                    product_wait(dve, t)
                    if t == 5:
                        dve.wait_ge(act_ready.sem, act_ready.at(1))
                        g = ga.rearrange("p t n -> p (t n)")
                        dve.tensor_tensor(g, ps[:, t % 2, :], g, ALU.mult) \
                           .then_inc(unit_free[t % 2].sem, 1)
                    else:
                        dst = flat.get(t, tokens.get(t)).rearrange("p h t -> p (h t)")
                        dve.tensor_copy(dst, ps[:, t % 2, :]).then_inc(unit_free[t % 2].sem, 1)
        act_ready.base += 1
        units_used(n)
        weights.end()

    def gate_projection(l, gates):
        weights.begin(f"gates{l}")
        with nc.Block() as block:
            @block.sync
            def _(sp):
                weights.feed(sp)

            @block.tensor
            def _(pe):
                for t in range(4):
                    unit_wait(pe, t % 2, t // 2)
                    project_features(pe, t, blocks_of(t % 2), hT)

            @block.scalar
            def _(act):
                for t in range(4):
                    split_ahead(act=act, tile=(t, t % 2, t // 2))
                    product_wait(act, t)
                    g = gates[:, t * 4:(t + 1) * 4, :].rearrange("p b t -> p (b t)")
                    act.activation(g, ps[:, t % 2, :], ACT.Sigmoid).then_inc(unit_free[t % 2].sem, 1)

            @block.vector
            def _(dve):
                for t in range(4):
                    split_ahead(dve=dve, tile=(t, t % 2, t // 2))
        units_used(4)
        weights.end()

    def hgrn(l, qa, sg, km, ia, ga, oaT, tmp):
        B, E, qe, ke, scores, cross, o, sq = tmp
        blocks = HG_HEADS * TT
        NL = len(LEVELS)
        with nc.Block() as block:
            @block.tensor
            def _(pe):
                pe.wait_ge(vec_ready.sem, vec_ready.at(1))
                for h in range(HG_HEADS):
                    for t in range(TT):
                        b = h * TT + t
                        mm = pe.matmul(ps[:, 0, b * P:(b + 1) * P], km[:, h, t * P:(t + 1) * P],
                                       qa[:, h, t * P:(t + 1) * P], start=True, stop=True)
                mm.then_inc(pe_done.sem, 1)
                for n in range(NL):
                    pe.wait_ge(vec_ready.sem, vec_ready.at(2 + n))
                    for b in range(blocks):
                        mm = pe.matmul(ps[:, (n + 1) % 2, b * P:(b + 1) * P],
                                       ke[:, b * P:(b + 1) * P], qe[:, b * P:(b + 1) * P],
                                       start=True, stop=True)
                    mm.then_inc(pe_done.sem, 1)
                pe.wait_ge(vec_ready.sem, vec_ready.at(2 + NL))
                for h in range(HG_HEADS):
                    mm = pe.matmul(ps[:, 2, h * P:(h + 1) * P], ke[:, 2 * h * P:(2 * h + 1) * P],
                                   qe[:, (2 * h + 1) * P:(2 * h + 2) * P], start=True, stop=True)
                mm.then_inc(pe_done.sem, 1)
                pe.wait_ge(vec_ready.sem, vec_ready.at(3 + NL))
                for t in range(TT):
                    for h in range(HG_HEADS):
                        b = h * TT + t
                        dst = ps[:, 3, t * 512 + h * P:t * 512 + (h + 1) * P]
                        mm = pe.matmul(dst, scores[:, b * P:(b + 1) * P], ia[:, t, h * P:(h + 1) * P],
                                       start=True, stop=(t == 0))
                        if t == 1:
                            mm = pe.matmul(dst, cross[:, h * P:(h + 1) * P],
                                           ia[:, 0, h * P:(h + 1) * P], start=False, stop=True)
                mm.then_inc(pe_done.sem, 1)
                pe.wait_ge(vec_ready.sem, vec_ready.at(5 + NL))
                for h in range(HG_HEADS):
                    for t in range(TT):
                        mm = pe.transpose(ps[:, 0, h * SEQ + t * P:h * SEQ + (t + 1) * P],
                                          o[:, t, h * P:(h + 1) * P], ident[:])
                mm.then_inc(pe_done.sem, 1)

            @block.scalar
            def _(act):
                act.wait_ge(cols_ready.sem, cols_ready.at(1))
                act.activation(sg.rearrange("p h t -> p (h t)"), sg.rearrange("p h t -> p (h t)"),
                               ACT.Ln).then_inc(act_ready.sem, 1)
                for n in range(NL + 1):
                    act.wait_ge(cols_ready.sem, cols_ready.at(2 + n))
                    act.activation(E[:], E[:], ACT.Exp).then_inc(act_ready.sem, 1)
                act.wait_ge(vec_ready.sem, vec_ready.at(4 + NL))
                act.activation(stat[:, 8:16], stat[:, 0:8], ACT.Sqrt).then_inc(act_ready.sem, 1)

            @block.vector
            def _(dve):
                v = Steps(dve, vec_step)
                v.tick(dve.memset(qe[:], 0.0))
                v.tick(dve.memset(ke[:], 0.0))
                v.tick(dve.memset(scores[:], 0.0))
                for h in range(HG_HEADS):
                    ins = dve.tensor_scalar(sg[:, h, :], sg[:, h, :], lbcol[:, l, 1, h:h + 1],
                                            lbcol[:, l, 0, h:h + 1], ALU.mult, ALU.add)
                    if h < HG_HEADS - 1:
                        v.tick(ins)
                v.wait()
                ins.then_inc(cols_ready.sem, 1)
                for h in range(HG_HEADS):
                    ins = dve.tensor_scalar(km[:, h, :], km[:, h, :], lbcol[:, l, 1, h:h + 1], None,
                                            ALU.mult)
                    if h < HG_HEADS - 1:
                        v.tick(ins)
                v.wait()
                ins.then_inc(vec_ready.sem, 1)
                dve.wait_ge(act_ready.sem, act_ready.at(1))
                for h in range(HG_HEADS):
                    for t in range(TT):
                        b = h * TT + t
                        v.tick(dve.tensor_tensor_scan(
                            B[:, b * P:(b + 1) * P], ones[:], sg[:, h, t * P:(t + 1) * P], 0.0,
                            ALU.mult, ALU.add))
                v.wait()
                q_all = qa.rearrange("p h t -> p (h t)")
                k_all = km.rearrange("p h t -> p (h t)")

                def take(n):
                    dve.wait_ge(pe_done.sem, pe_done.at(n + 1))
                    mask = level_mask[:, n, :].unsqueeze(1).to_broadcast([P, blocks, P])
                    v.link(dve.copy_predicated(
                        scores.rearrange("p (b t) -> p b t", t=P), mask,
                        ps[:, n % 2, :].rearrange("p (b t) -> p b t", t=P)))

                for n, m in enumerate(LEVELS):
                    nb = 1024 // (2 * m)

                    def halves(ap):
                        r = ap.rearrange("p (b two m) -> p b two m", two=2, m=m)
                        return r[:, :, 0, :], r[:, :, 1, :]
                    b_lo, b_hi = halves(B)
                    e_lo, e_hi = halves(E)
                    mid = b_lo[:, :, m - 1:m].to_broadcast([P, nb, m])
                    v.tick(dve.tensor_tensor(e_hi, b_hi, mid, ALU.subtract))
                    v.wait()
                    dve.tensor_tensor(e_lo, mid, b_lo, ALU.subtract).then_inc(cols_ready.sem, 1)
                    if n >= 1:
                        take(n - 1)
                    dve.wait_ge(act_ready.sem, act_ready.at(2 + n))
                    if n >= 1:
                        dve.wait_ge(pe_done.sem, pe_done.at(n + 1))
                    v.link(dve.tensor_tensor(halves(qe)[1], halves(q_all)[1], e_hi, ALU.mult))
                    dve.tensor_tensor(halves(ke)[0], halves(k_all)[0], e_lo, ALU.mult) \
                       .then_inc(vec_ready.sem, 1)
                    dve.wait_ge(vec_ready.sem, vec_ready.at(2 + n))
                tiles = [ap.rearrange("p (h t m) -> p h t m", t=TT, m=P) for ap in (B, E, qe, ke, q_all, k_all)]
                tb, te, tq, tk, tqa, tka = tiles
                v.link(dve.tensor_copy(te[:, :, 1, :], tb[:, :, 1, :]))
                dve.tensor_tensor(te[:, :, 0, :], tb[:, :, 0, P - 1:P].to_broadcast([P, HG_HEADS, P]),
                                  tb[:, :, 0, :], ALU.subtract).then_inc(cols_ready.sem, 1)
                take(NL - 1)
                dve.wait_ge(act_ready.sem, act_ready.at(2 + NL))
                dve.wait_ge(pe_done.sem, pe_done.at(NL + 1))
                v.link(dve.tensor_tensor(tq[:, :, 1, :], tqa[:, :, 1, :], te[:, :, 1, :], ALU.mult))
                dve.tensor_tensor(tk[:, :, 0, :], tka[:, :, 0, :], te[:, :, 0, :], ALU.mult) \
                   .then_inc(vec_ready.sem, 1)
                take(NL)
                dve.wait_ge(pe_done.sem, pe_done.at(NL + 2))
                dve.tensor_copy(cross[:], ps[:, 2, 0:512]).then_inc(vec_ready.sem, 1)
                dve.wait_ge(pe_done.sem, pe_done.at(NL + 3))
                o_flat = o.rearrange("p t n -> p (t n)")
                v.link(dve.tensor_copy(o_flat, ps[:, 3, :]))
                v.link(dve.tensor_tensor(sq[:], o_flat, o_flat, ALU.mult))
                v.link(dve.tensor_reduce(stat[:, 0:8], sq.rearrange("p (b e) -> p b e", e=P), AX_X,
                                         ALU.add))
                dve.tensor_scalar(stat[:, 0:8], stat[:, 0:8], 1.0 / P, RMS_EPS, ALU.mult, ALU.add) \
                   .then_inc(vec_ready.sem, 1)
                v.link(dve.tensor_tensor(o_flat, o_flat, ga.rearrange("p t n -> p (t n)"), ALU.mult))
                dve.wait_ge(act_ready.sem, act_ready.at(3 + NL))
                v.link(dve.reciprocal(stat[:, 16:24], stat[:, 8:16]))
                o_heads = o_flat.rearrange("p (b e) -> p b e", e=P)
                dve.tensor_tensor(o_heads, o_heads,
                                  stat[:, 16:24].unsqueeze(2).to_broadcast([P, 8, P]), ALU.mult) \
                   .then_inc(vec_ready.sem, 1)
                dve.wait_ge(pe_done.sem, pe_done.at(4 + NL))
                for part in range(2):
                    for h in range(HG_HEADS):
                        gain = vcol[:, 3, V_HGG + 4 * l + h:V_HGG + 4 * l + h + 1]
                        src = ps[:, 0, h * SEQ:(h + 1) * SEQ]
                        if part == 0:
                            v.tick(dve.tensor_scalar(oaT[0][:, h, :], src, gain, None, ALU.mult))
                        else:
                            v.tick(dve.scalar_tensor_tensor(
                                out=oaT[1][:, h, :], in0=src, scalar=gain,
                                in1=oaT[0][:, h, :].bitcast(F32), op0=ALU.mult, op1=ALU.subtract))
                    v.wait()
        cols_ready.base += 2 + NL
        vec_ready.base += 5 + NL
        act_ready.base += 3 + NL
        pe_done.base += 4 + NL

    def stick_breaking(qb, kb, vb, obT, tmp):
        Y, L, S = tmp
        scale = 1.0 / math.sqrt(SB_DH)
        groups = SB_HEADS // 4
        W_ = SEQ + P

        def unit(base, n):
            return ps[:, base + n // 2, (n % 2) * 512:(n % 2) * 512 + W_]

        def both(base):
            return ps[:, base:base + 2, :].rearrange("p u (h n) -> p u h n", h=2)[:, :, :, 0:W_]

        def by_unit(ap):
            return ap.rearrange("p (u h) n -> p u h n", h=2)

        with nc.Block() as block:
            @block.tensor
            def _(pe):
                for g in range(groups):
                    if g:
                        pe.wait_ge(vec_ready.sem, vec_ready.at(3 * g))
                    for n in range(4):
                        h = 4 * g + n
                        at = slice(64 * (h % 2), 64 * (h % 2) + 64)
                        u = unit(0, n)
                        pe.matmul(u[:, 0:SEQ], kb[at, h // 2, 0:P], qb[at, h // 2, :],
                                  start=True, stop=True)
                        mm = pe.matmul(u[:, SEQ:W_], kb[at, h // 2, P:SEQ], qb[at, h // 2, P:SEQ],
                                       start=True, stop=True)
                    mm.then_inc(pe_done.sem, 1)
                    pe.wait_ge(vec_ready.sem, vec_ready.at(3 * g + 1))
                    for n in range(4):
                        u = unit(2, n)
                        pe.matmul(u[:, 0:SEQ], tri[:], L[:, n, 0:SEQ], start=True, stop=False)
                        pe.matmul(u[:, P:SEQ], ones[:], L[:, n, SEQ:W_], start=False, stop=True)
                        mm = pe.matmul(u[:, SEQ:W_], tri[:], L[:, n, SEQ:W_], start=True, stop=True)
                    mm.then_inc(pe_done.sem, 1)
                    pe.wait_ge(act_ready.sem, act_ready.at(4 * g + 4))
                    for n in range(4):
                        h = 4 * g + n
                        dst = ps[64 * (h % 2):64 * (h % 2) + 64, 0, (n // 2) * SEQ:(n // 2 + 1) * SEQ]
                        pe.matmul(dst, vb[:, 0, h * 64:(h + 1) * 64], S[:, n, 0:SEQ],
                                  start=True, stop=False, skip_group_check=True)
                        mm = pe.matmul(dst[:, P:SEQ], vb[:, 1, h * 64:(h + 1) * 64], S[:, n, SEQ:W_],
                                       start=False, stop=True, skip_group_check=True)
                    mm.then_inc(pe_done.sem, 1)

            @block.scalar
            def _(act):
                s = Steps(act, act_step)
                for g in range(groups):
                    act.wait_ge(pe_done.sem, pe_done.at(3 * g + 1))
                    act.activation(by_unit(Y), both(0), ACT.Copy, scale=scale) \
                       .then_inc(act_ready.sem, 1)
                    act.wait_ge(act_ready.sem, act_ready.at(4 * g + 1))
                    if g:
                        act.wait_ge(vec_ready.sem, vec_ready.at(3 * g))
                    s.link(act.activation(L[:], Y[:], ACT.Abs))
                    s.link(act.activation(L[:], L[:], ACT.Exp, scale=-1.0))
                    act.activation(L[:], L[:], ACT.Ln, bias=1.0).then_inc(act_ready.sem, 1)
                    act.wait_ge(vec_ready.sem, vec_ready.at(3 * g + 2))
                    act.activation(S[:], S[:], ACT.Exp).then_inc(act_ready.sem, 2)

            @block.vector
            def _(dve):
                v = Steps(dve, vec_step)
                for g in range(groups):
                    dve.wait_ge(act_ready.sem, act_ready.at(4 * g + 2))
                    v.link(dve.scalar_tensor_tensor(out=L[:], in0=Y[:], scalar=0.0, in1=L[:],
                                                    op0=ALU.max, op1=ALU.add))
                    mask = before[:].unsqueeze(1).to_broadcast([P, 4, P])
                    v.link(dve.tensor_tensor(L[:, :, 0:P], L[:, :, 0:P], mask, ALU.mult))
                    dve.tensor_tensor(L[:, :, SEQ:W_], L[:, :, SEQ:W_], mask, ALU.mult) \
                       .then_inc(vec_ready.sem, 1)
                    dve.wait_ge(pe_done.sem, pe_done.at(3 * g + 2))
                    v.link(dve.tensor_tensor(by_unit(S), by_unit(Y), both(2), ALU.subtract))
                    neg = before_neg[:].unsqueeze(1).to_broadcast([P, 4, P])
                    v.link(dve.tensor_tensor(S[:, :, 0:P], S[:, :, 0:P], neg, ALU.add))
                    dve.tensor_tensor(S[:, :, SEQ:W_], S[:, :, SEQ:W_], neg, ALU.add) \
                       .then_inc(vec_ready.sem, 1)
                    dve.wait_ge(pe_done.sem, pe_done.at(3 * g + 3))
                    hi, lo = [o[:, 2 * g:2 * g + 2, :].rearrange("p c t -> p (c t)") for o in obT]
                    v.link(dve.tensor_copy(hi, ps[:, 0, 0:512]))
                    dve.tensor_tensor(lo, ps[:, 0, 0:512], hi.bitcast(F32), ALU.subtract) \
                       .then_inc(vec_ready.sem, 1)
        vec_ready.base += 3 * groups
        act_ready.base += 4 * groups
        pe_done.base += 3 * groups

    def merge(l, oaT, obT, gates):
        weights.begin(f"up{l}")
        with nc.Block() as block:
            @block.sync
            def _(sp):
                weights.feed(sp)

            @block.tensor
            def _(pe):
                for k, src in enumerate((oaT, obT)):
                    project_features(pe, k, lambda b, k=k: ps[:, 2 * k + b // 4,
                                                              b % 4 * SEQ:(b % 4 + 1) * SEQ], src)

            @block.scalar
            def _(act):
                for t in range(2):
                    split_ahead(act=act, tile=(t, t, 0))
                act.wait_ge(vec_ready.sem, vec_ready.at(1))
                act.activation(hT_hi[:], gates[:, 0:KC, :], ACT.Copy).then_inc(act_ready.sem, 1)

            @block.vector
            def _(dve):
                v = Steps(dve, vec_step)
                for k in range(2):
                    split_ahead(dve=dve, tile=(k, k, 0))
                    product_wait(dve, k)
                    g = gates[:, k * KC:(k + 1) * KC, :].rearrange("p (u b) t -> p u (b t)", u=2)
                    v.link(dve.tensor_tensor(g, g, ps[:, 2 * k:2 * k + 2, :], ALU.mult))
                dve.tensor_tensor(gates[:, 0:KC, :], gates[:, 0:KC, :], gates[:, KC:2 * KC, :],
                                  ALU.add).then_inc(vec_ready.sem, 1)
                dve.wait_ge(act_ready.sem, act_ready.at(1))
                v.tick(dve.tensor_tensor(hT_lo[:], gates[:, 0:KC, :], hT_hi[:].bitcast(F32),
                                         ALU.subtract))
        vec_ready.base += 1
        act_ready.base += 1
        weights.end()

    def residual_norm(dve, act_, v, pieces, gate, gain, shift):
        for t, c0, part in pieces:
            cols = slice(c0, c0 + 512)
            v.link(dve.tensor_tensor(y_tok[:, t, cols], part, gate[:, cols], ALU.mult))
            v.link(dve.scalar_tensor_tensor(out=x_tok[:, t, cols], in0=x_tok[:, t, cols],
                                            scalar=DN_ALPHA, in1=y_tok[:, t, cols],
                                            op0=ALU.mult, op1=ALU.add))
        for t in range(TT):
            for k in range(2):
                v.link(dve.bn_stats(stat[:, 16 + 12 * t + 6 * k:22 + 12 * t + 6 * k],
                                    x_tok[:, t, k * 512:(k + 1) * 512]))
            v.link(dve.bn_aggr(stat[:, 2 * t:2 * t + 2], stat[:, 16 + 12 * t:28 + 12 * t]))
        mean_var = stat[:, 0:4].rearrange("p (t k) -> p t k", k=2)
        dve.tensor_scalar(stat[:, 4:6], mean_var[:, :, 1], LN_EPS, None, ALU.add) \
           .then_inc(vec_ready.sem, 1)
        dve.wait_ge(act_ready.sem, act_ready.at(act_))
        v.link(dve.reciprocal(stat[:, 8:10], stat[:, 6:8]))
        for t in range(TT):
            v.link(dve.tensor_scalar(x_tok[:, t, :], x_tok[:, t, :], stat[:, 2 * t:2 * t + 1],
                                     stat[:, 8 + t:9 + t], ALU.subtract, ALU.mult))
            v.link(dve.tensor_tensor(x_tok[:, t, :], x_tok[:, t, :], gain, ALU.mult))
            v.tick(dve.tensor_tensor(x_tok[:, t, :], x_tok[:, t, :], shift, ALU.add))

    def load_rows(sp, l, k):
        sp.dma_start(rows[:, 1, :], a["ln_g"][l, k:k + 1, :].to_broadcast([P, D])) \
          .then_inc(loaded.sem, 16)
        sp.dma_start(rows[:, 2, :], a["ln_b"][l, k:k + 1, :].to_broadcast([P, D])) \
          .then_inc(loaded.sem, 16)

    def output_projection(l):
        weights.begin(f"o{l}")
        with nc.Block() as block:
            @block.sync
            def _(sp):
                load_rows(sp, l, 0)
                weights.feed(sp)

            @block.tensor
            def _(pe):
                broadcast_row(pe, lambda c: adacol[:, l, 16 + c:17 + c], 2).then_inc(pe_done.sem, 1)
                for t in range(2):
                    project_tokens(pe, t, tiles_of(t), hT)

            @block.scalar
            def _(act):
                for t in range(2):
                    split_ahead(act=act, tile=(t, t, 0))
                act.wait_ge(pe_done.sem, pe_done.at(1))
                act.copy(rows[:, 0, :], ps[:, 2, :]).then_inc(act_ready.sem, 1)
                act.wait_ge(vec_ready.sem, vec_ready.at(1))
                act.activation(stat[:, 6:8], stat[:, 4:6], ACT.Sqrt).then_inc(act_ready.sem, 1)

            @block.vector
            def _(dve):
                v = Steps(dve, vec_step)
                for t in range(2):
                    split_ahead(dve=dve, tile=(t, t, 0))
                dve.wait_ge(act_ready.sem, act_ready.at(1))
                dve.wait_ge(loaded.sem, loaded.at(32))
                product_wait(dve, 1)
                pieces = [(t, k * 512, ps[:, k, t * 512:(t + 1) * 512])
                          for k in range(2) for t in range(TT)]
                residual_norm(dve, 2, v, pieces, rows[:, 0, :], rows[:, 1, :], rows[:, 2, :])
        loaded.base += 32
        pe_done.base += 1
        act_ready.base += 2
        vec_ready.base += 1
        weights.end()

    def peer_queries(l, hf_tok, pqT, keys, keysT, sc):
        weights.begin(f"pq{l}")
        with nc.Block() as block:
            @block.sync
            def _(sp):
                for half in range(2):
                    sp.dma_start(keys[:, :, half * 64:(half + 1) * 64],
                                 a["sub_keys"][l, half].rearrange("h n d -> n h d")) \
                      .then_inc(loaded.sem, 16)
                weights.feed(sp)

            @block.tensor
            def _(pe):
                for t in range(2):
                    project_features(pe, t, blocks_of(t), hT)
                broadcast_row(pe, lambda c: scol[:, c:c + 1], 2).then_inc(pe_done.sem, 1)
                broadcast_row(pe, lambda c: adacol[:, l, 24 + c:25 + c], 3).then_inc(pe_done.sem, 1)
                pe.wait_ge(loaded.sem, loaded.at(32))
                pe.wait_ge(act_ready.sem, act_ready.at(1))
                for h in range(PEER_HEADS):
                    mm = pe.transpose(ps[:, 2, h * P:(h + 1) * P], keys[:, h, :], ident[:])
                mm.then_inc(pe_done.sem, 1)
                pe.wait_ge(act_ready.sem, act_ready.at(4))
                for t in range(TT):
                    if t:
                        pe.wait_ge(act_ready.sem, act_ready.at(5))
                    for h in range(PEER_HEADS):
                        for half in range(2):
                            at = slice(64 * half, 64 * half + 64)
                            mm = pe.matmul(ps[:, half, h * P:(h + 1) * P],
                                           pqT[at, h, t * P:(t + 1) * P], keysT[at, h, :],
                                           start=True, stop=True)
                    mm.then_inc(pe_done.sem, 1)

            @block.scalar
            def _(act):
                for t in range(2):
                    split_ahead(act=act, tile=(t, t, 0))
                act.wait_ge(pe_done.sem, pe_done.at(1))
                act.copy(rows[:, 0, :], ps[:, 2, :]).then_inc(act_ready.sem, 1)
                product_wait(act, 1)
                for t in range(2):
                    ins = act.copy(pqT[:, 4 * t:4 * t + 4, :].rearrange("p b t -> p (b t)"),
                                   ps[:, t, :])
                    if t:
                        ins.then_inc(act_ready.sem, 1)
                act.wait_ge(pe_done.sem, pe_done.at(2))
                act.copy(rows[:, 1, :], ps[:, 3, :]).then_inc(act_ready.sem, 1)
                act.wait_ge(pe_done.sem, pe_done.at(3))
                act.copy(keysT.rearrange("p h n -> p (h n)"), ps[:, 2, :]).then_inc(act_ready.sem, 1)
                for t in range(TT):
                    act.wait_ge(pe_done.sem, pe_done.at(4 + t))
                    act.copy(sc[:, t], ps[:, 0:2, :]) \
                       .then_inc(act_ready.sem, 1)

            @block.vector
            def _(dve):
                v = Steps(dve, vec_step)
                for t in range(2):
                    split_ahead(dve=dve, tile=(t, t, 0))
                dve.wait_ge(act_ready.sem, act_ready.at(3))
                for t in range(TT):
                    v.link(dve.tensor_tensor(hf_tok[:, t, :], x_tok[:, t, :], rows[:, 0, :], ALU.mult))
                    v.link(dve.tensor_tensor(hf_tok[:, t, :], hf_tok[:, t, :], rows[:, 1, :], ALU.add))
        loaded.base += 32
        pe_done.base += 5
        act_ready.base += 6
        weights.end()

    def modulation_programs(l, row):
        n = 18

        def tensor(pe):
            def turn_row(t, j):
                pe.wait_ge(mod_rows.sem, t + mod_rows.at(1))
                for b in range(4):
                    mm = pe.matmul(ps[:, j, 512 + 2 * b:514 + 2 * b], row[:, j, b * P:(b + 1) * P],
                                   ident[0:2, 0:2], start=True, stop=True)
                mm.then_inc(mod_turned.sem, 1)

            def tile(t, j, turn):
                unit_wait(pe, j, turn)
                for start, chunks, (part,) in weights.sections(pe, t, j, turn):
                    for c in range(chunks):
                        mm = pe.matmul(ps[0:2, j, 0:512], condT[:, start + c, 1:3], part[:, c, :],
                                       start=start + c == 0, stop=start + c == KC - 1)
                    weights.section_done(mm)
                if j == 1:
                    turn_row(t - 1, 0)
                    turn_row(t, 1)
            in_pairs(n, pe, tile)

        def scalar(act, first, last):
            with act.Fori(first, last) as i:
                for j in range(2):
                    product_wait(act, i * 2 + j)
                    act.copy(row[:, j, :], ps[0:2, j, 0:512]).then_inc(mod_rows.sem, 1)
                for j in range(2):
                    act.wait_ge(mod_turned.sem, i * 2 + mod_turned.at(1 + j))
                    act.copy(modcol[:, l, bass.ds(i * 8 + 4 * j, 4), :],
                             ps[:, j, 512:520].rearrange("p (b k) -> p b k", k=2)) \
                       .then_inc(unit_free[j].sem, 1)
        return n, tensor, scalar

    def peer_select(l, sc, best, bestf, cand, pos, p12, eq, sel, index, gate):
        def top16(dve, v, values, idx, scores):
            v.link(dve.max(values[:, 0:8], scores))
            v.link(dve.max_index(idx[:, 0:8], values[:, 0:8], scores))
            v.link(dve.match_replace(scores, values[:, 0:8], scores, -3.0e38))
            v.link(dve.max(values[:, 8:16], scores))
            v.tick(dve.max_index(idx[:, 8:16], values[:, 8:16], scores))

        weights.begin(f"mod{l}")
        tiles, mod_tensor, mod_scalar = modulation_programs(
            l, rows[0:2, 0, :].rearrange("k (u n) -> k u n", u=2))
        with nc.Block() as block:
            @block.sync
            def _(sp):
                weights.feed(sp)

            @block.tensor
            def _(pe):
                mod_tensor(pe)

            @block.scalar
            def _(act):
                for t in range(TT):
                    mod_scalar(act, t * 4, 4 + t * (tiles // 2 - 4))
                    act.wait_ge(vec_ready.sem, vec_ready.at(t + 1))
                    act.activation(gate[:, t], gate[:, t], ACT.Exp).then_inc(act_ready.sem, 1)

            @block.vector
            def _(dve):
                v = Steps(dve, vec_step)
                for t in range(TT):
                    for h in range(PEER_HEADS):
                        for half in range(2):
                            n = h * 2 + half
                            top16(dve, v, best[:, n, :], pos[:, n, :], sc[:, t, half, h * P:(h + 1) * P])
                    v.wait()
                    v.link(dve.tensor_copy(bestf, pos))
                    b = best.rearrange("p (h two) k -> p h two k", two=2)
                    v.link(dve.tensor_tensor(
                        cand.rearrange("p h (i j) -> p h i j", j=TOPK),
                        b[:, :, 0, :].unsqueeze(3).to_broadcast([P, PEER_HEADS, TOPK, TOPK]),
                        b[:, :, 1, :].unsqueeze(2).to_broadcast([P, PEER_HEADS, TOPK, TOPK]),
                        ALU.add))
                    top = gate[:, t]
                    for h in range(PEER_HEADS):
                        top16(dve, v, top[:, h, :], pos[:, h, :], cand[:, h, :])
                    v.wait()
                    at = pos[:, 0:PEER_HEADS, :]
                    v.link(dve.tensor_scalar(p12[:, 0], at, 4, None, ALU.logical_shift_right))
                    v.link(dve.tensor_scalar(p12[:, 1], at, 15, None, ALU.bitwise_and))
                    v.link(dve.tensor_copy(sel, p12))
                    bf = bestf.rearrange("p (h two) k -> p h two k", two=2)
                    shape = [P, PEER_HEADS, TOPK, TOPK]
                    e4 = eq.rearrange("p h (k j) -> p h k j", j=TOPK)
                    steps16 = iota16[:].unsqueeze(1).unsqueeze(1).to_broadcast(shape)
                    for k in range(2):
                        v.link(dve.tensor_tensor(e4, sel[:, k].unsqueeze(3).to_broadcast(shape),
                                                 steps16, ALU.is_equal))
                        v.link(dve.tensor_tensor(e4, e4, bf[:, :, k, :].unsqueeze(2).to_broadcast(shape),
                                                 ALU.mult))
                        v.link(dve.tensor_reduce(sel[:, k], e4, AX_X, ALU.add))
                    v.link(dve.tensor_scalar(sel[:, 1], sel[:, 1], float(l * NKEYS * NKEYS), None,
                                             ALU.add))
                    v.link(dve.scalar_tensor_tensor(out=index[:, t], in0=sel[:, 0],
                                                    scalar=float(NKEYS), in1=sel[:, 1],
                                                    op0=ALU.mult, op1=ALU.add))
                    v.link(dve.tensor_copy(stat[:, 0:8], top[:, :, 0]))
                    m = stat[:, 0:8].unsqueeze(2).to_broadcast([P, PEER_HEADS, TOPK])
                    dve.tensor_tensor(top, top, m, ALU.subtract).then_inc(vec_ready.sem, 1)
                    dve.wait_ge(act_ready.sem, act_ready.at(t + 1))
                    v.link(dve.tensor_reduce(stat[:, 8:16], top, AX_X, ALU.add))
                    v.link(dve.reciprocal(stat[:, 16:24], stat[:, 8:16]))
                    r = stat[:, 16:24].unsqueeze(2).to_broadcast([P, PEER_HEADS, TOPK])
                    v.link(dve.tensor_tensor(top, top, r, ALU.mult))
                for u in range(2):
                    dve.wait_ge(unit_free[u].sem, unit_free[u].at(1 + tiles // 2))
                bias = vcol[:, 1 + l, V_BMOD:V_BMOD + 72].unsqueeze(2).to_broadcast([P, 72, 2])
                v.tick(dve.tensor_tensor(modcol[:, l], modcol[:, l], bias, ALU.add))
        vec_ready.base += TT
        act_ready.base += TT
        units_used(tiles)
        mod_rows.base += tiles
        mod_turned.base += tiles
        weights.end()

    TURNS = TT * PEER_HEADS // 2

    def gather(gp, table, index, cells, grow, zero, tick):
        p_ = Steps(gp, pool_step)
        p_.tick(gp.memset(tick, 0))
        p_.link(gp.memset(zero, 0))

        def turn(i):
            for half in range(2):
                p_.tick(gp.tensor_copy(cells[:, half, :], index[:, bass.ds(i * 32 + half * TOPK, TOPK)]))
                for k in range(TOPK):
                    slot = half * TOPK + k
                    if k % 2 == 0:
                        p_.wait()
                        gp.wait_ge(row_used.sem, row_used.at(i * 32 + slot + 2))
                        p_.tick(gp.tensor_tensor(tick, tick, zero, ALU.add))
                    gp.indirect_dma_start(
                        grow[:, slot % GR, :], None, table,
                        bass.IndirectOffsetOnAxis(ap=cells[:, half, k:k + 1], axis=0)) \
                      .then_inc(row_landed[slot % GR].sem, 16)
        p_.loop(TURNS, 2 + TOPK, turn)

    def fetching(block, dots, heads):
        if dots is not None:
            @block.gpsimd
            def _(gp):
                dots.fetch(gp, heads)

    def landed(eng, i, slot):
        eng.wait_ge(row_landed[slot % GR].sem,
                    i * (16 * 32 // GR) + row_landed[slot % GR].at(16 * (slot // GR + 1)))

    PER_TILE = TURNS // TT

    class ExpertDots:

        def __init__(self, l, hf_tok, index, grow, cell, acts):
            self.hf_tok, self.index, self.grow, self.cell, self.acts = hf_tok, index, grow, cell, acts
            self.table = a["peer_u"].rearrange("l n d -> (l n) d")
            self.done, self.fetched = 0, 0

        def fetch(self, gp, heads):
            upto = min(TT * SLOTS, (self.done + heads) * TOPK + GR)
            for slot in range(self.fetched, upto):
                gp.wait_ge(row_used.sem, row_used.at(slot + 1))
                gp.indirect_dma_start(
                    self.grow[:, slot % GR, :], None, self.table,
                    bass.IndirectOffsetOnAxis(ap=self.index[:, slot:slot + 1], axis=0)) \
                  .then_inc(row_landed[slot % GR].sem, 16)
            self.fetched = upto

        def dot(self, dve, head, first, last, turn=0):
            q = self.done + head
            t = q // PEER_HEADS
            if first == 0:
                dve.wait_ge(dots_kept.sem, turn + dots_kept.at(q + 1))
            for k in range(first, last):
                dve.wait_ge(row_landed[k % GR].sem,
                            turn * (16 * TOPK // GR)
                            + row_landed[k % GR].at(16 * (q * TOPK // GR + k // GR + 1)))
                dve.tensor_tensor_reduce(self.grow[:, k % GR, :], self.grow[:, k % GR, :],
                                         self.hf_tok[:, t, :], 1.0, 0.0, ALU.mult, ALU.add,
                                         self.cell[:, k:k + 1]).then_inc(row_used.sem, 1)
            if last == TOPK:
                dve.wait_ge(row_used.sem, turn * TOPK + row_used.at(GR + (q + 1) * TOPK))
                at = bass.ds(turn * TOPK + q * TOPK, TOPK)
                dve.tensor_copy(self.acts[:, at], self.cell[:, 0:TOPK]).then_inc(dots_kept.sem, 1)

        def end_phase(self, heads):
            self.done += heads

        def end(self):
            assert self.done == TT * PEER_HEADS
            row_used.base += TT * SLOTS
            dots_kept.base += TT * PEER_HEADS
            for s_ in range(GR):
                row_landed[s_].base += 16 * TT * SLOTS // GR

    def peer_up(l, index, cells, grow, tick, zero, acts, gate, w_cells, zeros_w):
        row_hi, row_lo = w_hi, w_lo
        diag_hi, diag_lo, w_all_hi = carve((4, P), (4, P), (TT * SLOTS,), of=parts)
        w_hi_cell, w_lo_cell = w_cells
        ahead = weights.first_tile(weights.group())
        with nc.Block() as block:
            @block.sync
            def _(sp):
                load_rows(sp, l, 1)

            @block.gpsimd
            def _(gp):
                gather(gp, a["peer_v"].rearrange("l n d -> (l n) d"), index, cells, grow, zero, tick)

            @block.tensor
            def _(pe):
                broadcast_row(pe, lambda c: adacol[:, l, 40 + c:41 + c], 3).then_inc(pe_done.sem, 1)
                pe.wait_ge(zeros_made.sem, zeros_made.at(1))
                for t in range(TT):
                    for half in range(2):
                        pe.matmul(ps[:, t, half * 512:(half + 1) * 512], zeros_w, x_tok[:, 0, 0:512],
                                  start=True, stop=False, skip_group_check=True)
                    with pe.Fori(t * PER_TILE, (t + 1) * PER_TILE) as q:
                        for slot in range(32):
                            b = slot % 4
                            pe.wait_ge(rows_split.sem, q * 32 + rows_split.at(2 + slot))
                            for half in range(2):
                                cols = slice(half * 512, (half + 1) * 512)
                                for dv, rv in passes((diag_hi[:, b, :], diag_lo[:, b, :]),
                                                     (row_hi[:, b, cols], row_lo[:, b, cols])):
                                    mm = pe.matmul(ps[:, t, cols], dv, rv, start=False, stop=False,
                                                   skip_group_check=True)
                            mm.then_inc(slot_summed.sem, 1)
                    for half in range(2):
                        mm = pe.matmul(ps[:, t, half * 512:(half + 1) * 512], zeros_w, x_tok[:, 0, 0:512],
                                       start=False, stop=True, skip_group_check=True)
                    mm.then_inc(pe_done.sem, 1)

            @block.scalar
            def _(act):
                s_ = Steps(act, act_step)
                act.activation(acts, acts, ACT.Gelu).then_inc(act_ready.sem, 1)
                act.wait_ge(pe_done.sem, pe_done.at(1))
                act.copy(rows[:, 0, :], ps[:, 3, :]).then_inc(act_ready.sem, 1)
                act.wait_ge(vec_ready.sem, vec_ready.at(1))
                act.activation(w_all_hi, acts, ACT.Copy).then_inc(act_ready.sem, 1)
                act.wait_ge(act_ready.sem, act_ready.at(3))

                def turn(i):
                    act.wait_ge(rows_rounded.sem, i * 32 + rows_rounded.at(1))
                    s_.link(act.copy(w_hi_cell, w_all_hi[:, bass.ds(i * 32, 32)].bitcast(F32)))
                    for slot in range(32):
                        b = slot % 4
                        landed(act, i, slot)
                        act.wait_ge(slot_summed.sem, i * 32 + slot_summed.at(1 + slot))
                        act.activation(diag_hi[:, b, :], ident[:], ACT.Copy,
                                       scale=w_hi_cell[:, slot:slot + 1])
                        act.activation(row_hi[:, b, :], grow[:, slot % GR, :], ACT.Copy) \
                           .then_inc(rows_rounded.sem, 1)
                s_.loop(TURNS, 1, turn)
                act.wait_ge(vec_ready.sem, vec_ready.at(2))
                act.activation(stat[:, 6:8], stat[:, 4:6], ACT.Sqrt).then_inc(act_ready.sem, 1)
                weights.split_hi(act, ahead)

            @block.vector
            def _(dve):
                v = Steps(dve, vec_step)
                dve.memset(zeros_w, 0.0).then_inc(zeros_made.sem, 1)
                dve.wait_ge(act_ready.sem, act_ready.at(1))
                dve.tensor_tensor(acts, acts, gate.rearrange("p t h k -> p (t h k)"), ALU.mult) \
                   .then_inc(vec_ready.sem, 1)
                dve.wait_ge(act_ready.sem, act_ready.at(3))
                v.link(dve.tensor_tensor(acts, acts, w_all_hi.bitcast(F32), ALU.subtract))

                def turn(i):
                    dve.wait_ge(rows_split.sem, i * 32 + rows_split.at(1))
                    v.link(dve.tensor_copy(w_lo_cell, acts[:, bass.ds(i * 32, 32)]))
                    for slot in range(32):
                        b = slot % 4
                        dve.wait_ge(rows_rounded.sem, i * 32 + rows_rounded.at(2 + slot))
                        dve.tensor_tensor(row_lo[:, b, :], grow[:, slot % GR, :],
                                          row_hi[:, b, :].bitcast(F32), ALU.subtract) \
                           .then_inc(row_used.sem, 1)
                        dve.tensor_scalar(diag_lo[:, b, :], ident[:], w_lo_cell[:, slot:slot + 1],
                                          None, ALU.mult).then_inc(rows_split.sem, 1)
                v.loop(TURNS, 1, turn)
                dve.wait_ge(act_ready.sem, act_ready.at(2))
                dve.wait_ge(loaded.sem, loaded.at(32))
                dve.wait_ge(pe_done.sem, pe_done.at(3))
                pieces = [(t, k * 512, ps[:, t, k * 512:(k + 1) * 512])
                          for k in range(2) for t in range(TT)]
                residual_norm(dve, 4, v, pieces, rows[:, 0, :], rows[:, 1, :], rows[:, 2, :])
                weights.split_lo(dve, ahead)
        row_used.base += TT * SLOTS
        for s in range(GR):
            row_landed[s].base += 16 * TT * SLOTS // GR
        zeros_made.base += 1
        for signal_ in (rows_rounded, rows_split, slot_summed):
            signal_.base += TT * SLOTS
        loaded.base += 32
        pe_done.base += 3
        act_ready.base += 4
        vec_ready.base += 2

    def gate_up(name, h, hff, silu, prod, dots=None, heads=0):
        weights.begin(f"gu_{name}")
        split = weights.group().split
        with nc.Block() as block:
            @block.sync
            def _(sp):
                weights.feed(sp)

            fetching(block, dots, heads)

            @block.tensor
            def _(pe):
                def tile(t, j, turn):
                    unit_wait(pe, j, turn)
                    project_features(pe, t, blocks_of(j), h, j, turn)
                in_pairs(11, pe, tile)

            @block.scalar
            def _(act):
                def tile(t, j, turn):
                    split_ahead(act=act, tile=(t, j, turn))
                    product_wait(act, t)
                    unit_wait(act, j, turn)
                    act.activation(silu[:, j, :], ps[:, j, 0:512], ACT.Silu) \
                       .then_inc(act_ready.sem, 1)
                with_last(11, act, tile)

            @block.vector
            def _(dve):
                v = Steps(dve, vec_step)
                start = v.n

                def tile(t, j, turn):
                    split_ahead(dve=dve, tile=(t, j, turn))
                    dve.wait_ge(act_ready.sem, act_ready.at(1) + t)
                    at = bass.ds(t * 512, 512)
                    if not split:
                        dve.tensor_tensor(hff[0][:, at], silu[:, j, :], ps[:, j, 512:1024],
                                          ALU.mult).then_inc(unit_free[j].sem, 1)
                    else:
                        dve.tensor_tensor(prod[:, j, :], silu[:, j, :], ps[:, j, 512:1024],
                                          ALU.mult).then_inc(unit_free[j].sem, 1)
                        dve.wait_ge(unit_free[j].sem, turn + unit_free[j].at(2))
                        v.n = start + 2 * t
                        v.link(dve.tensor_copy(hff[0][:, at], prod[:, j, :]))
                        v.tick(dve.tensor_tensor(hff[1][:, at], prod[:, j, :],
                                                 hff[0][:, at].bitcast(F32), ALU.subtract))
                    if dots is not None:
                        if isinstance(t, int):
                            dots.dot(dve, 5, 0, TOPK)
                        else:
                            dots.dot(dve, 0, 8 * j, 8 * j + 8, turn)
                with_last(11, dve, tile)
                vec_step.base = start + (2 * 11 if split else 0)
        if dots is not None:
            dots.end_phase(heads)
        act_ready.base += 11
        units_used(11)
        weights.end()

    def down(name, hff, dots=None, heads=0):
        weights.begin(f"down_{name}")
        width = 256
        parts = [h.rearrange("p (c t) -> p c t", t=SEQ) for h in hff]
        with nc.Block() as block:
            @block.sync
            def _(sp):
                weights.feed(sp)

            fetching(block, dots, heads)

            @block.tensor
            def _(pe):
                for t in range(8):
                    g, half = t // 2, t % 2
                    if half == 0:
                        unit_wait(pe, g % 2, g // 2)
                    project_tokens(pe, t, tiles_of(g % 2, width), parts, half * 11,
                                   opens=(half == 0), closes=(half == 1))

            @block.scalar
            def _(act):
                for t in range(8):
                    split_ahead(act=act, tile=(t, t % 2, t // 2))

            @block.vector
            def _(dve):
                for t in range(8):
                    split_ahead(dve=dve, tile=(t, t % 2, t // 2))
                    if t % 2:
                        g = t // 2
                        product_wait(dve, t)
                        src = ps[:, g % 2, :].rearrange("p (t n) -> p t n", t=TT)[:, :, 0:width]
                        dve.tensor_copy(y_tok[:, :, g * width:(g + 1) * width], src) \
                           .then_inc(unit_free[g % 2].sem, 1)
                    if t // 2 < heads:
                        dots.dot(dve, t // 2, 8 * (t % 2), 8 * (t % 2) + 8)
        if dots is not None:
            dots.end_phase(heads)
        units_used(4)
        weights.end()

    def project_out(name, h, dots=None, heads=0):
        weights.begin(name)
        with nc.Block() as block:
            @block.sync
            def _(sp):
                weights.feed(sp)

            fetching(block, dots, heads)

            @block.tensor
            def _(pe):
                for t in range(2):
                    unit_wait(pe, t, 0)
                    project_tokens(pe, t, tiles_of(t), h)

            @block.scalar
            def _(act):
                for t in range(2):
                    split_ahead(act=act, tile=(t, t, 0))

            @block.vector
            def _(dve):
                for t in range(2):
                    split_ahead(dve=dve, tile=(t, t, 0))
                    product_wait(dve, t)
                    dve.tensor_copy(y_tok[:, :, t * 512:(t + 1) * 512],
                                    ps[:, t, :].rearrange("p (t n) -> p t n", t=TT)) \
                       .then_inc(unit_free[t].sem, 1)
                    if heads:
                        dots.dot(dve, 0, 8 * t, 8 * t + 8)
        if dots is not None:
            dots.end_phase(heads)
        units_used(2)
        weights.end()

    def add_normed(tok, gate, gain, weight, dots=None, heads=0):
        junk = rows[:, 1:3, :]
        with nc.Block() as block:
            fetching(block, dots, heads)

            @block.vector
            def _(dve):
                v = Steps(dve, vec_step)
                dve.scalar_tensor_tensor(out=scol[:], in0=gate, scalar=weight, in1=gain,
                                         op0=ALU.mult, op1=ALU.mult).then_inc(cols_ready.sem, 1)
                for t in range(TT):
                    v.tick(dve.tensor_tensor_reduce(junk[:, t, :], y_tok[:, t, :], y_tok[:, t, :],
                                                    1.0, 0.0, ALU.mult, ALU.add, stat[:, t:t + 1]))
                v.wait()
                dve.tensor_scalar(stat[:, 0:2], stat[:, 0:2], 1.0 / D, RMS_EPS, ALU.mult, ALU.add) \
                   .then_inc(vec_ready.sem, 1)
                dve.wait_ge(act_ready.sem, act_ready.at(1))
                v.link(dve.reciprocal(stat[:, 4:6], stat[:, 2:4]))
                dve.wait_ge(pe_done.sem, pe_done.at(1))
                for t in range(TT):
                    v.link(dve.scalar_tensor_tensor(out=y_tok[:, t, :], in0=y_tok[:, t, :],
                                                    scalar=stat[:, 4 + t:5 + t], in1=ps[:, 3, :],
                                                    op0=ALU.mult, op1=ALU.mult))
                    v.link(dve.tensor_tensor(tok[:, t, :], tok[:, t, :], y_tok[:, t, :], ALU.add))
                for head in range(heads):
                    dots.dot(dve, head, 0, TOPK)

            @block.tensor
            def _(pe):
                pe.wait_ge(cols_ready.sem, cols_ready.at(1))
                broadcast_row(pe, lambda c: scol[:, c:c + 1], 3).then_inc(pe_done.sem, 1)

            @block.scalar
            def _(act):
                act.wait_ge(vec_ready.sem, vec_ready.at(1))
                act.activation(stat[:, 2:4], stat[:, 0:2], ACT.Sqrt).then_inc(act_ready.sem, 1)
        if dots is not None:
            dots.end_phase(heads)
        cols_ready.base += 1
        vec_ready.base += 1
        act_ready.base += 1
        pe_done.base += 1

    def mod_cols(l, k, s):
        return modcol[:, l, k * KC:(k + 1) * KC, s]

    def gain_cols(l, k):
        at = V_NG + (l * 6 + k) * KC
        return vcol[:, 3, at:at + KC]

    def norm_in(tok, s, l, k, gain, full=None):
        whole = full is not None
        if not whole:
            (full,) = carve((KC, SEQ))
        modulated_features(tok, mod_cols(l, k + 1, s),
                           lambda c: modcol[:, l, k * KC + c, s:s + 1], full, gain_cols(l, gain),
                           whole)

    def ffn(name, tok, s, l, k, gain):
        begin_stretch(f"ffn_{name}", 2048, 2 * D_FF * TT)
        hff = carve((D_FF * TT,), (D_FF * TT,), of=parts)
        silu, prod = carve((2, 512), (2, 512))
        norm_in(tok, s, l, k, gain)
        gate_up(name, hT, hff, silu, prod)
        down(name, hff)
        add_normed(tok, mod_cols(l, k + 2, s), gain_cols(l, gain + 1), 0.5)

    def context_ffn(name, l, k, gain, dots, heads):
        h, hff = carve((KC, SEQ), (D_FF * TT,), of=parts)
        silu = rows[:, 0, :].rearrange("p (u n) -> p u n", u=2)
        norm_in(z_tok, 1, l, k, gain, h)
        gate_up(name, (h,), (hff,), silu, None, dots, heads[0])
        down(name, (hff,), dots, heads[1])
        add_normed(z_tok, mod_cols(l, k + 2, 1), gain_cols(l, gain + 1), 0.5, dots, heads[2])

    def conv_projection(name, h, b_gate, u, up, dots=None, heads=0):
        weights.begin(f"conv_{name}")
        with nc.Block() as block:
            @block.sync
            def _(sp):
                weights.feed(sp)

            fetching(block, dots, heads)

            @block.tensor
            def _(pe):
                for t in range(6):
                    unit_wait(pe, t % 2, t // 2)
                    project_features(pe, t, blocks_of(t % 2), h)

            @block.scalar
            def _(act):
                for t in range(6):
                    split_ahead(act=act, tile=(t, t % 2, t // 2))
                    if t not in (2, 3):
                        continue
                    product_wait(act, t)
                    act.copy(u[:, 4 * (t - 2):4 * (t - 1), :],
                             ps[:, t % 2, :].rearrange("p (b t) -> p b t", t=SEQ)) \
                       .then_inc(unit_free[t % 2].sem, 1)

            @block.vector
            def _(dve):
                v = Steps(dve, vec_step)
                v.tick(dve.memset(up[:, :, 0:1], 0.0))
                v.tick(dve.memset(up[:, :, SEQ + 1:SEQ + 2], 0.0))
                for t in range(6):
                    split_ahead(dve=dve, tile=(t, t % 2, t // 2))
                    if t // 2 < heads:
                        dots.dot(dve, t // 2, 8 * (t % 2), 8 * (t % 2) + 8)
                    if t in (2, 3):
                        continue
                    product_wait(dve, t)
                    src = ps[:, t % 2, :].rearrange("p (b t) -> p b t", t=SEQ)
                    if t < 2:
                        dve.tensor_copy(b_gate[:, 4 * t:4 * t + 4, :], src).then_inc(unit_free[t % 2].sem, 1)
                    else:
                        at = slice(4 * (t - 4), 4 * (t - 3))
                        dve.tensor_tensor(up[:, at, 1:SEQ + 1], u[:, at, :], src, ALU.mult) \
                           .then_inc(unit_free[t % 2].sem, 1)
        if dots is not None:
            dots.end_phase(heads)
        units_used(6)
        weights.end()

    def conv_taps(b_gate, up, y, h=None):
        with nc.Block() as block:
            @block.vector
            def _(dve):
                v = Steps(dve, vec_step)

                def tap(k, c):
                    if k == 2:
                        return vcol[:, 1, 72 + c:73 + c]
                    at = V_CW + k * KC + c
                    return vcol[:, 3, at:at + 1]
                for c in range(KC):
                    v.tick(dve.tensor_scalar(y[:, c, :], up[:, c, 0:SEQ], tap(0, c), None, ALU.mult))
                for k in (1, 2):
                    v.wait()
                    for c in range(KC):
                        v.tick(dve.scalar_tensor_tensor(
                            out=y[:, c, :], in0=up[:, c, k:k + SEQ], scalar=tap(k, c), in1=y[:, c, :],
                            op0=ALU.mult, op1=ALU.add))
                v.wait()
                if h is not None:
                    v.tick(dve.tensor_tensor(h, y, b_gate, ALU.mult))
                    return
                dve.tensor_tensor(y, y, b_gate, ALU.mult).then_inc(vec_ready.sem, 1)
                dve.wait_ge(act_ready.sem, act_ready.at(1))
                v.tick(dve.tensor_tensor(hT_lo[:], y, hT_hi[:].bitcast(F32), ALU.subtract))

            if h is None:
                @block.scalar
                def _(act):
                    act.wait_ge(vec_ready.sem, vec_ready.at(1))
                    act.activation(hT_hi[:], y, ACT.Copy).then_inc(act_ready.sem, 1)
        if h is None:
            vec_ready.base += 1
            act_ready.base += 1

    def conv():
        begin_stretch("conv_x", 8208, 0)
        b_gate, u, up, y = carve((KC, SEQ), (KC, SEQ), (KC, SEQ + 2), (KC, SEQ))
        norm_in(x_tok, 0, 0, 3, 2)
        conv_projection("x", hT, b_gate, u, up)
        conv_taps(b_gate, up, y)
        project_out("convout_x", hT)
        add_normed(x_tok, mod_cols(0, 5, 0), gain_cols(0, 3), 1.0)

    def context_conv(dots):
        h, b_gate, up = carve((KC, SEQ), (KC, SEQ), (KC, SEQ + 2), of=parts)
        u = rows[:, 1:3, :].rearrange("p k (c t) -> p (k c) t", t=SEQ)
        norm_in(z_tok, 1, 0, 3, 2, h)
        conv_projection("z", (h,), b_gate, u, up, dots, 3)
        conv_taps(b_gate, up, u, h)
        project_out("convout_z", (h,), dots, 1)
        add_normed(z_tok, mod_cols(0, 5, 1), gain_cols(0, 3), 1.0, dots, 1)

    def rotate(dve, v, t, heads, out_, src, cos, sin, tmp):
        s5 = src.rearrange("p h (a two q) -> p h a two q", a=2, two=2)
        o5 = out_.rearrange("p h (a two q) -> p h a two q", a=2, two=2)
        t4 = tmp.rearrange("p (h a q) -> p h a q", a=2, q=16)
        shape = [P, heads, 2, 16]
        c4 = cos[:, t].unsqueeze(1).to_broadcast(shape)
        n4 = sin[:, t].unsqueeze(1).to_broadcast(shape)
        for half, op in ((0, ALU.subtract), (1, ALU.add)):
            mine, other = s5[:, :, :, half, :], s5[:, :, :, 1 - half, :]
            v.link(dve.tensor_tensor(t4, other, n4, ALU.mult))
            v.link(dve.tensor_tensor(o5[:, :, :, half, :], mine, c4, ALU.mult))
            v.link(dve.tensor_tensor(o5[:, :, :, half, :], o5[:, :, :, half, :], t4, op))

    def context_keys(h, kz, vz, kzT):
        weights.begin("kv_z")
        with nc.Block() as block:
            @block.sync
            def _(sp):
                weights.feed(sp)

            @block.tensor
            def _(pe):
                for t in range(2):
                    project_tokens(pe, t, tiles_of(2 * t, 256), (h,))
                pe.wait_ge(vec_ready.sem, vec_ready.at(1))
                for c in range(4):
                    for t in range(TT):
                        mm = pe.transpose(ps[:, 1, c * SEQ + t * P:c * SEQ + (t + 1) * P],
                                          kz[:, t, 2 * c:2 * c + 2, :], ident[:])
                mm.then_inc(pe_done.sem, 1)

            @block.scalar
            def _(act):
                for t in range(2):
                    split_ahead(act=act, tile=(t, t, 0))

            @block.vector
            def _(dve):
                v = Steps(dve, vec_step)
                for t in range(2):
                    split_ahead(dve=dve, tile=(t, t, 0))
                product_wait(dve, 1)
                k_src, v_src = [ps[:, u, :].rearrange("p (t n) -> p t n", t=TT)[:, :, 0:256]
                                for u in (0, 2)]
                copy_keys(dve, v, kz, 0, k_src)
                dve.tensor_copy(vz, v_src).then_inc(vec_ready.sem, 1)
                dve.wait_ge(pe_done.sem, pe_done.at(1))
                dve.tensor_copy(kzT.rearrange("p c t -> p (c t)"), ps[:, 1, :])
        vec_ready.base += 1
        pe_done.base += 1
        weights.end()

    def copy_keys(dve, v, dst, head0, src):
        for t in range(TT):
            k4 = src[:, t, 0:256].rearrange("p (h d) -> p h d", d=HD)
            v.tick(dve.tensor_copy(dst[:, t, head0:head0 + 4, :], k4))
            pairs = src[:, t, 0:256].rearrange("p (c two d) -> p c two d", two=2, d=HD)
            out4 = dst[:, t, head0 + 4:head0 + 8, :].rearrange("p (c two) d -> p c two d", two=2)
            for e in range(2):
                v.tick(dve.tensor_copy(out4[:, :, e, :], pairs[:, :, 1 - e, :]))
        v.wait()

    def queries_and_keys(qk, rot, vx, qkT, cos, sin, tmp):
        heads = NQ + 2 * NKV
        weights.begin("qkv")
        with nc.Block() as block:
            @block.sync
            def _(sp):
                sp.dma_start(cos, a["k_cos"]).then_inc(loaded.sem, 16)
                sp.dma_start(sin, a["k_sin"]).then_inc(loaded.sem, 16)
                weights.feed(sp)

            @block.tensor
            def _(pe):
                for t in range(3):
                    project_tokens(pe, t, tiles_of(t), hT)
                pe.wait_ge(vec_ready.sem, vec_ready.at(1))
                for u in range(3):
                    for c in range(4):
                        for t in range(TT):
                            h = 8 * u + 2 * c
                            mm = pe.transpose(ps[:, u, c * SEQ + t * P:c * SEQ + (t + 1) * P],
                                              rot[:, t, h:h + 2, :], ident[:])
                    mm.then_inc(pe_done.sem, 1)

            @block.scalar
            def _(act):
                for k in range(2):
                    split_ahead(act=act, tile=(k, k, 0))
                    product_wait(act, k)
                    for t in range(TT):
                        ins = act.activation(qk[:, t, 8 * k:8 * k + 8, :],
                                             ps[:, k, t * 512:(t + 1) * 512].rearrange(
                                                 "p (h d) -> p h d", d=HD),
                                             ACT.Copy, scale=HD ** -0.5)
                ins.then_inc(act_ready.sem, 1)
                split_ahead(act=act, tile=(2, 0, 1))
                for u in range(3):
                    act.wait_ge(pe_done.sem, pe_done.at(u + 1))
                    act.copy(qkT[:, 4 * u:4 * u + 4, :].rearrange("p c t -> p (c t)"), ps[:, u, :])

            @block.vector
            def _(dve):
                v = Steps(dve, vec_step)
                for t in range(3):
                    split_ahead(dve=dve, tile=(t, t % 2, t // 2))
                product_wait(dve, 2)
                src = ps[:, 2, :].rearrange("p (t n) -> p t n", t=TT)
                copy_keys(dve, v, qk, NQ, src)
                v.tick(dve.tensor_copy(vx, src[:, :, 256:512]))
                dve.wait_ge(act_ready.sem, act_ready.at(1))
                dve.wait_ge(loaded.sem, loaded.at(32))
                for t in range(TT):
                    rotate(dve, v, t, heads, rot[:, t], qk[:, t], cos, sin, tmp)
                dve.memset(stat[:, 0:1], 0.0).then_inc(vec_ready.sem, 1)
        loaded.base += 32
        vec_ready.base += 1
        act_ready.base += 1
        pe_done.base += 3
        weights.end()

    def window_attention(qkT, kzT, vx, vz, s, pT, band, sink):
        with nc.Block() as block:
            @block.sync
            def _(sp):
                sp.dma_start(band, a["k_band"]).then_inc(loaded.sem, 16)
                sp.dma_start(sink, a["attn_sink_2"].to_broadcast([P, NQ])).then_inc(loaded.sem, 16)

            @block.tensor
            def _(pe):
                def scores(h):
                    if h >= 2:
                        pe.wait_ge(vec_ready.sem, vec_ready.at(3 * (h - 2) + 1))
                    kv = h // (NQ // NKV)
                    same = h % 2 == kv % 2
                    at = slice(64 * (h % 2), 64 * (h % 2) + 64)
                    kx = qkT[at, 8 + kv // 2 + (0 if same else 2), :]
                    kz = kzT[at, kv // 2 + (0 if same else 2), :]
                    for t in range(TT):
                        q = qkT[at, h // 2, t * P:(t + 1) * P]
                        pe.matmul(ps[:, h % 2, t * 512:t * 512 + 256], q, kx, start=True, stop=True)
                        mm = pe.matmul(ps[:, h % 2, t * 512 + 256:(t + 1) * 512], q, kz,
                                       start=True, stop=True)
                    mm.then_inc(pe_done.sem, 1)

                scores(0)
                for h in range(NQ):
                    if h + 1 < NQ:
                        scores(h + 1)
                    pe.wait_ge(vec_ready.sem, vec_ready.at(3 * h + 3))
                    for c in range(4):
                        for t in range(TT):
                            mm = pe.transpose(ps[:, 2, c * SEQ + t * P:c * SEQ + (t + 1) * P],
                                              s[:, h % 2, t, c * P:(c + 1) * P], ident[:])
                    mm.then_inc(turned.sem, 1)
                    pe.wait_ge(act_ready.sem, act_ready.at(2 * h + 2))
                    if h == 8:
                        pe.wait_ge(cols_ready.sem, cols_ready.at(1))
                    kv = h // (NQ // NKV)
                    dst = ps[64 * (h % 2):64 * (h % 2) + 64, 3,
                             (h % 8 // 2) * SEQ:(h % 8 // 2 + 1) * SEQ]
                    for c in range(4):
                        values = (vx if c < 2 else vz)[:, c % 2, kv * HD:(kv + 1) * HD]
                        mm = pe.matmul(dst, values, pT[:, c, :], start=(c == 0), stop=(c == 3),
                                       skip_group_check=True)
                    mm.then_inc(summed.sem, 1)

            @block.scalar
            def _(act):
                def turn_out(h):
                    act.wait_ge(turned.sem, turned.at(h + 1))
                    if h >= 1:
                        act.wait_ge(summed.sem, summed.at(h))
                    act.copy(pT.rearrange("p c t -> p (c t)"), ps[:, 2, :]) \
                       .then_inc(act_ready.sem, 1)

                for h in range(NQ):
                    act.wait_ge(vec_ready.sem, vec_ready.at(3 * h + 2))
                    b = 8 * (h % 2)
                    for t in range(TT):
                        act.activation(s[:, h % 2, t, :], s[:, h % 2, t, :], ACT.Exp,
                                       bias=stat[:, b + t:b + t + 1],
                                       accum_out=stat[:, b + 2 + t:b + 3 + t])
                    act.activation(stat[:, b + 4:b + 6], stat[:, b:b + 2], ACT.Exp,
                                   bias=sink[:, h:h + 1]).then_inc(act_ready.sem, 1)
                    turn_out(h)

            @block.vector
            def _(dve):
                v = Steps(dve, vec_step)
                dve.wait_ge(loaded.sem, loaded.at(32))
                for h in range(NQ):
                    b = 8 * (h % 2)
                    dve.wait_ge(pe_done.sem, pe_done.at(h + 1))
                    if h >= 2:
                        dve.wait_ge(turned.sem, turned.at(h - 1))
                    dve.tensor_tensor(s[:, h % 2], ps[:, h % 2, :].rearrange("p (t n) -> p t n", t=TT),
                                      band, ALU.add).then_inc(vec_ready.sem, 1)
                    dve.wait_ge(vec_ready.sem, vec_ready.at(3 * h + 1))
                    v.link(dve.tensor_reduce(stat[:, b:b + 2], s[:, h % 2], AX_X, ALU.max))
                    dve.tensor_scalar(stat[:, b:b + 2], stat[:, b:b + 2], sink[:, h:h + 1], -1.0,
                                      ALU.max, ALU.mult).then_inc(vec_ready.sem, 1)
                    dve.wait_ge(act_ready.sem, act_ready.at(2 * h + 1))
                    v.link(dve.tensor_tensor(stat[:, b + 6:b + 8], stat[:, b + 2:b + 4],
                                             stat[:, b + 4:b + 6], ALU.add))
                    v.link(dve.reciprocal(stat[:, b + 6:b + 8], stat[:, b + 6:b + 8]))
                    dve.tensor_tensor(s[:, h % 2], s[:, h % 2],
                                      stat[:, b + 6:b + 8].unsqueeze(2).to_broadcast([P, TT, 512]),
                                      ALU.mult).then_inc(vec_ready.sem, 1)
                    if h % 8 == 7:
                        dve.wait_ge(summed.sem, summed.at(h + 1))
                        hi, lo = [o[:, h // 8 * 4:h // 8 * 4 + 4, :].rearrange("p c t -> p (c t)")
                                  for o in hT]
                        v.link(dve.tensor_copy(hi, ps[:, 3, :]))
                        dve.tensor_tensor(lo, ps[:, 3, :], hi.bitcast(F32), ALU.subtract) \
                           .then_inc(cols_ready.sem, 1)
        loaded.base += 32
        pe_done.base += NQ
        turned.base += NQ
        summed.base += NQ
        vec_ready.base += 3 * NQ
        act_ready.base += 2 * NQ
        cols_ready.base += 2

    for l in range(DEPTH):
        ada_modulation(l)

    for l in range(DEPTH):
        begin_stretch(f"layer{l}", 11264, 4096)
        (qa, sg, km, ia, ga, qb, kb, vb, work) = carve(
            (4, SEQ), (4, SEQ), (4, SEQ), (TT, 512), (TT, 512), (4, SEQ), (4, SEQ), (TT, 512),
            (3072,))
        oa_hi, oa_lo, ob_hi, ob_lo = carve((4, SEQ), (4, SEQ), (4, SEQ), (4, SEQ), of=parts)
        modulated_features(x_tok, adacol[:, l, 8:16], lambda c: adacol[:, l, c:c + 1],
                           arena[:, 0:2048].rearrange("p (c t) -> p c t", t=SEQ))
        input_projection(l, qa, sg, km, ia, ga, qb, kb, vb)
        oaT, obT = (oa_hi, oa_lo), (ob_hi, ob_lo)
        ke, scores, cross = work[:, 0:1024], work[:, 1024:2048], work[:, 2048:2560]
        o, sq = y_tok[:, 0, :].rearrange("p (t n) -> p t n", t=TT), y_tok[:, 1, :]
        hgrn(l, qa, sg, km, ia, ga, oaT,
             (rows[:, 0, :], rows[:, 1, :], rows[:, 2, :], ke, scores, cross, o, sq))
        sbt = [v.rearrange("p (n w) -> p n w", n=4) for v in (
            work[:, 0:1536], work[:, 1536:3072],
            rows[:].rearrange("p k n -> p (k n)")[:, 0:1536])]
        stick_breaking(qb, kb, vb, obT, sbt)
        _, gates = carve((4096,), (2 * KC, SEQ))
        gate_projection(l, gates)
        merge(l, oaT, obT, gates)
        output_projection(l)

        hf_tok, index, gate, small, rest = carve((TT, D), (TT, PEER_HEADS, TOPK),
                                                 (TT, PEER_HEADS, TOPK), (128,), (8576,))
        modulated_features(x_tok, adacol[:, l, 32:40], lambda c: adacol[:, l, 24 + c:25 + c],
                           rest[:, 0:2048].rearrange("p (c t) -> p c t", t=SEQ))
        index = index.bitcast(U32)
        pqT = rest[:, 0:2048].rearrange("p (h t) -> p h t", h=PEER_HEADS)
        keys = rest[:, 2048:3072].rearrange("p (h t) -> p h t", h=PEER_HEADS)
        keysT = rest[:, 3072:4096].rearrange("p (h t) -> p h t", h=PEER_HEADS)
        sc = rest[:, 4096:8192].rearrange("p (t half n) -> p t half n", t=TT, half=2)
        best, bestf, pos, p12, sel = [y_tok[:, 0, k * 256:(k + 1) * 256] for k in range(4)] \
            + [y_tok[:, 1, 0:256]]
        best, bestf, pos = [x.rearrange("p (n k) -> p n k", k=TOPK) for x in (best, bestf, pos)]
        p12, sel = [x.rearrange("p (z h k) -> p z h k", z=2, k=TOPK) for x in (p12, sel)]
        pos, p12 = pos.bitcast(U32), p12.bitcast(U32)
        cand = rest[:, 0:2048].rearrange("p (h n) -> p h n", h=PEER_HEADS)
        eq = rest[:, 2048:4096].rearrange("p (h n) -> p h n", h=PEER_HEADS)
        peer_queries(l, hf_tok, pqT, keys, keysT, sc)
        peer_select(l, sc, best, bestf, cand, pos, p12, eq, sel, index, gate)
        grow = rest[:, 0:GR * D].rearrange("p (r n) -> p r n", r=GR)
        acts, zeros_w = rest[:, GR * D:GR * D + 256], rest[:, GR * D + 256:GR * D + 384]
        cells = small[:, 0:32].rearrange("p (a k) -> p a k", a=2).bitcast(U32)
        w_cells = small[:, 32:64], small[:, 64:96]
        tick, zero = small[:, 96:97].bitcast(U32), small[:, 97:98].bitcast(U32)
        flat_index = index.rearrange("p t h k -> p (t h k)")

        begin_parts(f"context_{l}", 2048 + D_FF * TT, F32)
        dots = ExpertDots(l, hf_tok, flat_index, grow, w_cells[0], acts)
        if l == 0:
            context_ffn("z00", 0, 0, 0, dots, (6, 4, 1))
            context_conv(dots)
        else:
            context_ffn("z01", 0, 6, 4, dots, (6, 4, 0))
            context_ffn("z10", 1, 0, 0, dots, (6, 0, 0))
            h, kz = carve((KC, SEQ), (TT, 2 * NKV, HD), of=parts)
            norm_in(z_tok, 1, 1, 3, 2, h)
            context_keys(h, kz, context_v[:], context_kT[:])
        dots.end()
        begin_parts(f"experts_{l}", 8 * P + TT * SLOTS)
        peer_up(l, flat_index, cells, grow, tick, zero, acts, gate, w_cells, zeros_w)

    ffn("x00", x_tok, 0, 0, 0, 0)
    conv()
    ffn("x01", x_tok, 0, 0, 6, 4)
    ffn("x10", x_tok, 0, 1, 0, 0)
    begin_stretch("attention", 12288, 0)
    norm_in(x_tok, 0, 1, 3, 2)
    qk, rot, vx, qkT, cos, sin, tmp = carve((TT, 24, HD), (TT, 24, HD), (TT, 256), (12, SEQ),
                                            (TT, 2, 16), (TT, 2, 16), (24 * 32,))
    queries_and_keys(qk, rot, vx, qkT, cos, sin, tmp)
    scores, pT, band, sink = carve((2, TT, 512), (4, SEQ), (TT, 512), (NQ,))
    window_attention(qkT, context_kT[:], vx, context_v[:], scores, pT, band, sink)
    project_out("attn_o", hT)
    add_normed(x_tok, mod_cols(1, 5, 0), gain_cols(1, 3), 1.0)
    ffn("x11", x_tok, 0, 1, 6, 4)

    with nc.Block() as block:
        @block.sync
        def _(sp):
            sp.dma_start(out[0].rearrange("(t p) d -> p t d", p=P), x_tok[:]).then_inc(stored.sem, 16)
            sp.wait_ge(stored.sem, 16)


def constants():
    i = np.arange(P)
    s, t = i[:, None], i[None, :]
    levels = [s == t] + [(s // (2 * m) == t // (2 * m)) & (s % (2 * m) < m) & (t % (2 * m) >= m)
                         for m in LEVELS]
    tok = np.arange(SEQ)
    grid_w, quarter = 64, HD // 4
    freq = (np.float32(10000.0) ** (-np.arange(quarter, dtype=np.float32) / np.float32(quarter)))
    ang = np.stack([(tok // grid_w).astype(np.float32)[:, None] * freq,
                    (tok % grid_w).astype(np.float32)[:, None] * freq], axis=1)
    table = lambda f: np.ascontiguousarray(
        f(ang).astype(np.float32).reshape(TT, P, 2, quarter).transpose(1, 0, 2, 3))
    band = np.zeros((P, TT, 512), np.float32)
    q = tok.reshape(TT, P).T
    band[:, :, 0:SEQ] = np.where(np.abs(tok[None, None, :] - q[:, :, None]) <= 128, 0.0, NEG)
    f = np.float32
    return {
        "k_ident": (s == t).astype(f),
        "k_tri": (s >= t).astype(f),
        "k_before": (s < t).astype(f),
        "k_before_neg": np.where(s < t, 0.0, NEG).astype(f),
        "k_levels": np.ascontiguousarray(np.stack(levels, 1).astype(np.uint32)),
        "k_iota16": np.tile(np.arange(TOPK, dtype=f), (P, 1)),
        "k_cos": table(np.cos),
        "k_sin": table(np.sin),
        "k_band": band,
    }


_INS = ["x", "c", "w_ada", "b_ada", "w_in", "lb_logits", "hg_norm_g", "w_up_a", "w_up_b", "w_o",
        "w_pq", "sub_keys", "peer_u", "peer_v", "ln_g", "ln_b", "c_2", "ctx_2", "c_ctx_2",
        "w_mod_2", "b_mod_2", "norm_g_2", "ffn_w_gu_2", "ffn_w_down_2", "conv_w_in_2", "conv_w_2",
        "conv_w_out_2", "attn_w_qkv_2", "attn_w_o_2", "attn_sink_2"]


def kernel(**inputs):
    import concourse.bacc as bacc
    from concourse.bass_utils import run_bass_kernel_spmd

    nc = bacc.Bacc("TRN2", target_bir_lowering=False, num_devices=1)
    arrays, aps = {}, {}
    for name, value in [(n, inputs[n]) for n in _INS] + list(constants().items()):
        value = np.ascontiguousarray(value)
        arrays[f"in_{name}"] = value
        aps[name] = nc.dram_tensor(f"in_{name}", value.shape, mybir.dt.from_np(value.dtype),
                                   kind="ExternalInput").ap()
    out = nc.dram_tensor("out", (1, SEQ, D), F32, kind="ExternalOutput").ap()
    build(nc, aps, out)
    r = run_bass_kernel_spmd(nc, [arrays], core_ids=[0])
    return r.results[0]["out"]
```

```python
import math
from contextlib import ExitStack

import numpy as np

import concourse.bass as bass
from concourse import mybir

F32 = mybir.dt.float32
U32 = mybir.dt.uint32
F32R = mybir.dt.float32r
ALU = mybir.AluOpType
ACT = mybir.ActivationFunctionType
AX_X = mybir.AxisListType.X

P = 128
D = 1024
KC = D // P
SEQ = 256
TT = SEQ // P
DEPTH = 2
DN_ALPHA = (2.0 * DEPTH) ** 0.25
LN_EPS = 1e-5
RMS_EPS = 1e-6

HG_HEADS = 4
SB_HEADS = 8
SB_DH = 64
PEER_HEADS = 8
TOPK = 16
NKEYS = 128
HALF_KEY = 64
SLOTS = PEER_HEADS * TOPK

D_FF = 2816
FC = D_FF // P
HD = 64
NQ = 16
NKV = 4
NEG = -1e30

QUARTERS = 4
QUARTER = 1024
ADA_FIRST = 4
BESIDE_MIXERS = ((6, 6), (6, 4))
MOD_BESIDE = 2
LEVELS = (64, 32, 16, 8, 4, 2, 1)


class Signal:

    def __init__(self, sem):
        self.sem = sem
        self.base = 0

    def at(self, k):
        return self.base + k


class Steps:

    def __init__(self, eng, count):
        self.eng, self.count, self.n = eng, count, count.base

    def tick(self, ins):
        ins.then_inc(self.count.sem, 1)
        self.n += 1
        self.count.base = self.n

    def wait(self):
        self.eng.wait_ge(self.count.sem, self.n)

    def link(self, ins):
        self.tick(ins)
        self.wait()

    def loop(self, turns, per_turn, body):
        start = self.n
        with self.eng.Fori(0, turns) as i:
            self.n = start + i * per_turn
            body(i)
        self.n = self.count.base = start + turns * per_turn


def in_pairs(n, eng, body):
    if n >= 4:
        with eng.Fori(0, n // 2) as i:
            for j in range(2):
                body(i * 2 + j, j, i)
    else:
        for t in range(n // 2 * 2):
            body(t, t % 2, t // 2)
    if n % 2:
        body(n - 1, 0, n // 2)


def with_last(n, eng, body):
    in_pairs(n - 1, eng, body)
    body(n - 1, (n - 1) % 2, (n - 1) // 2)


class Group:

    def __init__(self, name, n, chunks, cols, source, split, first, index):
        self.name, self.n, self.chunks, self.cols = name, n, chunks, cols
        self.source, self.split, self.first, self.index = source, split, first, index

    def starts(self, k):
        return sum(self.chunks[:k])

    def place(self, j, turn):
        return (self.first + j) % 2, turn + (self.first + j) // 2


class WeightStream:

    def __init__(self, raw, hi, lo, landed, hi_made, lo_made, used, whole_used):
        self.raw, self.hi, self.lo = raw, hi, lo
        self.landed, self.hi_made, self.lo_made = landed, hi_made, lo_made
        self.used, self.whole_used = used, whole_used
        self.groups = []
        self.now = 0

    def add(self, name, n, chunks, cols, source, split=True):
        assert n >= 2
        first = sum(g.n for g in self.groups)
        index = sum(g.n for g in self.groups if g.split == split)
        self.groups.append(Group(name, n, chunks, cols, source, split, first, index))

    def begin(self, name):
        assert self.group().name == name, (name, self.group().name)

    def end(self):
        self.now += 1

    def group(self, after=0):
        at = self.now + after
        return self.groups[at] if 0 <= at < len(self.groups) else None

    def wait_product(self, eng, t):
        g = self.group()
        if g.split:
            eng.wait_ge(self.used.sem, t * QUARTERS + (g.index * QUARTERS + 2 * QUARTERS))
        else:
            eng.wait_ge(self.whole_used.sem, t * 2 + (g.index * 2 + 2))

    def wait_raw_free(self, sp, g, t, half):
        if g.split:
            sp.wait_ge(self.lo_made.sem, t * QUARTERS + (g.index * QUARTERS + 2 * half + 2))
        else:
            sp.wait_ge(self.whole_used.sem, t * 2 + (g.index * 2 + half + 1))

    def raw_part(self, g, parity, half, c0, c1):
        at = g.starts(2 * half)
        return self.raw[:, 2 * parity + half, (c0 - at) * g.cols:(c1 - at) * g.cols]

    def load(self, sp, at, t, parity):
        g = self.groups[at]
        for half in range(2):
            c0, c1 = g.starts(2 * half), g.starts(2 * half + 2)
            if not isinstance(t, int) or t >= 2:
                self.wait_raw_free(sp, g, t - 2, half)
            elif at > 0:
                before = self.groups[at - 1]
                self.wait_raw_free(sp, before, before.n + t - 2, half)
            dst = self.raw_part(g, parity, half, c0, c1).rearrange("p (c n) -> p c n", n=g.cols)
            parts = g.source(t, c0, c1)
            done = self.landed[2 * parity + half]
            if isinstance(parts, list):
                wide = g.cols // 2
                for two, part in enumerate(parts):
                    sp.dma_start(dst[:, :, two * wide:(two + 1) * wide], part).then_inc(done, 16)
            else:
                sp.dma_start(dst, parts).then_inc(done, 32)

    def feed(self, sp, f=0, n=None):
        g = self.group()
        n = g.n if n is None else n
        left = n - f - 2
        done = f + 2
        if left >= 8:
            with sp.Fori(done // 2, done // 2 + left // 2) as i:
                for j in range(2):
                    self.load(sp, self.now, i * 2 + j, (g.first + j) % 2)
            done += left // 2 * 2
        for t in range(done, min(n + 2, g.n)):
            self.load(sp, self.now, t, (g.first + t) % 2)
        if n == g.n:
            self.ahead_loads(sp, self.now + 1)

    def ahead_loads(self, sp, at):
        if at < len(self.groups):
            for t in range(2):
                self.load(sp, at, t, (self.groups[at].first + t) % 2)

    def next_tile(self, t, j, turn):
        g = self.group()
        if isinstance(t, int) and t == g.n - 1:
            return self.first_tile(self.group(1))
        return (g, t + 1) + g.place(j + 1, turn)

    def first_tile(self, g):
        return (g, 0) + g.place(0, 0) if g is not None and g.split else None

    def split_hi(self, act, tile):
        if tile is None:
            return
        g, t, parity, turn = tile
        for k in range(QUARTERS):
            if k % 2 == 0:
                act.wait_ge(self.landed[2 * parity + k // 2], turn * 32 + 32)
            act.wait_ge(self.used.sem, t * QUARTERS + (g.index * QUARTERS + k + 1))
            act.activation(self.hi[:, k, 0:g.chunks[k] * g.cols],
                           self.raw_part(g, parity, k // 2, g.starts(k), g.starts(k + 1)),
                           ACT.Copy).then_inc(self.hi_made.sem, 1)

    def split_lo(self, dve, tile):
        if tile is None:
            return
        g, t, parity, _ = tile
        for k in range(QUARTERS):
            n = g.chunks[k] * g.cols
            dve.wait_ge(self.hi_made.sem, t * QUARTERS + (g.index * QUARTERS + k + 1))
            dve.tensor_tensor(self.lo[:, k, 0:n],
                              self.raw_part(g, parity, k // 2, g.starts(k), g.starts(k + 1)),
                              self.hi[:, k, 0:n].bitcast(F32), ALU.subtract) \
               .then_inc(self.lo_made.sem, 1)

    def sections(self, pe, t, j, turn):
        g = self.group()
        parity, at = g.place(j, turn)
        if g.split:
            for k in range(QUARTERS):
                pe.wait_ge(self.lo_made.sem, t * QUARTERS + (g.index * QUARTERS + k + 1))
                yield g.starts(k), g.chunks[k], [
                    slots[:, k, 0:g.chunks[k] * g.cols].rearrange("p (c n) -> p c n", n=g.cols)
                    for slots in (self.hi, self.lo)]
        else:
            for half in range(2):
                pe.wait_ge(self.landed[2 * parity + half], at * 32 + 32)
                c0, c1 = g.starts(2 * half), g.starts(2 * half + 2)
                yield c0, c1 - c0, [self.raw_part(g, parity, half, c0, c1)
                                    .rearrange("p (c n) -> p c n", n=g.cols)]

    def section_done(self, mm):
        mm.then_inc(self.used.sem if self.group().split else self.whole_used.sem, 1)


def columns(w, cols):
    v = w.rearrange("(c p) n -> p c n", p=P)
    if isinstance(cols, range):
        return lambda t, c0, c1: v[:, c0:c1, bass.ds(t * cols.step + cols.start, 512)]
    return lambda t, c0, c1: v[:, c0:c1, cols[t]:cols[t] + 512]


EVEN = (2, 2, 2, 2)
DOWN = (3, 3, 3, 2)


def build(nc, a, out):
    ctx = ExitStack()
    with ctx:
        _build(nc, ctx, a, out)


def _build(nc, ctx, a, out):
    def sb(name, shape, dt=F32):
        return ctx.enter_context(nc.sbuf_tensor(name, shape, dt))

    def signal(name):
        return Signal(ctx.enter_context(nc.semaphore(name)))

    raw = sb("raw", [P, 4, 2 * QUARTER])
    w_hi = sb("w_hi", [P, QUARTERS, QUARTER], F32R)
    w_lo = sb("w_lo", [P, QUARTERS, QUARTER], F32R)
    x_tok = sb("x_tok", [P, TT, D])
    z_tok = sb("z_tok", [P, TT, D])
    y_tok = sb("y_tok", [P, TT, D])
    hT_hi = sb("hT_hi", [P, KC, SEQ], F32R)
    hT_lo = sb("hT_lo", [P, KC, SEQ], F32R)
    hT = (hT_hi, hT_lo)
    ident = sb("ident", [P, P])
    tri = sb("tri", [P, P])
    before = sb("before", [P, P])
    before_neg = sb("before_neg", [P, P])
    ones = sb("ones", [P, P])
    level_mask = sb("level_mask", [P, len(LEVELS) + 1, P], U32)
    iota16 = sb("iota16", [P, TOPK])
    vcol = sb("vcol", [P, 4, P])
    condT = sb("condT", [P, KC, 4])
    cond_parts = sb("cond_parts", [P, KC, 2], F32R)
    adacol = sb("adacol", [P, DEPTH, 48])
    modcol = sb("modcol", [P, DEPTH, 72, 2])
    scol = sb("scol", [P, KC])
    bcol = sb("bcol", [P, KC])
    lbcol = sb("lbcol", [P, DEPTH, 2, HG_HEADS])
    stat = sb("stat", [P, 64])
    eps = sb("eps", [P, 1])
    rows = sb("rows", [P, 3, D])
    context_kT = sb("context_kT", [P, 4, SEQ])
    context_v = sb("context_v", [P, TT, NKV * HD])
    ps = ctx.enter_context(nc.psum_tensor("ps", [P, 4, 1024], F32))

    arena, parts, side = None, None, None
    outer, inner = ExitStack(), ExitStack()
    ctx.enter_context(outer)
    ctx.enter_context(inner)

    def begin_parts(name, size, dt=F32R, side_size=0):
        nonlocal parts, side
        inner.close()
        side = None
        if side_size:
            side = inner.enter_context(nc.sbuf_tensor(f"side_{name}", [P, side_size], F32))
        parts = None
        if size:
            parts = inner.enter_context(nc.sbuf_tensor(f"parts_{name}", [P, size], dt))

    def begin_stretch(name, arena_size, parts_size, side_size=0):
        nonlocal arena
        inner.close()
        outer.close()
        arena = outer.enter_context(nc.sbuf_tensor(f"arena_{name}", [P, arena_size], F32))
        begin_parts(name, parts_size, F32R, side_size)

    def carve(*shapes, of=None):
        whole = arena if of is None else of
        at, out_ = 0, []
        for shape in shapes:
            n = math.prod(shape)
            v = whole[:, at:at + n]
            if len(shape) > 1:
                names = [f"d{i}" for i in range(len(shape))]
                v = v.rearrange(f"p ({' '.join(names)}) -> p {' '.join(names)}",
                                **{m: s for m, s in zip(names[1:], shape[1:])})
            out_.append(v)
            at += n
        assert at <= whole.shape[1], (at, whole.shape)
        return out_

    used = signal("quarters_used")
    whole_used = signal("whole_halves_used")
    hi_made = signal("quarters_rounded")
    lo_made = signal("quarters_split")
    unit_free = [signal(f"unit_free_{u}") for u in range(2)]
    vec_step = signal("vec_step")
    act_step = signal("act_step")
    pool_step = signal("pool_step")
    loaded = signal("loaded")
    tokens_loaded = signal("tokens_loaded")
    stored = signal("stored")
    pe_done = signal("pe_done")
    vec_ready = signal("vec_ready")
    act_ready = signal("act_ready")
    cols_ready = signal("cols_ready")
    halves_landed = [ctx.enter_context(nc.semaphore(f"half_landed_{k}")) for k in range(4)]
    GR = 8
    row_landed = [signal(f"rows_landed_{s}") for s in range(GR)]
    row_used = signal("row_used")
    turned = signal("turned")
    masked = signal("masked")
    expd = signal("exponentials_made")
    normalised = signal("normalised")
    summed = signal("summed")
    dots_kept = signal("dots_kept")
    mod_rows = signal("mod_rows")
    mod_turned = signal("mod_turned")
    mod_copied = signal("mod_copied")

    weights = WeightStream(raw, w_hi, w_lo, halves_landed, hi_made, lo_made, used, whole_used)

    def w(name, l):
        return a[name][l]

    CHUNK_KV = 2 * 512
    def modulation_tiles(*ranges):
        each = [(w_.rearrange("(c p) n -> p c n", p=P), t) for w_, t0, t1 in ranges
                for t in range(t0, t1)]
        return len(each), lambda t, c0, c1: each[t][0][:, c0:c1, each[t][1] * 512:(each[t][1] + 1) * 512]

    n, source = modulation_tiles((w("w_ada", 0), 0, ADA_FIRST))
    weights.add("ada0", n, EVEN, 512, source)

    def add_block_1(l):
        weights.add(f"in{l}", 7, EVEN, 512, columns(
            w("w_in", l), [0, 512, 2048, 2560, 1024, 1536, 3072]))
        n, source = modulation_tiles(
            (w("w_ada", l), ADA_FIRST, 12),
            (w("w_ada", 1), 0, ADA_FIRST) if l == 0 else (w("w_mod_2", 1), 0, MOD_BESIDE))
        assert n == sum(BESIDE_MIXERS[l])
        weights.add(f"beside{l}", n, EVEN, 512, source, False)
        weights.add(f"gates{l}", 4, EVEN, 512, columns(w("w_in", l), range(3584, 5632, 512)))
        up = [w("w_up_a", l), w("w_up_b", l)]
        weights.add(f"up{l}", 2, (1, 1, 1, 1), 1024, lambda t, c0, c1, up=up:
                    up[t].rearrange("(c p) n -> p c n", p=P)[:, c0:c1, :])
        weights.add(f"o{l}", 2, EVEN, 512, columns(w("w_o", l), range(0, 1024, 512)))
        weights.add(f"pq{l}", 2, EVEN, 512, columns(w("w_pq", l), range(0, 1024, 512)))

    def add_ffn(name, l, k, split=True):
        gu = a["ffn_w_gu_2"][l, k].rearrange("(c p) (two f) -> p c two f", p=P, two=2)
        down_ = a["ffn_w_down_2"][l, k].rearrange("(h c p) n -> p h c n", p=P, h=2)
        weights.add(f"gu_{name}", 11, EVEN, 512, lambda t, c0, c1:
                    [gu[:, c0:c1, two, bass.ds(t * 256, 256)] for two in range(2)], split)
        weights.add(f"down_{name}", 8, DOWN, 256, lambda t, c0, c1:
                    down_[:, t % 2, c0:c1, t // 2 * 256:t // 2 * 256 + 256], split)

    def add_conv(name, split=True):
        weights.add(f"conv_{name}", 6, EVEN, 512,
                    columns(a["conv_w_in_2"][0], range(0, 3072, 512)), split)
        weights.add(f"convout_{name}", 2, EVEN, 512,
                    columns(a["conv_w_out_2"][0], range(0, 1024, 512)), split)

    for l in range(DEPTH):
        add_block_1(l)
        at = MOD_BESIDE * l
        weights.add(f"mod{l}", 18 - at, EVEN, 512,
                    columns(w("w_mod_2", l), range(at * 512, 9216, 512)), False)
        if l == 0:
            add_ffn("z00", 0, 0, False)
            add_conv("z", False)
            add_ffn("z01", 0, 1, False)
        else:
            add_ffn("z10", 1, 0, False)
            kv = a["attn_w_qkv_2"][0].rearrange("(c p) n -> p c n", p=P)
            weights.add("kv_z", 2, EVEN, 256, lambda t, c0, c1:
                        kv[:, c0:c1, CHUNK_KV + t * 256:CHUNK_KV + (t + 1) * 256], False)
    add_ffn("x00", 0, 0)
    add_conv("x")
    add_ffn("x01", 0, 1)
    add_ffn("x10", 1, 0)
    weights.add("qkv", 3, EVEN, 512, columns(a["attn_w_qkv_2"][0], range(0, 1536, 512)))
    weights.add("attn_o", 2, EVEN, 512, columns(a["attn_w_o_2"][0], range(0, 1024, 512)))
    add_ffn("x11", 1, 1)

    begin_stretch("setup", 1024, 0)
    vrows = carve((4, P))[0]
    V_C, V_C2, V_CCTX, V_BADA = 0, 8, 16, 24
    V_BMOD = 0
    V_LB, V_HGG = 0, 8
    V_NG, V_CW = 16, 112
    with nc.Block() as block:
        @block.sync
        def _(sp):
            def small(dst, src):
                sp.dma_start(dst, src).then_inc(loaded.sem, 16)
                loaded.base += 16
            small(vrows[V_C:V_C + 8, 0, :], a["c"].rearrange("a (r p) -> (a r) p", p=P))
            small(vrows[V_C2:V_C2 + 8, 0, :], a["c_2"].rearrange("a (r p) -> (a r) p", p=P))
            small(vrows[V_CCTX:V_CCTX + 8, 0, :], a["c_ctx_2"].rearrange("(r p) -> r p", p=P))
            small(vrows[V_BADA:V_BADA + 96, 0, :], a["b_ada"].rearrange("l (r p) -> (l r) p", p=P))
            for l in range(DEPTH):
                small(vrows[0:72, 1 + l, :], a["b_mod_2"][l].rearrange("(r p) -> r p", p=P))
            small(vrows[V_LB:V_LB + 8, 3, :], a["lb_logits"].rearrange("l (r p) -> (l r) p", p=P))
            small(vrows[V_HGG:V_HGG + 8, 3, :], a["hg_norm_g"].rearrange("l (r p) -> (l r) p", p=P))
            small(vrows[V_NG:V_NG + 96, 3, :], a["norm_g_2"].rearrange("l k (r p) -> (l k r) p", p=P))
            cw = a["conv_w_2"][0].rearrange("k (r p) -> (k r) p", p=P)
            small(vrows[V_CW:V_CW + 16, 3, :], cw[0:16, :])
            small(vrows[72:80, 1, :], cw[16:24, :])
            small(ident[:], a["k_ident"])
            small(tri[:], a["k_tri"])
            small(before[:], a["k_before"])
            small(before_neg[:], a["k_before_neg"])
            small(level_mask[:], a["k_levels"])
            small(iota16[:], a["k_iota16"])
            weights.ahead_loads(sp, 0)
            for tok, src in ((x_tok, a["x"]), (z_tok, a["ctx_2"])):
                sp.dma_start(tok[:], src[0].rearrange("(t p) d -> p t d", p=P)) \
                  .then_inc(tokens_loaded.sem, 16)

        group_rows = (120, 80, 72, 128)

        @block.tensor
        def _(pe):
            pe.wait_ge(loaded.sem, loaded.base)
            for g, n in enumerate(group_rows):
                pe.transpose(ps[:, 0, g * P:g * P + n], vrows[0:n, g, :], ident[0:n, 0:n]) \
                    .then_inc(pe_done.sem, 1)

        @block.scalar
        def _(act):
            act.wait_ge(vec_ready.sem, vec_ready.at(1))
            for k, at in enumerate((V_C, V_C2, V_CCTX)):
                ins = act.activation(condT[:, :, k], vcol[:, 0, at:at + 8], ACT.Silu)
            ins.then_inc(act_ready.sem, 1)
            act.wait_ge(act_ready.sem, act_ready.at(1))
            act.activation(cond_parts[:, :, 0], condT[:, :, 0], ACT.Copy).then_inc(act_ready.sem, 1)
            weights.split_hi(act, weights.first_tile(weights.group()))

        @block.vector
        def _(dve):
            v = Steps(dve, vec_step)
            v.tick(dve.memset(ones[:], 1.0))
            dve.wait_ge(pe_done.sem, pe_done.at(4))
            for g, n in enumerate(group_rows):
                ins = dve.tensor_copy(vcol[:, g, 0:n], ps[:, 0, g * P:g * P + n])
                if g < 3:
                    v.tick(ins)
            ins.then_inc(vec_ready.sem, 1)
            dve.wait_ge(vec_ready.sem, vec_ready.at(1))
            v.tick(dve.memset(lbcol[:, 0, 0, :], 0.0))
            v.link(dve.tensor_tensor(lbcol[:, 1, 0, :], vcol[:, 3, V_LB:V_LB + 4],
                                     vcol[:, 3, V_LB + 4:V_LB + 8], ALU.subtract))
            for u in range(2):
                dve.memset(stat[:, u:u + 1], 0.0).then_inc(unit_free[u].sem, 1)
            dve.memset(stat[:, 2:3], 0.0).then_inc(row_used.sem, GR)
            dve.memset(stat[:, 3:4], 0.0).then_inc(used.sem, QUARTERS)
            v.tick(dve.memset(eps[:], RMS_EPS))
            dve.memset(stat[:, 5:6], 0.0).then_inc(dots_kept.sem, 1)
            dve.wait_ge(act_ready.sem, act_ready.at(2))
            v.tick(dve.tensor_tensor(cond_parts[:, :, 1], condT[:, :, 0],
                                     cond_parts[:, :, 0].bitcast(F32), ALU.subtract))
            weights.split_lo(dve, weights.first_tile(weights.group()))

    pe_done.base += 4
    vec_ready.base += 1
    act_ready.base += 2

    with nc.Block() as block:
        @block.scalar
        def _(act):
            s = Steps(act, act_step)
            s.link(act.activation(lbcol[:, 1, 0, :], lbcol[:, 1, 0, :], ACT.Sigmoid, scale=-1.0))

        @block.vector
        def _(dve):
            dve.wait_ge(act_step.sem, act_step.base)
            for l in range(DEPTH):
                dve.tensor_scalar(lbcol[:, l, 1, :], lbcol[:, l, 0, :], -1.0, 1.0,
                                  ALU.mult, ALU.add)

    def unit_wait(eng, j, turn):
        eng.wait_ge(unit_free[j].sem, turn + unit_free[j].at(1))

    def units_used(n):
        for u in range(2):
            unit_free[u].base += (n + 1 - u) // 2

    def passes(w_parts, x_parts):
        (wh, wl), (xh, xl) = w_parts, x_parts
        return ((wh, xh), (wh, xl), (wl, xh))

    def product(pe, out_, x_slices, w_slices, weights_stay, start, stop):
        combos = passes(w_slices, x_slices) if len(w_slices) == 2 else [w_slices + x_slices]
        for n, (wv, xv) in enumerate(combos):
            stay, move = (wv, xv) if weights_stay else (xv, wv)
            mm = pe.matmul(out_, stay, move, start=start and n == 0,
                           stop=stop and n == len(combos) - 1, skip_group_check=True)
        return mm

    def project_features(pe, t, bank, x_parts, j=None, turn=None):
        g = weights.group()
        last = sum(g.chunks) - 1
        if j is None:
            j, turn = t % 2, t // 2
        for start, n, parts in weights.sections(pe, t, j, turn):
            for b in range(g.cols // P):
                for c in range(n):
                    row = start + c
                    mm = product(pe, bank(b), [x[:, row, :] for x in x_parts],
                                 [w_[:, c, b * P:(b + 1) * P] for w_ in parts], True,
                                 row == 0 and b % 2 == 0, row == last)
            weights.section_done(mm)

    def project_tokens(pe, t, place, x_parts, chunk0=0, opens=True, closes=True):
        g = weights.group()
        last = sum(g.chunks) - 1
        for start, n, parts in weights.sections(pe, t, t % 2, t // 2):
            for m in range(TT):
                for c in range(n):
                    row = start + c
                    mm = product(pe, place(m),
                                 [x[:, chunk0 + row, m * P:(m + 1) * P] for x in x_parts],
                                 [w_[:, c, :] for w_ in parts], False,
                                 opens and row == 0, closes and row == last)
            weights.section_done(mm)

    def blocks_of(unit):
        return lambda b: ps[:, unit, b * SEQ:(b + 1) * SEQ]

    def tiles_of(unit, width=512):
        return lambda m: ps[:, unit, m * 512:m * 512 + width]

    def split_ahead(act=None, dve=None, tile=None):
        if not weights.group().split:
            return
        if act is not None:
            weights.split_hi(act, weights.next_tile(*tile))
        if dve is not None:
            weights.split_lo(dve, weights.next_tile(*tile))

    def product_wait(eng, t):
        weights.wait_product(eng, t)

    def ada_modulation(l):
        n = ADA_FIRST
        dst, bias = adacol[:, l, :], vcol[:, 0, V_BADA + 48 * l:V_BADA + 48 * (l + 1)]
        row = arena[0:2, 0:1024].rearrange("k (u n) -> k u n", u=2)
        weights.begin(f"ada{l}")
        with nc.Block() as block:
            @block.sync
            def _(sp):
                weights.feed(sp)

            @block.tensor
            def _(pe):
                def turn_row(t, j):
                    pe.wait_ge(mod_rows.sem, t + mod_rows.at(1))
                    for b in range(4):
                        mm = pe.matmul(ps[:, j, 512 + b:513 + b], row[:, j, b * P:(b + 1) * P],
                                       ones[0:2, 0:1], start=True, stop=True)
                    mm.then_inc(mod_turned.sem, 1)

                def tile(t, j, turn):
                    unit_wait(pe, j, turn)
                    for start, chunks, parts in weights.sections(pe, t, j, turn):
                        for c in range(chunks):
                            for k, part in enumerate(parts):
                                mm = pe.matmul(ps[0:2, j, 0:512], cond_parts[:, start + c, :],
                                               part[:, c, :], start=start + c == 0 and k == 0,
                                               stop=start + c == KC - 1 and k == 1)
                        weights.section_done(mm)
                    if j == 1:
                        turn_row(t - 1, 0)
                        turn_row(t, 1)
                in_pairs(n, pe, tile)
                pe.wait_ge(tokens_loaded.sem, 32)

            @block.scalar
            def _(act):
                def tile(t, j, turn):
                    split_ahead(act=act, tile=(t, j, turn))
                    product_wait(act, t)
                    act.copy(row[:, j, :], ps[0:2, j, 0:512]).then_inc(mod_rows.sem, 1)
                with_last(n, act, tile)

            @block.vector
            def _(dve):
                def tile(t, j, turn):
                    split_ahead(dve=dve, tile=(t, j, turn))
                    if j == 1:
                        for back in (1, 0):
                            u = t - back
                            dve.wait_ge(mod_turned.sem, u + mod_turned.at(1))
                            at = bass.ds(u * 4, 4)
                            dve.tensor_tensor(dst[:, at], ps[:, 1 - back, 512:516], bias[:, at],
                                              ALU.add).then_inc(unit_free[1 - back].sem, 1)
                with_last(n, dve, tile)
        units_used(n)
        mod_rows.base += n
        mod_turned.base += n
        weights.end()

    def modulated_features(src, scale, shift, full, gain=None):
        normed = y_tok
        with nc.Block() as block:
            @block.tensor
            def _(pe):
                tokens = src if gain is None else normed
                for t in range(TT):
                    if gain is not None:
                        pe.wait_ge(vec_ready.sem, vec_ready.at(2 + t))
                    for c in range(KC):
                        mm = pe.transpose(ps[:, t, c * P:(c + 1) * P],
                                          tokens[:, t, c * P:(c + 1) * P], ident[:])
                    mm.then_inc(pe_done.sem, 1)

            @block.scalar
            def _(act):
                s_ = Steps(act, act_step)
                if gain is not None:
                    act.wait_ge(vec_ready.sem, vec_ready.at(1))
                    act.activation(stat[:, 2:4], stat[:, 0:2], ACT.Sqrt).then_inc(turned.sem, 1)
                act.wait_ge(cols_ready.sem, cols_ready.at(1))
                act.wait_ge(pe_done.sem, pe_done.at(1))
                for c in range(KC):
                    s_.tick(act.activation(full[:, c, 0:P], ps[:, 0, c * P:(c + 1) * P], ACT.Identity,
                                           bias=shift(c), scale=scol[:, c:c + 1]))
                s_.wait()
                act.activation(hT_hi[:, :, 0:P], full[:, :, 0:P], ACT.Copy).then_inc(act_ready.sem, 1)

            @block.vector
            def _(dve):
                v = Steps(dve, vec_step)
                if gain is None:
                    dve.tensor_scalar(scol[:], scale, 1.0, None, ALU.add).then_inc(cols_ready.sem, 1)
                else:
                    dve.scalar_tensor_tensor(out=scol[:], in0=scale, scalar=1.0, in1=gain,
                                             op0=ALU.add, op1=ALU.mult).then_inc(cols_ready.sem, 1)
                    for t in range(TT):
                        v.tick(dve.tensor_tensor_reduce(normed[:, t, :], src[:, t, :], src[:, t, :],
                                                        1.0, 0.0, ALU.mult, ALU.add,
                                                        stat[:, t:t + 1]))
                    v.wait()
                    dve.tensor_scalar(stat[:, 0:2], stat[:, 0:2], 1.0 / D, RMS_EPS,
                                      ALU.mult, ALU.add).then_inc(vec_ready.sem, 1)
                    dve.wait_ge(turned.sem, turned.at(1))
                    v.link(dve.reciprocal(stat[:, 4:6], stat[:, 2:4]))
                    for t in range(TT):
                        dve.tensor_scalar(normed[:, t, :], src[:, t, :], stat[:, 4 + t:5 + t], None,
                                          ALU.mult).then_inc(vec_ready.sem, 1)
                dve.wait_ge(cols_ready.sem, cols_ready.at(1))
                dve.wait_ge(pe_done.sem, pe_done.at(2))
                for c in range(KC):
                    v.tick(dve.tensor_scalar(full[:, c, P:SEQ], ps[:, 1, c * P:(c + 1) * P],
                                             scol[:, c:c + 1], shift(c), ALU.mult, ALU.add))
                v.wait()
                v.link(dve.tensor_copy(hT_hi[:, :, P:SEQ], full[:, :, P:SEQ]))
                dve.wait_ge(act_ready.sem, act_ready.at(1))
                v.tick(dve.tensor_tensor(hT_lo[:], full, hT_hi[:].bitcast(F32), ALU.subtract))
        cols_ready.base += 1
        pe_done.base += 2
        act_ready.base += 1
        if gain is not None:
            vec_ready.base += 3
            turned.base += 1

    def context_norm(scale, shift, gain, full, experts, heads):
        normed = y_tok
        with nc.Block() as block:
            fetching(block, experts, heads)

            @block.tensor
            def _(pe):
                for t in range(TT):
                    pe.wait_ge(act_ready.sem, act_ready.at(2 + t))
                    for c in range(KC):
                        mm = pe.transpose(ps[:, t, c * P:(c + 1) * P],
                                          normed[:, t, c * P:(c + 1) * P], ident[:])
                    mm.then_inc(pe_done.sem, 1)

            @block.scalar
            def _(act):
                s_ = Steps(act, act_step)
                for t in range(TT):
                    s_.link(act.activation(normed[:, t, :], z_tok[:, t, :], ACT.Square,
                                           accum_out=stat[:, t:t + 1]))
                act.activation(stat[:, 2:4], stat[:, 0:2], ACT.Sqrt, bias=eps[:], scale=1.0 / D) \
                   .then_inc(act_ready.sem, 1)
                act.wait_ge(vec_ready.sem, vec_ready.at(1))
                for t in range(TT):
                    act.activation(normed[:, t, :], z_tok[:, t, :], ACT.Copy,
                                   scale=stat[:, 4 + t:5 + t]).then_inc(act_ready.sem, 1)
                act.wait_ge(cols_ready.sem, cols_ready.at(1))
                for t in range(TT):
                    act.wait_ge(pe_done.sem, pe_done.at(t + 1))
                    for c in range(KC):
                        act.activation(full[:, c, t * P:(t + 1) * P], ps[:, t, c * P:(c + 1) * P],
                                       ACT.Identity, bias=shift(c), scale=scol[:, c:c + 1])

            @block.vector
            def _(dve):
                dve.scalar_tensor_tensor(out=scol[:], in0=scale, scalar=1.0, in1=gain,
                                         op0=ALU.add, op1=ALU.mult).then_inc(cols_ready.sem, 1)
                if heads:
                    experts.use(dve, 0, 0, 2)
                dve.wait_ge(act_ready.sem, act_ready.at(1))
                dve.reciprocal(stat[:, 4:6], stat[:, 2:4]).then_inc(vec_ready.sem, 1)
                for head in range(heads):
                    experts.use(dve, head, 0 if head else 2, TOPK)
        experts.end_phase(heads)
        cols_ready.base += 1
        pe_done.base += 2
        act_ready.base += 3
        vec_ready.base += 1

    def broadcast_row(pe, column, unit):
        for c in range(KC):
            mm = pe.matmul(ps[:, unit, c * P:(c + 1) * P], column(c).to_broadcast([P, P]), ident[:],
                           start=True, stop=True)
        return mm

    def input_projection(l, qa, sg, km, ia, ga, qb, kb, vb):
        weights.begin(f"in{l}")
        flat = {0: qa, 2: qb, 3: kb}
        tokens = {4: ia, 6: vb}
        n = 7
        with nc.Block() as block:
            @block.sync
            def _(sp):
                weights.feed(sp)

            @block.tensor
            def _(pe):
                for t in range(n):
                    unit_wait(pe, t % 2, t // 2)
                    if t in (4, 5, 6):
                        project_tokens(pe, t, tiles_of(t % 2), hT)
                    else:
                        project_features(pe, t, blocks_of(t % 2), hT)

            @block.scalar
            def _(act):
                for t in range(n):
                    split_ahead(act=act, tile=(t, t % 2, t // 2))
                    if t == 1:
                        product_wait(act, t)
                        act.activation(sg.rearrange("p h t -> p (h t)"), ps[:, t % 2, :], ACT.Sigmoid)
                        act.activation(km.rearrange("p h t -> p (h t)"), ps[:, t % 2, :],
                                       ACT.Sigmoid, scale=-1.0).then_inc(unit_free[t % 2].sem, 1)
                    elif t == 5:
                        product_wait(act, t)
                        act.activation(ga.rearrange("p t n -> p (t n)"), ps[:, t % 2, :],
                                       ACT.Sigmoid).then_inc(act_ready.sem, 1)

            @block.vector
            def _(dve):
                for t in range(n):
                    split_ahead(dve=dve, tile=(t, t % 2, t // 2))
                    if t == 1:
                        continue
                    product_wait(dve, t)
                    if t == 5:
                        dve.wait_ge(act_ready.sem, act_ready.at(1))
                        g = ga.rearrange("p t n -> p (t n)")
                        dve.tensor_tensor(g, ps[:, t % 2, :], g, ALU.mult) \
                           .then_inc(unit_free[t % 2].sem, 1)
                    else:
                        dst = flat.get(t, tokens.get(t)).rearrange("p h t -> p (h t)")
                        dve.tensor_copy(dst, ps[:, t % 2, :]).then_inc(unit_free[t % 2].sem, 1)
        act_ready.base += 1
        units_used(n)
        weights.end()

    def gate_projection(l, gates):
        weights.begin(f"gates{l}")
        with nc.Block() as block:
            @block.sync
            def _(sp):
                weights.feed(sp)

            @block.tensor
            def _(pe):
                for t in range(4):
                    unit_wait(pe, t % 2, t // 2)
                    project_features(pe, t, blocks_of(t % 2), hT)

            @block.scalar
            def _(act):
                for t in range(4):
                    split_ahead(act=act, tile=(t, t % 2, t // 2))
                    product_wait(act, t)
                    g = gates[:, t * 4:(t + 1) * 4, :].rearrange("p b t -> p (b t)")
                    act.activation(g, ps[:, t % 2, :], ACT.Sigmoid).then_inc(unit_free[t % 2].sem, 1)

            @block.vector
            def _(dve):
                for t in range(4):
                    split_ahead(dve=dve, tile=(t, t % 2, t // 2))
        units_used(4)
        weights.end()

    def hgrn(l, qa, sg, km, ia, ga, oaT, tmp, beside):
        B, E, qe, ke, scores, cross, o, sq = tmp
        blocks = HG_HEADS * TT
        NL = len(LEVELS)
        with nc.Block() as block:
            @block.sync
            def _(sp):
                beside.feed(sp)

            @block.tensor
            def _(pe):
                beside.halves(pe, 0, 3)
                pe.wait_ge(vec_ready.sem, vec_ready.at(1))
                for h in range(HG_HEADS):
                    for t in range(TT):
                        b = h * TT + t
                        mm = pe.matmul(ps[:, 0, b * P:(b + 1) * P], km[:, h, t * P:(t + 1) * P],
                                       qa[:, h, t * P:(t + 1) * P], start=True, stop=True)
                mm.then_inc(pe_done.sem, 1)
                for n in range(NL):
                    pe.wait_ge(vec_ready.sem, vec_ready.at(2 + n))
                    for b in range(blocks):
                        mm = pe.matmul(ps[:, (n + 1) % 2, b * P:(b + 1) * P],
                                       ke[:, b * P:(b + 1) * P], qe[:, b * P:(b + 1) * P],
                                       start=True, stop=True)
                    mm.then_inc(pe_done.sem, 1)
                    beside.halves(pe, 3 + n, 4 + n)
                pe.wait_ge(vec_ready.sem, vec_ready.at(2 + NL))
                for h in range(HG_HEADS):
                    mm = pe.matmul(ps[:, 0, h * P:(h + 1) * P], ke[:, 2 * h * P:(2 * h + 1) * P],
                                   qe[:, (2 * h + 1) * P:(2 * h + 2) * P], start=True, stop=True)
                mm.then_inc(pe_done.sem, 1)
                beside.halves(pe, 3 + NL, 4 + NL)
                pe.wait_ge(vec_ready.sem, vec_ready.at(3 + NL))
                for t in range(TT):
                    for h in range(HG_HEADS):
                        b = h * TT + t
                        dst = ps[:, 1, t * 512 + h * P:t * 512 + (h + 1) * P]
                        mm = pe.matmul(dst, scores[:, b * P:(b + 1) * P], ia[:, t, h * P:(h + 1) * P],
                                       start=True, stop=(t == 0))
                        if t == 1:
                            mm = pe.matmul(dst, cross[:, h * P:(h + 1) * P],
                                           ia[:, 0, h * P:(h + 1) * P], start=False, stop=True)
                mm.then_inc(pe_done.sem, 1)
                beside.halves(pe, 4 + NL, 5 + NL)
                pe.wait_ge(vec_ready.sem, vec_ready.at(5 + NL))
                for h in range(HG_HEADS):
                    for t in range(TT):
                        mm = pe.transpose(ps[:, 0, h * SEQ + t * P:h * SEQ + (t + 1) * P],
                                          o[:, t, h * P:(h + 1) * P], ident[:])
                mm.then_inc(pe_done.sem, 1)
                beside.halves(pe, 5 + NL, 2 * beside.tiles)

            @block.scalar
            def _(act):
                act.wait_ge(cols_ready.sem, cols_ready.at(1))
                act.activation(sg.rearrange("p h t -> p (h t)"), sg.rearrange("p h t -> p (h t)"),
                               ACT.Ln).then_inc(act_ready.sem, 1)
                beside.copies(act, 0)
                for n in range(NL + 1):
                    act.wait_ge(cols_ready.sem, cols_ready.at(2 + n))
                    act.activation(E[:], E[:], ACT.Exp).then_inc(act_ready.sem, 1)
                    if n % 2:
                        beside.copies(act, (n + 1) // 2)
                act.wait_ge(vec_ready.sem, vec_ready.at(4 + NL))
                act.activation(stat[:, 8:16], stat[:, 0:8], ACT.Sqrt).then_inc(act_ready.sem, 1)
                for t in range((NL + 3) // 2, beside.tiles):
                    beside.copies(act, t)

            @block.vector
            def _(dve):
                v = Steps(dve, vec_step)
                v.tick(dve.memset(qe[:], 0.0))
                v.tick(dve.memset(ke[:], 0.0))
                v.tick(dve.memset(scores[:], 0.0))
                for h in range(HG_HEADS):
                    ins = dve.tensor_scalar(sg[:, h, :], sg[:, h, :], lbcol[:, l, 1, h:h + 1],
                                            lbcol[:, l, 0, h:h + 1], ALU.mult, ALU.add)
                    if h < HG_HEADS - 1:
                        v.tick(ins)
                v.wait()
                ins.then_inc(cols_ready.sem, 1)
                for h in range(HG_HEADS):
                    ins = dve.tensor_scalar(km[:, h, :], km[:, h, :], lbcol[:, l, 1, h:h + 1], None,
                                            ALU.mult)
                    if h < HG_HEADS - 1:
                        v.tick(ins)
                v.wait()
                ins.then_inc(vec_ready.sem, 1)
                dve.wait_ge(act_ready.sem, act_ready.at(1))
                for h in range(HG_HEADS):
                    for t in range(TT):
                        b = h * TT + t
                        v.tick(dve.tensor_tensor_scan(
                            B[:, b * P:(b + 1) * P], ones[:], sg[:, h, t * P:(t + 1) * P], 0.0,
                            ALU.mult, ALU.add))
                v.wait()
                q_all = qa.rearrange("p h t -> p (h t)")
                k_all = km.rearrange("p h t -> p (h t)")

                def take(n):
                    dve.wait_ge(pe_done.sem, pe_done.at(n + 1))
                    mask = level_mask[:, n, :].unsqueeze(1).to_broadcast([P, blocks, P])
                    v.link(dve.copy_predicated(
                        scores.rearrange("p (b t) -> p b t", t=P), mask,
                        ps[:, n % 2, :].rearrange("p (b t) -> p b t", t=P)))

                for n, m in enumerate(LEVELS):
                    nb = 1024 // (2 * m)

                    def halves(ap):
                        r = ap.rearrange("p (b two m) -> p b two m", two=2, m=m)
                        return r[:, :, 0, :], r[:, :, 1, :]
                    b_lo, b_hi = halves(B)
                    e_lo, e_hi = halves(E)
                    mid = b_lo[:, :, m - 1:m].to_broadcast([P, nb, m])
                    v.tick(dve.tensor_tensor(e_hi, b_hi, mid, ALU.subtract))
                    v.wait()
                    dve.tensor_tensor(e_lo, mid, b_lo, ALU.subtract).then_inc(cols_ready.sem, 1)
                    if n >= 1:
                        take(n - 1)
                    dve.wait_ge(act_ready.sem, act_ready.at(2 + n))
                    if n >= 1:
                        dve.wait_ge(pe_done.sem, pe_done.at(n + 1))
                    v.link(dve.tensor_tensor(halves(qe)[1], halves(q_all)[1], e_hi, ALU.mult))
                    dve.tensor_tensor(halves(ke)[0], halves(k_all)[0], e_lo, ALU.mult) \
                       .then_inc(vec_ready.sem, 1)
                    dve.wait_ge(vec_ready.sem, vec_ready.at(2 + n))
                tiles = [ap.rearrange("p (h t m) -> p h t m", t=TT, m=P) for ap in (B, E, qe, ke, q_all, k_all)]
                tb, te, tq, tk, tqa, tka = tiles
                v.link(dve.tensor_copy(te[:, :, 1, :], tb[:, :, 1, :]))
                dve.tensor_tensor(te[:, :, 0, :], tb[:, :, 0, P - 1:P].to_broadcast([P, HG_HEADS, P]),
                                  tb[:, :, 0, :], ALU.subtract).then_inc(cols_ready.sem, 1)
                take(NL - 1)
                dve.wait_ge(act_ready.sem, act_ready.at(2 + NL))
                dve.wait_ge(pe_done.sem, pe_done.at(NL + 1))
                v.link(dve.tensor_tensor(tq[:, :, 1, :], tqa[:, :, 1, :], te[:, :, 1, :], ALU.mult))
                dve.tensor_tensor(tk[:, :, 0, :], tka[:, :, 0, :], te[:, :, 0, :], ALU.mult) \
                   .then_inc(vec_ready.sem, 1)
                take(NL)
                dve.wait_ge(pe_done.sem, pe_done.at(NL + 2))
                dve.tensor_copy(cross[:], ps[:, 0, 0:512]).then_inc(vec_ready.sem, 1)
                dve.wait_ge(pe_done.sem, pe_done.at(NL + 3))
                o_flat = o.rearrange("p t n -> p (t n)")
                v.link(dve.tensor_copy(o_flat, ps[:, 1, :]))
                v.link(dve.tensor_tensor(sq[:], o_flat, o_flat, ALU.mult))
                v.link(dve.tensor_reduce(stat[:, 0:8], sq.rearrange("p (b e) -> p b e", e=P), AX_X,
                                         ALU.add))
                dve.tensor_scalar(stat[:, 0:8], stat[:, 0:8], 1.0 / P, RMS_EPS, ALU.mult, ALU.add) \
                   .then_inc(vec_ready.sem, 1)
                v.link(dve.tensor_tensor(o_flat, o_flat, ga.rearrange("p t n -> p (t n)"), ALU.mult))
                dve.wait_ge(act_ready.sem, act_ready.at(3 + NL))
                v.link(dve.reciprocal(stat[:, 16:24], stat[:, 8:16]))
                o_heads = o_flat.rearrange("p (b e) -> p b e", e=P)
                dve.tensor_tensor(o_heads, o_heads,
                                  stat[:, 16:24].unsqueeze(2).to_broadcast([P, 8, P]), ALU.mult) \
                   .then_inc(vec_ready.sem, 1)
                dve.wait_ge(pe_done.sem, pe_done.at(4 + NL))
                for part in range(2):
                    for h in range(HG_HEADS):
                        gain = vcol[:, 3, V_HGG + 4 * l + h:V_HGG + 4 * l + h + 1]
                        src = ps[:, 0, h * SEQ:(h + 1) * SEQ]
                        if part == 0:
                            v.tick(dve.tensor_scalar(oaT[0][:, h, :], src, gain, None, ALU.mult))
                        else:
                            v.tick(dve.scalar_tensor_tensor(
                                out=oaT[1][:, h, :], in0=src, scalar=gain,
                                in1=oaT[0][:, h, :].bitcast(F32), op0=ALU.mult, op1=ALU.subtract))
                    v.wait()
        cols_ready.base += 2 + NL
        vec_ready.base += 5 + NL
        act_ready.base += 3 + NL
        pe_done.base += 4 + NL
        beside.end_phase()

    def stick_breaking(qb, kb, vb, obT, tmp, beside):
        Y, L, S = tmp
        scale = 1.0 / math.sqrt(SB_DH)
        groups = SB_HEADS // 4
        ahead = weights.first_tile(weights.group(1 if beside.tiles else 0))
        W_ = SEQ + P

        def unit(base, n):
            return ps[:, base + n // 2, (n % 2) * 512:(n % 2) * 512 + W_]

        def both(base):
            return ps[:, base:base + 2, :].rearrange("p u (h n) -> p u h n", h=2)[:, :, :, 0:W_]

        def by_unit(ap):
            return ap.rearrange("p (u h) n -> p u h n", h=2)

        with nc.Block() as block:
            if beside.tiles:
                @block.sync
                def _(sp):
                    beside.feed(sp)

            @block.tensor
            def _(pe):
                for g in range(groups):
                    if g:
                        pe.wait_ge(vec_ready.sem, vec_ready.at(3 * g))
                    for n in range(4):
                        h = 4 * g + n
                        at = slice(64 * (h % 2), 64 * (h % 2) + 64)
                        u = unit(0, n)
                        pe.matmul(u[:, 0:SEQ], kb[at, h // 2, 0:P], qb[at, h // 2, :],
                                  start=True, stop=True)
                        mm = pe.matmul(u[:, SEQ:W_], kb[at, h // 2, P:SEQ], qb[at, h // 2, P:SEQ],
                                       start=True, stop=True)
                    mm.then_inc(pe_done.sem, 1)
                    beside.halves(pe, 5 * g, 5 * g + 4)
                    pe.wait_ge(vec_ready.sem, vec_ready.at(3 * g + 1))
                    for n in range(4):
                        u = unit(0, n)
                        pe.matmul(u[:, 0:SEQ], tri[:], L[:, n, 0:SEQ], start=True, stop=False)
                        pe.matmul(u[:, P:SEQ], ones[:], L[:, n, SEQ:W_], start=False, stop=True)
                        mm = pe.matmul(u[:, SEQ:W_], tri[:], L[:, n, SEQ:W_], start=True, stop=True)
                    mm.then_inc(pe_done.sem, 1)
                    beside.halves(pe, 5 * g + 4, 5 * g + 5)
                    pe.wait_ge(act_ready.sem, act_ready.at(4 * g + 4))
                    for n in range(4):
                        h = 4 * g + n
                        dst = ps[64 * (h % 2):64 * (h % 2) + 64, 0, (n // 2) * SEQ:(n // 2 + 1) * SEQ]
                        pe.matmul(dst, vb[:, 0, h * 64:(h + 1) * 64], S[:, n, 0:SEQ],
                                  start=True, stop=False, skip_group_check=True)
                        mm = pe.matmul(dst[:, P:SEQ], vb[:, 1, h * 64:(h + 1) * 64], S[:, n, SEQ:W_],
                                       start=False, stop=True, skip_group_check=True)
                    mm.then_inc(pe_done.sem, 1)
                beside.halves(pe, 5 * groups, 2 * beside.tiles)

            @block.scalar
            def _(act):
                s = Steps(act, act_step)
                for g in range(groups):
                    act.wait_ge(pe_done.sem, pe_done.at(3 * g + 1))
                    act.activation(by_unit(Y), both(0), ACT.Copy, scale=scale) \
                       .then_inc(act_ready.sem, 1)
                    act.wait_ge(act_ready.sem, act_ready.at(4 * g + 1))
                    if g:
                        act.wait_ge(vec_ready.sem, vec_ready.at(3 * g))
                    s.link(act.activation(L[:], Y[:], ACT.Abs))
                    s.link(act.activation(L[:], L[:], ACT.Exp, scale=-1.0))
                    act.activation(L[:], L[:], ACT.Ln, bias=1.0).then_inc(act_ready.sem, 1)
                    for t in ((0,), (2, 3))[g]:
                        beside.copies(act, t)
                    act.wait_ge(vec_ready.sem, vec_ready.at(3 * g + 2))
                    act.activation(S[:], S[:], ACT.Exp).then_inc(act_ready.sem, 2)
                    beside.copies(act, (1, 4)[g])
                for t in range(5, beside.tiles):
                    beside.copies(act, t)
                weights.split_hi(act, ahead)

            @block.vector
            def _(dve):
                v = Steps(dve, vec_step)
                for g in range(groups):
                    dve.wait_ge(act_ready.sem, act_ready.at(4 * g + 2))
                    v.link(dve.scalar_tensor_tensor(out=L[:], in0=Y[:], scalar=0.0, in1=L[:],
                                                    op0=ALU.max, op1=ALU.add))
                    mask = before[:].unsqueeze(1).to_broadcast([P, 4, P])
                    v.link(dve.tensor_tensor(L[:, :, 0:P], L[:, :, 0:P], mask, ALU.mult))
                    dve.tensor_tensor(L[:, :, SEQ:W_], L[:, :, SEQ:W_], mask, ALU.mult) \
                       .then_inc(vec_ready.sem, 1)
                    dve.wait_ge(pe_done.sem, pe_done.at(3 * g + 2))
                    v.link(dve.tensor_tensor(by_unit(S), by_unit(Y), both(0), ALU.subtract))
                    neg = before_neg[:].unsqueeze(1).to_broadcast([P, 4, P])
                    v.link(dve.tensor_tensor(S[:, :, 0:P], S[:, :, 0:P], neg, ALU.add))
                    dve.tensor_tensor(S[:, :, SEQ:W_], S[:, :, SEQ:W_], neg, ALU.add) \
                       .then_inc(vec_ready.sem, 1)
                    dve.wait_ge(pe_done.sem, pe_done.at(3 * g + 3))
                    hi, lo = [o[:, 2 * g:2 * g + 2, :].rearrange("p c t -> p (c t)") for o in obT]
                    v.link(dve.tensor_copy(hi, ps[:, 0, 0:512]))
                    dve.tensor_tensor(lo, ps[:, 0, 0:512], hi.bitcast(F32), ALU.subtract) \
                       .then_inc(vec_ready.sem, 1)
                dve.wait_ge(mod_copied.sem, mod_copied.at(beside.tiles))
                for _, cond, dst, bias in beside.targets:
                    v.tick(dve.tensor_tensor(dst, dst, bias.unsqueeze(2).to_broadcast(dst.shape),
                                             ALU.add))
                weights.split_lo(dve, ahead)
        beside.end_phase()
        vec_ready.base += 3 * groups
        act_ready.base += 4 * groups
        pe_done.base += 3 * groups

    def merge(l, oaT, obT, gates):
        weights.begin(f"up{l}")
        with nc.Block() as block:
            @block.sync
            def _(sp):
                weights.feed(sp)

            @block.tensor
            def _(pe):
                for k, src in enumerate((oaT, obT)):
                    project_features(pe, k, lambda b, k=k: ps[:, 2 * k + b // 4,
                                                              b % 4 * SEQ:(b % 4 + 1) * SEQ], src)

            @block.scalar
            def _(act):
                for t in range(2):
                    split_ahead(act=act, tile=(t, t, 0))
                act.wait_ge(vec_ready.sem, vec_ready.at(1))
                act.activation(hT_hi[:], gates[:, 0:KC, :], ACT.Copy).then_inc(act_ready.sem, 1)

            @block.vector
            def _(dve):
                v = Steps(dve, vec_step)
                for k in range(2):
                    split_ahead(dve=dve, tile=(k, k, 0))
                    product_wait(dve, k)
                    g = gates[:, k * KC:(k + 1) * KC, :].rearrange("p (u b) t -> p u (b t)", u=2)
                    v.link(dve.tensor_tensor(g, g, ps[:, 2 * k:2 * k + 2, :], ALU.mult))
                dve.tensor_tensor(gates[:, 0:KC, :], gates[:, 0:KC, :], gates[:, KC:2 * KC, :],
                                  ALU.add).then_inc(vec_ready.sem, 1)
                dve.wait_ge(act_ready.sem, act_ready.at(1))
                v.tick(dve.tensor_tensor(hT_lo[:], gates[:, 0:KC, :], hT_hi[:].bitcast(F32),
                                         ALU.subtract))
        vec_ready.base += 1
        act_ready.base += 1
        weights.end()

    def residual_norm(dve, act_, v, pieces, gate, gain, shift):
        for t, c0, part in pieces:
            cols = slice(c0, c0 + 512)
            v.link(dve.tensor_tensor(y_tok[:, t, cols], part, gate[:, cols], ALU.mult))
            v.link(dve.scalar_tensor_tensor(out=x_tok[:, t, cols], in0=x_tok[:, t, cols],
                                            scalar=DN_ALPHA, in1=y_tok[:, t, cols],
                                            op0=ALU.mult, op1=ALU.add))
        for t in range(TT):
            for k in range(2):
                v.link(dve.bn_stats(stat[:, 16 + 12 * t + 6 * k:22 + 12 * t + 6 * k],
                                    x_tok[:, t, k * 512:(k + 1) * 512]))
            v.link(dve.bn_aggr(stat[:, 2 * t:2 * t + 2], stat[:, 16 + 12 * t:28 + 12 * t]))
        mean_var = stat[:, 0:4].rearrange("p (t k) -> p t k", k=2)
        dve.tensor_scalar(stat[:, 4:6], mean_var[:, :, 1], LN_EPS, None, ALU.add) \
           .then_inc(vec_ready.sem, 1)
        dve.wait_ge(act_ready.sem, act_ready.at(act_))
        v.link(dve.reciprocal(stat[:, 8:10], stat[:, 6:8]))
        for t in range(TT):
            v.link(dve.tensor_scalar(x_tok[:, t, :], x_tok[:, t, :], stat[:, 2 * t:2 * t + 1],
                                     stat[:, 8 + t:9 + t], ALU.subtract, ALU.mult))
            v.link(dve.tensor_tensor(x_tok[:, t, :], x_tok[:, t, :], gain, ALU.mult))
            v.tick(dve.tensor_tensor(x_tok[:, t, :], x_tok[:, t, :], shift, ALU.add))

    def load_rows(sp, l, k):
        sp.dma_start(rows[:, 1, :], a["ln_g"][l, k:k + 1, :].to_broadcast([P, D])) \
          .then_inc(loaded.sem, 16)
        sp.dma_start(rows[:, 2, :], a["ln_b"][l, k:k + 1, :].to_broadcast([P, D])) \
          .then_inc(loaded.sem, 16)

    def output_projection(l):
        weights.begin(f"o{l}")
        with nc.Block() as block:
            @block.sync
            def _(sp):
                load_rows(sp, l, 0)
                weights.feed(sp)

            @block.tensor
            def _(pe):
                broadcast_row(pe, lambda c: adacol[:, l, 16 + c:17 + c], 2).then_inc(pe_done.sem, 1)
                for t in range(2):
                    project_tokens(pe, t, tiles_of(t), hT)

            @block.scalar
            def _(act):
                for t in range(2):
                    split_ahead(act=act, tile=(t, t, 0))
                act.wait_ge(pe_done.sem, pe_done.at(1))
                act.copy(rows[:, 0, :], ps[:, 2, :]).then_inc(act_ready.sem, 1)
                act.wait_ge(vec_ready.sem, vec_ready.at(1))
                act.activation(stat[:, 6:8], stat[:, 4:6], ACT.Sqrt).then_inc(act_ready.sem, 1)

            @block.vector
            def _(dve):
                v = Steps(dve, vec_step)
                for t in range(2):
                    split_ahead(dve=dve, tile=(t, t, 0))
                dve.wait_ge(act_ready.sem, act_ready.at(1))
                dve.wait_ge(loaded.sem, loaded.at(32))
                product_wait(dve, 1)
                pieces = [(t, k * 512, ps[:, k, t * 512:(t + 1) * 512])
                          for k in range(2) for t in range(TT)]
                residual_norm(dve, 2, v, pieces, rows[:, 0, :], rows[:, 1, :], rows[:, 2, :])
        loaded.base += 32
        pe_done.base += 1
        act_ready.base += 2
        vec_ready.base += 1
        weights.end()

    def peer_queries(l, hf_tok, pqT, keys, keysT, sc):
        weights.begin(f"pq{l}")
        with nc.Block() as block:
            @block.sync
            def _(sp):
                for half in range(2):
                    sp.dma_start(keys[:, :, half * 64:(half + 1) * 64],
                                 a["sub_keys"][l, half].rearrange("h n d -> n h d")) \
                      .then_inc(loaded.sem, 16)
                weights.feed(sp)

            @block.tensor
            def _(pe):
                for t in range(2):
                    project_features(pe, t, blocks_of(t), hT)
                broadcast_row(pe, lambda c: scol[:, c:c + 1], 2).then_inc(pe_done.sem, 1)
                broadcast_row(pe, lambda c: adacol[:, l, 24 + c:25 + c], 3).then_inc(pe_done.sem, 1)
                pe.wait_ge(loaded.sem, loaded.at(32))
                pe.wait_ge(act_ready.sem, act_ready.at(1))
                for h in range(PEER_HEADS):
                    mm = pe.transpose(ps[:, 2, h * P:(h + 1) * P], keys[:, h, :], ident[:])
                mm.then_inc(pe_done.sem, 1)
                pe.wait_ge(act_ready.sem, act_ready.at(4))
                for t in range(TT):
                    if t:
                        pe.wait_ge(act_ready.sem, act_ready.at(5))
                    for h in range(PEER_HEADS):
                        for half in range(2):
                            at = slice(64 * half, 64 * half + 64)
                            mm = pe.matmul(ps[:, half, h * P:(h + 1) * P],
                                           pqT[at, h, t * P:(t + 1) * P], keysT[at, h, :],
                                           start=True, stop=True)
                    mm.then_inc(pe_done.sem, 1)

            @block.scalar
            def _(act):
                for t in range(2):
                    split_ahead(act=act, tile=(t, t, 0))
                act.wait_ge(pe_done.sem, pe_done.at(1))
                act.copy(rows[:, 0, :], ps[:, 2, :]).then_inc(act_ready.sem, 1)
                product_wait(act, 1)
                for t in range(2):
                    ins = act.copy(pqT[:, 4 * t:4 * t + 4, :].rearrange("p b t -> p (b t)"),
                                   ps[:, t, :])
                    if t:
                        ins.then_inc(act_ready.sem, 1)
                act.wait_ge(pe_done.sem, pe_done.at(2))
                act.copy(rows[:, 1, :], ps[:, 3, :]).then_inc(act_ready.sem, 1)
                act.wait_ge(pe_done.sem, pe_done.at(3))
                act.copy(keysT.rearrange("p h n -> p (h n)"), ps[:, 2, :]).then_inc(act_ready.sem, 1)
                for t in range(TT):
                    act.wait_ge(pe_done.sem, pe_done.at(4 + t))
                    act.copy(sc[:, t], ps[:, 0:2, :]) \
                       .then_inc(act_ready.sem, 1)

            @block.vector
            def _(dve):
                v = Steps(dve, vec_step)
                for t in range(2):
                    split_ahead(dve=dve, tile=(t, t, 0))
                dve.wait_ge(act_ready.sem, act_ready.at(3))
                for t in range(TT):
                    v.link(dve.tensor_tensor(hf_tok[:, t, :], x_tok[:, t, :], rows[:, 0, :], ALU.mult))
                    v.link(dve.tensor_tensor(hf_tok[:, t, :], hf_tok[:, t, :], rows[:, 1, :], ALU.add))
        loaded.base += 32
        pe_done.base += 5
        act_ready.base += 6
        weights.end()

    class SideModulation:

        def __init__(self, targets):
            self.targets = targets
            self.each = [(cond, dst[:, 4 * t:4 * t + 4, :]) for n, cond, dst, _ in targets
                         for t in range(n)]
            self.first, self.tiles = 0, 0

        def target(self, t):
            cond, dst = self.each[self.first + t]
            k = cond.shape[2]
            return cond, dst, k, side[0:k, t % 2 * 512:(t % 2 + 1) * 512]

        def turn_row(self, pe, t):
            pe.wait_ge(mod_rows.sem, mod_rows.at(t + 1))
            u, (_, _, k, row) = t % 2, self.target(t)
            for b in range(4):
                mm = pe.matmul(ps[:, 2 + u, 512 + k * b:512 + k * b + k],
                               row[:, b * P:(b + 1) * P], ident[0:k, 0:k],
                               start=True, stop=True)
            mm.then_inc(mod_turned.sem, 1)

        def halves(self, pe, first, last):
            for n in range(first, min(last, 2 * self.tiles)):
                t, half = n // 2, n % 2
                if half == 0:
                    if t >= 2:
                        pe.wait_ge(mod_copied.sem, mod_copied.at(t - 1))
                    self.sections = weights.sections(pe, self.first + t, t % 2,
                                                     (self.first + t) // 2)
                start, chunks, (part,) = next(self.sections)
                cond, _, k, _ = self.target(t)
                for c in range(chunks):
                    mm = pe.matmul(ps[0:k, 2 + t % 2, 0:512], cond[:, start + c, :],
                                   part[:, c, :], start=start + c == 0, stop=start + c == KC - 1,
                                   skip_group_check=True)
                weights.section_done(mm)
                if half == 0 and t >= 1:
                    self.turn_row(pe, t - 1)
                if n == 2 * self.tiles - 1:
                    self.turn_row(pe, t)

        def copy_columns(self, act, t):
            act.wait_ge(mod_turned.sem, mod_turned.at(t + 1))
            _, dst, k, _ = self.target(t)
            act.copy(dst, ps[:, 2 + t % 2, 512:512 + 4 * k].rearrange("p (b k) -> p b k", k=k)) \
               .then_inc(mod_copied.sem, 1)

        def copies(self, act, t):
            if t >= self.tiles:
                return
            product_wait(act, self.first + t)
            if t >= 2:
                act.wait_ge(mod_copied.sem, mod_copied.at(t - 1))
            _, _, k, row = self.target(t)
            act.copy(row, ps[0:k, 2 + t % 2, 0:512]).then_inc(mod_rows.sem, 1)
            if t:
                self.copy_columns(act, t - 1)
            if t == self.tiles - 1:
                self.copy_columns(act, t)

        def feed(self, sp):
            weights.feed(sp, self.first, self.first + self.tiles)

        def end_phase(self):
            self.first += self.tiles
            for signal_ in (mod_rows, mod_turned, mod_copied):
                signal_.base += self.tiles
            if self.first == weights.group().n:
                weights.end()

    def modulation_programs(l, row):
        n = weights.group().n
        at0 = 72 - 4 * n

        def tensor(pe):
            def turn_row(t, j):
                pe.wait_ge(mod_rows.sem, t + mod_rows.at(1))
                for b in range(4):
                    mm = pe.matmul(ps[:, j, 512 + 2 * b:514 + 2 * b], row[:, j, b * P:(b + 1) * P],
                                   ident[0:2, 0:2], start=True, stop=True)
                mm.then_inc(mod_turned.sem, 1)

            def tile(t, j, turn):
                unit_wait(pe, j, turn)
                for start, chunks, (part,) in weights.sections(pe, t, j, turn):
                    for c in range(chunks):
                        mm = pe.matmul(ps[0:2, j, 0:512], condT[:, start + c, 1:3], part[:, c, :],
                                       start=start + c == 0, stop=start + c == KC - 1)
                    weights.section_done(mm)
                if j == 1:
                    turn_row(t - 1, 0)
                    turn_row(t, 1)
            in_pairs(n, pe, tile)

        def scalar(act, first, last):
            if first == last:
                return
            with act.Fori(first, last) as i:
                for j in range(2):
                    product_wait(act, i * 2 + j)
                    act.copy(row[:, j, :], ps[0:2, j, 0:512]).then_inc(mod_rows.sem, 1)
                for j in range(2):
                    act.wait_ge(mod_turned.sem, i * 2 + mod_turned.at(1 + j))
                    act.copy(modcol[:, l, bass.ds(i * 8 + (at0 + 4 * j), 4), :],
                             ps[:, j, 512:520].rearrange("p (b k) -> p b k", k=2)) \
                       .then_inc(unit_free[j].sem, 1)
        return n, tensor, scalar

    def peer_select(l, sc, best, bestf, cand, pos, p12, eq, sel, index, gate):
        def top16(dve, v, values, idx, scores):
            v.link(dve.max(values[:, 0:8], scores))
            v.link(dve.max_index(idx[:, 0:8], values[:, 0:8], scores))
            v.link(dve.match_replace(scores, values[:, 0:8], scores, -3.0e38))
            v.link(dve.max(values[:, 8:16], scores))
            v.tick(dve.max_index(idx[:, 8:16], values[:, 8:16], scores))

        weights.begin(f"mod{l}")
        pairs = weights.group().n // 2
        tiles, mod_tensor, mod_scalar = modulation_programs(
            l, rows[0:2, 0, :].rearrange("k (u n) -> k u n", u=2))
        with nc.Block() as block:
            @block.sync
            def _(sp):
                weights.feed(sp)

            @block.tensor
            def _(pe):
                mod_tensor(pe)

            @block.scalar
            def _(act):
                for t in range(TT):
                    mod_scalar(act, t * (pairs // 2), pairs if t else pairs // 2)
                    act.wait_ge(vec_ready.sem, vec_ready.at(t + 1))
                    act.activation(gate[:, t], gate[:, t], ACT.Exp).then_inc(act_ready.sem, 1)

            @block.vector
            def _(dve):
                v = Steps(dve, vec_step)
                for t in range(TT):
                    for h in range(PEER_HEADS):
                        for half in range(2):
                            n = h * 2 + half
                            top16(dve, v, best[:, n, :], pos[:, n, :], sc[:, t, half, h * P:(h + 1) * P])
                    v.wait()
                    v.link(dve.tensor_copy(bestf, pos))
                    b = best.rearrange("p (h two) k -> p h two k", two=2)
                    v.link(dve.tensor_tensor(
                        cand.rearrange("p h (i j) -> p h i j", j=TOPK),
                        b[:, :, 0, :].unsqueeze(3).to_broadcast([P, PEER_HEADS, TOPK, TOPK]),
                        b[:, :, 1, :].unsqueeze(2).to_broadcast([P, PEER_HEADS, TOPK, TOPK]),
                        ALU.add))
                    top = gate[:, t]
                    for h in range(PEER_HEADS):
                        top16(dve, v, top[:, h, :], pos[:, h, :], cand[:, h, :])
                    v.wait()
                    at = pos[:, 0:PEER_HEADS, :]
                    v.link(dve.tensor_scalar(p12[:, 0], at, 4, None, ALU.logical_shift_right))
                    v.link(dve.tensor_scalar(p12[:, 1], at, 15, None, ALU.bitwise_and))
                    v.link(dve.tensor_copy(sel, p12))
                    bf = bestf.rearrange("p (h two) k -> p h two k", two=2)
                    shape = [P, PEER_HEADS, TOPK, TOPK]
                    e4 = eq.rearrange("p h (k j) -> p h k j", j=TOPK)
                    steps16 = iota16[:].unsqueeze(1).unsqueeze(1).to_broadcast(shape)
                    for k in range(2):
                        v.link(dve.tensor_tensor(e4, sel[:, k].unsqueeze(3).to_broadcast(shape),
                                                 steps16, ALU.is_equal))
                        v.link(dve.tensor_tensor(e4, e4, bf[:, :, k, :].unsqueeze(2).to_broadcast(shape),
                                                 ALU.mult))
                        v.link(dve.tensor_reduce(sel[:, k], e4, AX_X, ALU.add))
                    v.link(dve.tensor_scalar(sel[:, 1], sel[:, 1], float(l * NKEYS * NKEYS), None,
                                             ALU.add))
                    v.link(dve.scalar_tensor_tensor(out=index[:, t], in0=sel[:, 0],
                                                    scalar=float(NKEYS), in1=sel[:, 1],
                                                    op0=ALU.mult, op1=ALU.add))
                    v.link(dve.tensor_copy(stat[:, 0:8], top[:, :, 0]))
                    m = stat[:, 0:8].unsqueeze(2).to_broadcast([P, PEER_HEADS, TOPK])
                    dve.tensor_tensor(top, top, m, ALU.subtract).then_inc(vec_ready.sem, 1)
                    dve.wait_ge(act_ready.sem, act_ready.at(t + 1))
                    v.link(dve.tensor_reduce(stat[:, 8:16], top, AX_X, ALU.add))
                    v.link(dve.reciprocal(stat[:, 16:24], stat[:, 8:16]))
                    r = stat[:, 16:24].unsqueeze(2).to_broadcast([P, PEER_HEADS, TOPK])
                    v.link(dve.tensor_tensor(top, top, r, ALU.mult))
                for u in range(2):
                    dve.wait_ge(unit_free[u].sem, unit_free[u].at(1 + tiles // 2))
                dst, bias = modcol[:, l, 72 - 4 * tiles:], vcol[:, 1 + l, V_BMOD + 72 - 4 * tiles:V_BMOD + 72]
                v.tick(dve.tensor_tensor(dst, dst, bias.unsqueeze(2).to_broadcast([P, 4 * tiles, 2]),
                                         ALU.add))
        vec_ready.base += TT
        act_ready.base += TT
        units_used(tiles)
        mod_rows.base += tiles
        mod_turned.base += tiles
        weights.end()

    TURN = 2 * TOPK
    HEADS = 2 * TT * PEER_HEADS

    class Experts:

        def __init__(self, l, hf_tok, index, gate, grow, acts, small):
            self.hf_tok, self.index, self.gate, self.grow, self.acts = hf_tok, index, gate, grow, acts
            self.y = hf_tok
            self.tables = [a[name].rearrange("l n d -> (l n) d") for name in ("peer_u", "peer_v")]
            self.index_cells = small[:, 0:32].rearrange("p (a k) -> p a k", a=2).bitcast(U32)
            self.cell = small[:, 32:48]
            self.tick, self.zero = small[:, 96:97].bitcast(U32), small[:, 97:98].bitcast(U32)
            self.done, self.fetched = 0, 0

        def fetch(self, gp, heads):
            end = HEADS * TOPK
            upto = min(end, (self.done + heads) * TOPK + GR)
            at = self.fetched
            half_way = end // 2
            turns = (upto - at) // TURN
            if turns >= 3 and at >= half_way:
                self.fetch_loop(gp, at, turns)
                at += turns * TURN
            for slot in range(at, upto):
                gp.wait_ge(row_used.sem, row_used.at(slot + 1))
                k = slot % half_way
                gp.indirect_dma_start(
                    self.grow[:, slot % GR, :], None, self.tables[slot // half_way],
                    bass.IndirectOffsetOnAxis(ap=self.index[:, k:k + 1], axis=0)) \
                  .then_inc(row_landed[slot % GR].sem, 16)
            self.fetched = upto

        def fetch_loop(self, gp, first, turns):
            p_ = Steps(gp, pool_step)
            p_.tick(gp.memset(self.tick, 0))
            p_.link(gp.memset(self.zero, 0))

            def turn(i):
                for half in range(2):
                    at = bass.ds(i * TURN + (first % (HEADS * TOPK // 2) + half * TOPK), TOPK)
                    p_.tick(gp.tensor_copy(self.index_cells[:, half, :], self.index[:, at]))
                    for k in range(TOPK):
                        slot = half * TOPK + k
                        if k % 2 == 0:
                            p_.wait()
                            gp.wait_ge(row_used.sem, i * TURN + row_used.at(first + slot + 2))
                            p_.tick(gp.tensor_tensor(self.tick, self.tick, self.zero, ALU.add))
                        gp.indirect_dma_start(
                            self.grow[:, (first + slot) % GR, :], None, self.tables[1],
                            bass.IndirectOffsetOnAxis(ap=self.index_cells[:, half, k:k + 1], axis=0)) \
                          .then_inc(row_landed[(first + slot) % GR].sem, 16)
            p_.loop(turns, 2 + TOPK, turn)

        def use(self, dve, head, first, last, turn=0):
            q = self.done + head
            up, t = q // (HEADS // 2), q // PEER_HEADS % TT
            at = bass.ds(turn * TOPK + q % (HEADS // 2) * TOPK, TOPK)
            if first == 0 and not up:
                dve.wait_ge(dots_kept.sem, turn + dots_kept.at(q + 1))
            if first == 0 and up:
                dve.wait_ge(row_used.sem, turn * TOPK + row_used.at(GR + q * TOPK))
                dve.tensor_copy(self.cell, self.acts[:, at]).then_inc(dots_kept.sem, 1)
                dve.wait_ge(dots_kept.sem, turn + dots_kept.at(q + 2))
            for k in range(first, last):
                dve.wait_ge(row_landed[k % GR].sem,
                            turn * (16 * TOPK // GR)
                            + row_landed[k % GR].at(16 * (q * TOPK // GR + k // GR + 1)))
                row, cell = self.grow[:, k % GR, :], self.cell[:, k:k + 1]
                if up:
                    dve.wait_ge(row_used.sem, turn * TOPK + row_used.at(GR + q * TOPK + k))
                    dve.scalar_tensor_tensor(out=self.y[:, t, :], in0=row, scalar=cell,
                                             in1=self.y[:, t, :], op0=ALU.mult, op1=ALU.add) \
                       .then_inc(row_used.sem, 1)
                else:
                    dve.tensor_tensor_reduce(row, row, self.hf_tok[:, t, :], 1.0, 0.0,
                                             ALU.mult, ALU.add, cell).then_inc(row_used.sem, 1)
            if last == TOPK and not up:
                dve.wait_ge(row_used.sem, turn * TOPK + row_used.at(GR + (q + 1) * TOPK))
                dve.tensor_copy(self.acts[:, at], self.cell).then_inc(dots_kept.sem, 1)

        def end_phase(self, heads):
            self.done += heads

        def alone(self, heads):
            with nc.Block() as block:
                fetching(block, self, heads)

                @block.vector
                def _(dve):
                    head = 0
                    while head < heads:
                        n = min(heads - head, PEER_HEADS - (self.done + head) % PEER_HEADS)
                        with dve.Fori(0, n) as i:
                            self.use(dve, head, 0, TOPK, i)
                        head += n
            self.end_phase(heads)

        def weigh(self):
            assert self.done == HEADS // 2
            with nc.Block() as block:
                @block.scalar
                def _(act):
                    act.activation(self.acts, self.acts, ACT.Gelu).then_inc(act_ready.sem, 1)

                @block.vector
                def _(dve):
                    v = Steps(dve, vec_step)
                    v.tick(dve.memset(self.y, 0.0))
                    dve.wait_ge(act_ready.sem, act_ready.at(1))
                    v.link(dve.tensor_tensor(self.acts, self.acts,
                                             self.gate.rearrange("p t h k -> p (t h k)"), ALU.mult))
            act_ready.base += 1

        def end(self):
            assert self.done == HEADS
            row_used.base += HEADS * TOPK
            dots_kept.base += HEADS
            for s_ in range(GR):
                row_landed[s_].base += 16 * HEADS * TOPK // GR

    def fetching(block, experts, heads):
        if experts is not None:
            @block.gpsimd
            def _(gp):
                experts.fetch(gp, heads)

    def peer_end(l, y):
        ahead = weights.first_tile(weights.group())
        with nc.Block() as block:
            @block.sync
            def _(sp):
                load_rows(sp, l, 1)

            @block.tensor
            def _(pe):
                broadcast_row(pe, lambda c: adacol[:, l, 40 + c:41 + c], 3).then_inc(pe_done.sem, 1)

            @block.scalar
            def _(act):
                act.wait_ge(pe_done.sem, pe_done.at(1))
                act.copy(rows[:, 0, :], ps[:, 3, :]).then_inc(act_ready.sem, 1)
                act.wait_ge(vec_ready.sem, vec_ready.at(1))
                act.activation(stat[:, 6:8], stat[:, 4:6], ACT.Sqrt).then_inc(act_ready.sem, 1)
                weights.split_hi(act, ahead)

            @block.vector
            def _(dve):
                v = Steps(dve, vec_step)
                dve.wait_ge(act_ready.sem, act_ready.at(1))
                dve.wait_ge(loaded.sem, loaded.at(32))
                pieces = [(t, k * 512, y[:, t, k * 512:(k + 1) * 512])
                          for k in range(2) for t in range(TT)]
                residual_norm(dve, 2, v, pieces, rows[:, 0, :], rows[:, 1, :], rows[:, 2, :])
                weights.split_lo(dve, ahead)
        loaded.base += 32
        pe_done.base += 1
        act_ready.base += 2
        vec_ready.base += 1

    def gate_up(name, h, hff, silu, prod, experts=None, heads=0):
        weights.begin(f"gu_{name}")
        split = weights.group().split
        with nc.Block() as block:
            @block.sync
            def _(sp):
                weights.feed(sp)

            fetching(block, experts, heads)

            @block.tensor
            def _(pe):
                def tile(t, j, turn):
                    unit_wait(pe, j, turn)
                    project_features(pe, t, blocks_of(j), h, j, turn)
                in_pairs(11, pe, tile)

            @block.scalar
            def _(act):
                def tile(t, j, turn):
                    split_ahead(act=act, tile=(t, j, turn))
                    product_wait(act, t)
                    unit_wait(act, j, turn)
                    act.activation(silu[:, j, :], ps[:, j, 0:512], ACT.Silu) \
                       .then_inc(act_ready.sem, 1)
                with_last(11, act, tile)

            @block.vector
            def _(dve):
                v = Steps(dve, vec_step)
                start = v.n

                def tile(t, j, turn):
                    split_ahead(dve=dve, tile=(t, j, turn))
                    if experts is not None and not isinstance(t, int):
                        experts.use(dve, 0, 8 * j, 8 * j + 8, turn)
                    dve.wait_ge(act_ready.sem, act_ready.at(1) + t)
                    at = bass.ds(t * 512, 512)
                    if not split:
                        dve.tensor_tensor(hff[0][:, at], silu[:, j, :], ps[:, j, 512:1024],
                                          ALU.mult).then_inc(unit_free[j].sem, 1)
                    else:
                        dve.tensor_tensor(prod[:, j, :], silu[:, j, :], ps[:, j, 512:1024],
                                          ALU.mult).then_inc(unit_free[j].sem, 1)
                        dve.wait_ge(unit_free[j].sem, turn + unit_free[j].at(2))
                        v.n = start + 2 * t
                        v.link(dve.tensor_copy(hff[0][:, at], prod[:, j, :]))
                        v.tick(dve.tensor_tensor(hff[1][:, at], prod[:, j, :],
                                                 hff[0][:, at].bitcast(F32), ALU.subtract))
                with_last(11, dve, tile)
                vec_step.base = start + (2 * 11 if split else 0)
        if experts is not None:
            experts.end_phase(heads)
        act_ready.base += 11
        units_used(11)
        weights.end()

    def gate_columns(dve, gate, gain, weight):
        dve.scalar_tensor_tensor(out=bcol[:], in0=gate, scalar=weight, in1=gain,
                                 op0=ALU.mult, op1=ALU.mult).then_inc(cols_ready.sem, 1)

    def gate_row(pe):
        pe.wait_ge(cols_ready.sem, cols_ready.at(1))
        broadcast_row(pe, lambda c: bcol[:, c:c + 1], 3).then_inc(pe_done.sem, 1)

    def squares(act, g, width):
        act.wait_ge(unit_free[g % 2].sem, unit_free[g % 2].at(2 + g // 2))
        for t in range(TT):
            act.activation(rows[:, 1 + t, 0:width], y_tok[:, t, g * width:(g + 1) * width],
                           ACT.Square, accum_out=stat[:, 32 + 4 * t + g:33 + 4 * t + g])

    def add_and_norm(tok, parts_y, scale, shift, gain, full):
        normed = y_tok
        with nc.Block() as block:
            @block.tensor
            def _(pe):
                for t in range(TT):
                    pe.wait_ge(vec_ready.sem, vec_ready.at(4 + t))
                    for c in range(KC):
                        mm = pe.transpose(ps[:, t, c * P:(c + 1) * P],
                                          normed[:, t, c * P:(c + 1) * P], ident[:])
                    mm.then_inc(pe_done.sem, 1)

            @block.scalar
            def _(act):
                s_ = Steps(act, act_step)
                act.wait_ge(vec_ready.sem, vec_ready.at(1))
                act.activation(stat[:, 2:4], stat[:, 0:2], ACT.Sqrt, bias=eps[:], scale=1.0 / D) \
                   .then_inc(act_ready.sem, 1)
                for t in range(TT):
                    act.wait_ge(vec_ready.sem, vec_ready.at(2 + t))
                    s_.link(act.activation(rows[:, 1 + t, :], tok[:, t, :], ACT.Square,
                                           accum_out=stat[:, 8 + t:9 + t]))
                    act.activation(stat[:, 10 + t:11 + t], stat[:, 8 + t:9 + t], ACT.Sqrt,
                                   bias=eps[:], scale=1.0 / D).then_inc(act_ready.sem, 1)
                act.wait_ge(cols_ready.sem, cols_ready.at(1))
                act.wait_ge(pe_done.sem, pe_done.at(1))
                for c in range(KC):
                    s_.tick(act.activation(full[:, c, 0:P], ps[:, 0, c * P:(c + 1) * P], ACT.Identity,
                                           bias=shift(c), scale=scol[:, c:c + 1]))
                s_.wait()
                act.activation(hT_hi[:, :, 0:P], full[:, :, 0:P], ACT.Copy).then_inc(act_ready.sem, 1)

            @block.vector
            def _(dve):
                v = Steps(dve, vec_step)
                sums = stat[:, 32:40].rearrange("p (t g) -> p t g", g=4)[:, :, 0:parts_y]
                dve.tensor_reduce(stat[:, 0:2], sums, AX_X, ALU.add).then_inc(vec_ready.sem, 1)
                dve.scalar_tensor_tensor(out=scol[:], in0=scale, scalar=1.0, in1=gain,
                                         op0=ALU.add, op1=ALU.mult).then_inc(cols_ready.sem, 1)
                dve.wait_ge(act_ready.sem, act_ready.at(1))
                v.link(dve.reciprocal(stat[:, 4:6], stat[:, 2:4]))
                for t in range(TT):
                    v.link(dve.scalar_tensor_tensor(out=y_tok[:, t, :], in0=y_tok[:, t, :],
                                                    scalar=stat[:, 4 + t:5 + t], in1=ps[:, 3, :],
                                                    op0=ALU.mult, op1=ALU.mult))
                    dve.tensor_tensor(tok[:, t, :], tok[:, t, :], y_tok[:, t, :], ALU.add) \
                       .then_inc(vec_ready.sem, 1)
                for t in range(TT):
                    dve.wait_ge(act_ready.sem, act_ready.at(2 + t))
                    v.link(dve.reciprocal(stat[:, 12 + t:13 + t], stat[:, 10 + t:11 + t]))
                    dve.tensor_scalar(normed[:, t, :], tok[:, t, :], stat[:, 12 + t:13 + t], None,
                                      ALU.mult).then_inc(vec_ready.sem, 1)
                dve.wait_ge(cols_ready.sem, cols_ready.at(1))
                dve.wait_ge(pe_done.sem, pe_done.at(2))
                for c in range(KC):
                    v.tick(dve.tensor_scalar(full[:, c, P:SEQ], ps[:, 1, c * P:(c + 1) * P],
                                             scol[:, c:c + 1], shift(c), ALU.mult, ALU.add))
                v.wait()
                v.link(dve.tensor_copy(hT_hi[:, :, P:SEQ], full[:, :, P:SEQ]))
                dve.wait_ge(act_ready.sem, act_ready.at(4))
                v.tick(dve.tensor_tensor(hT_lo[:], full, hT_hi[:].bitcast(F32), ALU.subtract))
        cols_ready.base += 1
        pe_done.base += 2
        act_ready.base += 4
        vec_ready.base += 5

    def down(name, hff, experts=None, heads=0, row=None):
        weights.begin(f"down_{name}")
        width = 256

        def copy_group(eng, t):
            g = t // 2
            product_wait(eng, t)
            src = ps[:, g % 2, :].rearrange("p (t n) -> p t n", t=TT)[:, :, 0:width]
            copy_ = eng.copy if experts is not None else eng.tensor_copy
            copy_(y_tok[:, :, g * width:(g + 1) * width], src).then_inc(unit_free[g % 2].sem, 1)

        parts = [h.rearrange("p (c t) -> p c t", t=SEQ) for h in hff]
        with nc.Block() as block:
            @block.sync
            def _(sp):
                weights.feed(sp)

            fetching(block, experts, heads)

            @block.tensor
            def _(pe):
                if row is not None:
                    gate_row(pe)
                for t in range(8):
                    g, half = t // 2, t % 2
                    if half == 0:
                        unit_wait(pe, g % 2, g // 2)
                    project_tokens(pe, t, tiles_of(g % 2, width), parts, half * 11,
                                   opens=(half == 0), closes=(half == 1))

            @block.scalar
            def _(act):
                for t in range(8):
                    split_ahead(act=act, tile=(t, t % 2, t // 2))
                    if experts is not None and t % 2:
                        copy_group(act, t)
                    if row is not None and t % 2:
                        squares(act, t // 2, width)

            @block.vector
            def _(dve):
                if row is not None:
                    gate_columns(dve, *row)
                for t in range(8):
                    split_ahead(dve=dve, tile=(t, t % 2, t // 2))
                    if t % 2 and experts is None:
                        copy_group(dve, t)
                    if t // 2 < heads:
                        experts.use(dve, t // 2, 8 * (t % 2), 8 * (t % 2) + 8)
        if experts is not None:
            experts.end_phase(heads)
        if row is not None:
            cols_ready.base += 1
            pe_done.base += 1
        units_used(4)
        weights.end()

    def project_out(name, h, experts=None, heads=0, row=None):
        weights.begin(name)

        def copy_tile(eng, t):
            product_wait(eng, t)
            copy_ = eng.copy if experts is not None else eng.tensor_copy
            copy_(y_tok[:, :, t * 512:(t + 1) * 512],
                  ps[:, t, :].rearrange("p (t n) -> p t n", t=TT)).then_inc(unit_free[t].sem, 1)

        with nc.Block() as block:
            @block.sync
            def _(sp):
                weights.feed(sp)

            fetching(block, experts, heads)

            @block.tensor
            def _(pe):
                if row is not None:
                    gate_row(pe)
                for t in range(2):
                    unit_wait(pe, t, 0)
                    project_tokens(pe, t, tiles_of(t), h)

            @block.scalar
            def _(act):
                for t in range(2):
                    split_ahead(act=act, tile=(t, t, 0))
                    if experts is not None:
                        copy_tile(act, t)
                    if row is not None:
                        squares(act, t, 512)

            @block.vector
            def _(dve):
                if row is not None:
                    gate_columns(dve, *row)
                for t in range(2):
                    split_ahead(dve=dve, tile=(t, t, 0))
                    if experts is None:
                        copy_tile(dve, t)
                    if heads:
                        experts.use(dve, 0, 8 * t, 8 * t + 8)
        if experts is not None:
            experts.end_phase(heads)
        if row is not None:
            cols_ready.base += 1
            pe_done.base += 1
        units_used(2)
        weights.end()

    def context_add(parts_y, experts, heads):
        with nc.Block() as block:
            fetching(block, experts, heads)

            @block.scalar
            def _(act):
                act.wait_ge(vec_ready.sem, vec_ready.at(1))
                act.activation(stat[:, 2:4], stat[:, 0:2], ACT.Sqrt, bias=eps[:], scale=1.0 / D) \
                   .then_inc(act_ready.sem, 1)

            @block.vector
            def _(dve):
                v = Steps(dve, vec_step)
                sums = stat[:, 32:40].rearrange("p (t g) -> p t g", g=4)[:, :, 0:parts_y]
                dve.tensor_reduce(stat[:, 0:2], sums, AX_X, ALU.add).then_inc(vec_ready.sem, 1)
                dve.wait_ge(act_ready.sem, act_ready.at(1))
                v.link(dve.reciprocal(stat[:, 4:6], stat[:, 2:4]))
                for t in range(TT):
                    v.link(dve.scalar_tensor_tensor(out=y_tok[:, t, :], in0=y_tok[:, t, :],
                                                    scalar=stat[:, 4 + t:5 + t], in1=ps[:, 3, :],
                                                    op0=ALU.mult, op1=ALU.mult))
                    v.tick(dve.tensor_tensor(z_tok[:, t, :], z_tok[:, t, :], y_tok[:, t, :], ALU.add))
                for head in range(heads):
                    experts.use(dve, head, 0, TOPK)
        experts.end_phase(heads)
        vec_ready.base += 1
        act_ready.base += 1

    def add_normed(tok, gate, gain, weight):
        junk = rows[:, 1:3, :]
        with nc.Block() as block:
            @block.vector
            def _(dve):
                v = Steps(dve, vec_step)
                dve.scalar_tensor_tensor(out=scol[:], in0=gate, scalar=weight, in1=gain,
                                         op0=ALU.mult, op1=ALU.mult).then_inc(cols_ready.sem, 1)
                for t in range(TT):
                    v.tick(dve.tensor_tensor_reduce(junk[:, t, :], y_tok[:, t, :], y_tok[:, t, :],
                                                    1.0, 0.0, ALU.mult, ALU.add, stat[:, t:t + 1]))
                v.wait()
                dve.tensor_scalar(stat[:, 0:2], stat[:, 0:2], 1.0 / D, RMS_EPS, ALU.mult, ALU.add) \
                   .then_inc(vec_ready.sem, 1)
                dve.wait_ge(act_ready.sem, act_ready.at(1))
                v.link(dve.reciprocal(stat[:, 4:6], stat[:, 2:4]))
                dve.wait_ge(pe_done.sem, pe_done.at(1))
                for t in range(TT):
                    v.link(dve.scalar_tensor_tensor(out=y_tok[:, t, :], in0=y_tok[:, t, :],
                                                    scalar=stat[:, 4 + t:5 + t], in1=ps[:, 3, :],
                                                    op0=ALU.mult, op1=ALU.mult))
                    v.link(dve.tensor_tensor(tok[:, t, :], tok[:, t, :], y_tok[:, t, :], ALU.add))

            @block.tensor
            def _(pe):
                pe.wait_ge(cols_ready.sem, cols_ready.at(1))
                broadcast_row(pe, lambda c: scol[:, c:c + 1], 3).then_inc(pe_done.sem, 1)

            @block.scalar
            def _(act):
                act.wait_ge(vec_ready.sem, vec_ready.at(1))
                act.activation(stat[:, 2:4], stat[:, 0:2], ACT.Sqrt).then_inc(act_ready.sem, 1)
        cols_ready.base += 1
        vec_ready.base += 1
        act_ready.base += 1
        pe_done.base += 1

    def mod_cols(l, k, s):
        return modcol[:, l, k * KC:(k + 1) * KC, s]

    def gain_cols(l, k):
        at = V_NG + (l * 6 + k) * KC
        return vcol[:, 3, at:at + KC]

    def norm_in(l, k, gain):
        (full,) = carve((KC, SEQ))
        modulated_features(x_tok, mod_cols(l, k + 1, 0), lambda c: modcol[:, l, k * KC + c, 0:1],
                           full, gain_cols(l, gain))

    def context_norm_in(l, k, gain, full, experts, heads):
        context_norm(mod_cols(l, k + 1, 1), lambda c: modcol[:, l, k * KC + c, 1:2],
                     gain_cols(l, gain), full, experts, heads)

    def enter(before, l, k, gain):
        if before is None:
            norm_in(l, k, gain)
        else:
            (full,) = carve((KC, SEQ))
            add_and_norm(x_tok, before, mod_cols(l, k + 1, 0),
                         lambda c: modcol[:, l, k * KC + c, 0:1], gain_cols(l, gain), full)

    def ffn(name, before, l, k, gain, last=False):
        begin_stretch(f"ffn_{name}", 2048, 2 * D_FF * TT)
        hff = carve((D_FF * TT,), (D_FF * TT,), of=parts)
        silu, prod = carve((2, 512), (2, 512))
        enter(before, l, k, gain)
        gate_up(name, hT, hff, silu, prod)
        row = mod_cols(l, k + 2, 0), gain_cols(l, gain + 1), 0.5
        if last:
            down(name, hff)
            add_normed(x_tok, *row)
            return None
        down(name, hff, row=row)
        return 4

    def context_ffn(name, l, k, gain, experts, heads):
        h, hff = carve((KC, SEQ), (D_FF * TT,), of=parts)
        silu = rows[:, 0, :].rearrange("p (u n) -> p u n", u=2)
        context_norm_in(l, k, gain, h, experts, heads[0])
        gate_up(name, (h,), (hff,), silu, None, experts, heads[1])
        down(name, (hff,), experts, heads[2], (mod_cols(l, k + 2, 1), gain_cols(l, gain + 1), 0.5))
        context_add(4, experts, heads[3])

    def conv_projection(name, h, b_gate, u, up, experts=None, heads=0):
        weights.begin(f"conv_{name}")
        with nc.Block() as block:
            @block.sync
            def _(sp):
                weights.feed(sp)

            fetching(block, experts, heads)

            @block.tensor
            def _(pe):
                for t in range(6):
                    unit_wait(pe, t % 2, t // 2)
                    project_features(pe, t, blocks_of(t % 2), h)

            @block.scalar
            def _(act):
                for t in range(6):
                    split_ahead(act=act, tile=(t, t % 2, t // 2))
                    if t < 2 and experts is not None:
                        product_wait(act, t)
                        act.copy(b_gate[:, 4 * t:4 * t + 4, :],
                                 ps[:, t % 2, :].rearrange("p (b t) -> p b t", t=SEQ)) \
                           .then_inc(unit_free[t % 2].sem, 1)
                    if t not in (2, 3):
                        continue
                    product_wait(act, t)
                    act.copy(u[:, 4 * (t - 2):4 * (t - 1), :],
                             ps[:, t % 2, :].rearrange("p (b t) -> p b t", t=SEQ)) \
                       .then_inc(unit_free[t % 2].sem, 1)

            @block.vector
            def _(dve):
                v = Steps(dve, vec_step)
                v.tick(dve.memset(up[:, :, 0:1], 0.0))
                v.tick(dve.memset(up[:, :, SEQ + 1:SEQ + 2], 0.0))
                for t in range(6):
                    split_ahead(dve=dve, tile=(t, t % 2, t // 2))
                    if t // 2 < heads:
                        experts.use(dve, t // 2, 8 * (t % 2), 8 * (t % 2) + 8)
                    if t in (2, 3) or t < 2 and experts is not None:
                        continue
                    product_wait(dve, t)
                    src = ps[:, t % 2, :].rearrange("p (b t) -> p b t", t=SEQ)
                    if t < 2:
                        dve.tensor_copy(b_gate[:, 4 * t:4 * t + 4, :], src).then_inc(unit_free[t % 2].sem, 1)
                    else:
                        at = slice(4 * (t - 4), 4 * (t - 3))
                        dve.tensor_tensor(up[:, at, 1:SEQ + 1], u[:, at, :], src, ALU.mult) \
                           .then_inc(unit_free[t % 2].sem, 1)
        if experts is not None:
            experts.end_phase(heads)
        units_used(6)
        weights.end()

    def conv_taps(b_gate, up, y, h=None, experts=None, heads=0):
        with nc.Block() as block:
            fetching(block, experts, heads)

            @block.vector
            def _(dve):
                v = Steps(dve, vec_step)

                def tap(k, c):
                    if k == 2:
                        return vcol[:, 1, 72 + c:73 + c]
                    at = V_CW + k * KC + c
                    return vcol[:, 3, at:at + 1]
                for c in range(KC):
                    v.tick(dve.tensor_scalar(y[:, c, :], up[:, c, 0:SEQ], tap(0, c), None, ALU.mult))
                for k in (1, 2):
                    v.wait()
                    for c in range(KC):
                        v.tick(dve.scalar_tensor_tensor(
                            out=y[:, c, :], in0=up[:, c, k:k + SEQ], scalar=tap(k, c), in1=y[:, c, :],
                            op0=ALU.mult, op1=ALU.add))
                v.wait()
                if h is not None:
                    v.tick(dve.tensor_tensor(h, y, b_gate, ALU.mult))
                    for head in range(heads):
                        experts.use(dve, head, 0, TOPK)
                    return
                dve.tensor_tensor(y, y, b_gate, ALU.mult).then_inc(vec_ready.sem, 1)
                dve.wait_ge(act_ready.sem, act_ready.at(1))
                v.tick(dve.tensor_tensor(hT_lo[:], y, hT_hi[:].bitcast(F32), ALU.subtract))

            if h is None:
                @block.scalar
                def _(act):
                    act.wait_ge(vec_ready.sem, vec_ready.at(1))
                    act.activation(hT_hi[:], y, ACT.Copy).then_inc(act_ready.sem, 1)
        if experts is not None:
            experts.end_phase(heads)
        if h is None:
            vec_ready.base += 1
            act_ready.base += 1

    def conv(before):
        begin_stretch("conv_x", 8208, 0)
        b_gate, u, up, y = carve((KC, SEQ), (KC, SEQ), (KC, SEQ + 2), (KC, SEQ))
        enter(before, 0, 3, 2)
        conv_projection("x", hT, b_gate, u, up)
        conv_taps(b_gate, up, y)
        project_out("convout_x", hT, row=(mod_cols(0, 5, 0), gain_cols(0, 3), 1.0))
        return 2

    def context_conv(experts):
        h, b_gate, up = carve((KC, SEQ), (KC, SEQ), (KC, SEQ + 2), of=parts)
        u = rows[:, 1:3, :].rearrange("p k (c t) -> p (k c) t", t=SEQ)
        context_norm_in(0, 3, 2, h, experts, 1)
        conv_projection("z", (h,), b_gate, u, up, experts, 3)
        conv_taps(b_gate, up, u, h, experts, 1)
        project_out("convout_z", (h,), experts, 1, (mod_cols(0, 5, 1), gain_cols(0, 3), 1.0))
        experts.weigh()
        context_add(2, experts, 1)

    def rotate(dve, v, t, heads, out_, src, cos, sin, tmp):
        s5 = src.rearrange("p h (a two q) -> p h a two q", a=2, two=2)
        o5 = out_.rearrange("p h (a two q) -> p h a two q", a=2, two=2)
        t4 = tmp.rearrange("p (h a q) -> p h a q", a=2, q=16)
        shape = [P, heads, 2, 16]
        c4 = cos[:, t].unsqueeze(1).to_broadcast(shape)
        n4 = sin[:, t].unsqueeze(1).to_broadcast(shape)
        for half, op in ((0, ALU.subtract), (1, ALU.add)):
            mine, other = s5[:, :, :, half, :], s5[:, :, :, 1 - half, :]
            v.link(dve.tensor_tensor(t4, other, n4, ALU.mult))
            v.link(dve.tensor_tensor(o5[:, :, :, half, :], mine, c4, ALU.mult))
            v.link(dve.tensor_tensor(o5[:, :, :, half, :], o5[:, :, :, half, :], t4, op))

    def context_keys(h, kz, vz, kzT, experts, heads):
        weights.begin("kv_z")
        with nc.Block() as block:
            @block.sync
            def _(sp):
                weights.feed(sp)

            fetching(block, experts, heads)

            @block.tensor
            def _(pe):
                for t in range(2):
                    project_tokens(pe, t, tiles_of(2 * t, 256), (h,))
                pe.wait_ge(vec_ready.sem, vec_ready.at(1))
                for c in range(4):
                    for t in range(TT):
                        mm = pe.transpose(ps[:, 1, c * SEQ + t * P:c * SEQ + (t + 1) * P],
                                          kz[:, t, 2 * c:2 * c + 2, :], ident[:])
                mm.then_inc(pe_done.sem, 1)

            @block.scalar
            def _(act):
                for t in range(2):
                    split_ahead(act=act, tile=(t, t, 0))

            @block.vector
            def _(dve):
                v = Steps(dve, vec_step)
                for t in range(2):
                    split_ahead(dve=dve, tile=(t, t, 0))
                product_wait(dve, 1)
                k_src, v_src = [ps[:, u, :].rearrange("p (t n) -> p t n", t=TT)[:, :, 0:256]
                                for u in (0, 2)]
                copy_keys(dve, v, kz, 0, k_src)
                dve.tensor_copy(vz, v_src).then_inc(vec_ready.sem, 1)
                dve.wait_ge(pe_done.sem, pe_done.at(1))
                dve.tensor_copy(kzT.rearrange("p c t -> p (c t)"), ps[:, 1, :])
                for head in range(heads):
                    experts.use(dve, head, 0, TOPK)
        experts.end_phase(heads)
        vec_ready.base += 1
        pe_done.base += 1
        weights.end()

    def copy_keys(dve, v, dst, head0, src):
        for t in range(TT):
            k4 = src[:, t, 0:256].rearrange("p (h d) -> p h d", d=HD)
            v.tick(dve.tensor_copy(dst[:, t, head0:head0 + 4, :], k4))
            pairs = src[:, t, 0:256].rearrange("p (c two d) -> p c two d", two=2, d=HD)
            out4 = dst[:, t, head0 + 4:head0 + 8, :].rearrange("p (c two) d -> p c two d", two=2)
            for e in range(2):
                v.tick(dve.tensor_copy(out4[:, :, e, :], pairs[:, :, 1 - e, :]))
        v.wait()

    def queries_and_keys(qk, rot, vx, qkT, cos, sin, tmp):
        heads = NQ + 2 * NKV
        weights.begin("qkv")
        with nc.Block() as block:
            @block.sync
            def _(sp):
                sp.dma_start(cos, a["k_cos"]).then_inc(loaded.sem, 16)
                sp.dma_start(sin, a["k_sin"]).then_inc(loaded.sem, 16)
                weights.feed(sp)

            @block.tensor
            def _(pe):
                for t in range(3):
                    project_tokens(pe, t, tiles_of(t), hT)
                pe.wait_ge(vec_ready.sem, vec_ready.at(1))
                for u in range(3):
                    for c in range(4):
                        for t in range(TT):
                            h = 8 * u + 2 * c
                            mm = pe.transpose(ps[:, u, c * SEQ + t * P:c * SEQ + (t + 1) * P],
                                              rot[:, t, h:h + 2, :], ident[:])
                    mm.then_inc(pe_done.sem, 1)

            @block.scalar
            def _(act):
                for k in range(2):
                    split_ahead(act=act, tile=(k, k, 0))
                    product_wait(act, k)
                    for t in range(TT):
                        ins = act.activation(qk[:, t, 8 * k:8 * k + 8, :],
                                             ps[:, k, t * 512:(t + 1) * 512].rearrange(
                                                 "p (h d) -> p h d", d=HD),
                                             ACT.Copy, scale=HD ** -0.5)
                ins.then_inc(act_ready.sem, 1)
                split_ahead(act=act, tile=(2, 0, 1))
                for u in range(3):
                    act.wait_ge(pe_done.sem, pe_done.at(u + 1))
                    act.copy(qkT[:, 4 * u:4 * u + 4, :].rearrange("p c t -> p (c t)"), ps[:, u, :])

            @block.vector
            def _(dve):
                v = Steps(dve, vec_step)
                for t in range(3):
                    split_ahead(dve=dve, tile=(t, t % 2, t // 2))
                product_wait(dve, 2)
                src = ps[:, 2, :].rearrange("p (t n) -> p t n", t=TT)
                copy_keys(dve, v, qk, NQ, src)
                v.tick(dve.tensor_copy(vx, src[:, :, 256:512]))
                dve.wait_ge(act_ready.sem, act_ready.at(1))
                dve.wait_ge(loaded.sem, loaded.at(32))
                for t in range(TT):
                    rotate(dve, v, t, heads, rot[:, t], qk[:, t], cos, sin, tmp)
                dve.memset(stat[:, 0:1], 0.0).then_inc(vec_ready.sem, 1)
        loaded.base += 32
        vec_ready.base += 1
        act_ready.base += 1
        pe_done.base += 3
        weights.end()

    def window_attention(qkT, kzT, vx, vz, s, pT, band, sink):
        with nc.Block() as block:
            @block.sync
            def _(sp):
                sp.dma_start(band, a["k_band"]).then_inc(loaded.sem, 16)
                sp.dma_start(sink, a["attn_sink_2"].to_broadcast([P, NQ])).then_inc(loaded.sem, 16)

            @block.tensor
            def _(pe):
                def scores(h):
                    if h >= 2:
                        pe.wait_ge(masked.sem, masked.at(h - 1))
                    kv = h // (NQ // NKV)
                    same = h % 2 == kv % 2
                    at = slice(64 * (h % 2), 64 * (h % 2) + 64)
                    kx = qkT[at, 8 + kv // 2 + (0 if same else 2), :]
                    kz = kzT[at, kv // 2 + (0 if same else 2), :]
                    for t in range(TT):
                        q = qkT[at, h // 2, t * P:(t + 1) * P]
                        pe.matmul(ps[:, h % 2, t * 512:t * 512 + 256], q, kx, start=True, stop=True)
                        mm = pe.matmul(ps[:, h % 2, t * 512 + 256:(t + 1) * 512], q, kz,
                                       start=True, stop=True)
                    mm.then_inc(pe_done.sem, 1)

                scores(0)
                scores(1)
                for h in range(NQ):
                    if h + 2 < NQ:
                        scores(h + 2)
                    pe.wait_ge(normalised.sem, normalised.at(h + 1))
                    for c in range(4):
                        for t in range(TT):
                            mm = pe.transpose(ps[:, 2, c * SEQ + t * P:c * SEQ + (t + 1) * P],
                                              s[:, h % 3, t, c * P:(c + 1) * P], ident[:])
                    mm.then_inc(turned.sem, 1)
                    pe.wait_ge(act_ready.sem, act_ready.at(h + 1))
                    if h == 8:
                        pe.wait_ge(cols_ready.sem, cols_ready.at(1))
                    kv = h // (NQ // NKV)
                    dst = ps[64 * (h % 2):64 * (h % 2) + 64, 3,
                             (h % 8 // 2) * SEQ:(h % 8 // 2 + 1) * SEQ]
                    for c in range(4):
                        values = (vx if c < 2 else vz)[:, c % 2, kv * HD:(kv + 1) * HD]
                        mm = pe.matmul(dst, values, pT[:, c, :], start=(c == 0), stop=(c == 3),
                                       skip_group_check=True)
                    mm.then_inc(summed.sem, 1)

            @block.scalar
            def _(act):
                def turn_out(h):
                    act.wait_ge(turned.sem, turned.at(h + 1))
                    if h >= 1:
                        act.wait_ge(summed.sem, summed.at(h))
                    act.copy(pT.rearrange("p c t -> p (c t)"), ps[:, 2, :]) \
                       .then_inc(act_ready.sem, 1)

                for h in range(NQ):
                    act.wait_ge(vec_ready.sem, vec_ready.at(h + 1))
                    b = 8 * (h % 3)
                    for t in range(TT):
                        act.activation(s[:, h % 3, t, :], s[:, h % 3, t, :], ACT.Exp,
                                       bias=stat[:, b + t:b + t + 1],
                                       accum_out=stat[:, b + 2 + t:b + 3 + t])
                    act.activation(stat[:, b + 4:b + 6], stat[:, b:b + 2], ACT.Exp,
                                   bias=sink[:, h:h + 1]).then_inc(expd.sem, 1)
                    if h:
                        turn_out(h - 1)
                turn_out(NQ - 1)

            @block.vector
            def _(dve):
                v = Steps(dve, vec_step)
                dve.wait_ge(loaded.sem, loaded.at(32))
                def mask(h):
                    b = 8 * (h % 3)
                    dve.wait_ge(pe_done.sem, pe_done.at(h + 1))
                    if h >= 3:
                        dve.wait_ge(turned.sem, turned.at(h - 2))
                    dve.tensor_tensor(s[:, h % 3], ps[:, h % 2, :].rearrange("p (t n) -> p t n", t=TT),
                                      band, ALU.add).then_inc(masked.sem, 1)
                    dve.wait_ge(masked.sem, masked.at(h + 1))
                    v.link(dve.tensor_reduce(stat[:, b:b + 2], s[:, h % 3], AX_X, ALU.max))
                    dve.tensor_scalar(stat[:, b:b + 2], stat[:, b:b + 2], sink[:, h:h + 1], -1.0,
                                      ALU.max, ALU.mult).then_inc(vec_ready.sem, 1)

                mask(0)
                for h in range(NQ):
                    if h + 1 < NQ:
                        mask(h + 1)
                    b = 8 * (h % 3)
                    dve.wait_ge(expd.sem, expd.at(h + 1))
                    v.link(dve.tensor_tensor(stat[:, b + 6:b + 8], stat[:, b + 2:b + 4],
                                             stat[:, b + 4:b + 6], ALU.add))
                    v.link(dve.reciprocal(stat[:, b + 6:b + 8], stat[:, b + 6:b + 8]))
                    dve.tensor_tensor(s[:, h % 3], s[:, h % 3],
                                      stat[:, b + 6:b + 8].unsqueeze(2).to_broadcast([P, TT, 512]),
                                      ALU.mult).then_inc(normalised.sem, 1)
                    if h % 8 == 7:
                        dve.wait_ge(summed.sem, summed.at(h + 1))
                        hi, lo = [o[:, h // 8 * 4:h // 8 * 4 + 4, :].rearrange("p c t -> p (c t)")
                                  for o in hT]
                        v.link(dve.tensor_copy(hi, ps[:, 3, :]))
                        dve.tensor_tensor(lo, ps[:, 3, :], hi.bitcast(F32), ALU.subtract) \
                           .then_inc(cols_ready.sem, 1)
        loaded.base += 32
        pe_done.base += NQ
        turned.base += NQ
        summed.base += NQ
        for signal_ in (vec_ready, act_ready, masked, normalised, expd):
            signal_.base += NQ
        cols_ready.base += 2

    ada_modulation(0)

    for l in range(DEPTH):
        begin_stretch(f"layer{l}", 11264, 4096, 1024)
        (qa, sg, km, ia, ga, qb, kb, vb, work) = carve(
            (4, SEQ), (4, SEQ), (4, SEQ), (TT, 512), (TT, 512), (4, SEQ), (4, SEQ), (TT, 512),
            (3072,))
        oa_hi, oa_lo, ob_hi, ob_lo = carve((4, SEQ), (4, SEQ), (4, SEQ), (4, SEQ), of=parts)
        modulated_features(x_tok, adacol[:, l, 8:16], lambda c: adacol[:, l, c:c + 1],
                           arena[:, 0:2048].rearrange("p (c t) -> p c t", t=SEQ))
        input_projection(l, qa, sg, km, ia, ga, qb, kb, vb)
        oaT, obT = (oa_hi, oa_lo), (ob_hi, ob_lo)
        ke, scores, cross = work[:, 0:1024], work[:, 1024:2048], work[:, 2048:2560]
        o, sq = y_tok[:, 0, :].rearrange("p (t n) -> p t n", t=TT), y_tok[:, 1, :]
        weights.begin(f"beside{l}")
        ada_cond, at = condT[:, :, 0:1], 4 * ADA_FIRST
        beside = SideModulation([
            (12 - ADA_FIRST, ada_cond, adacol[:, l, at:48].unsqueeze(2),
             vcol[:, 0, V_BADA + 48 * l + at:V_BADA + 48 * (l + 1)]),
            (ADA_FIRST, ada_cond, adacol[:, 1, 0:at].unsqueeze(2), vcol[:, 0, V_BADA + 48:V_BADA + 48 + at])
            if l == 0 else
            (MOD_BESIDE, condT[:, :, 1:3], modcol[:, 1, 0:4 * MOD_BESIDE],
             vcol[:, 2, V_BMOD:V_BMOD + 4 * MOD_BESIDE])])
        beside.tiles = BESIDE_MIXERS[l][0]
        hgrn(l, qa, sg, km, ia, ga, oaT,
             (rows[:, 0, :], rows[:, 1, :], rows[:, 2, :], ke, scores, cross, o, sq), beside)
        sbt = [v.rearrange("p (n w) -> p n w", n=4) for v in (
            work[:, 0:1536], work[:, 1536:3072],
            rows[:].rearrange("p k n -> p (k n)")[:, 0:1536])]
        beside.tiles = BESIDE_MIXERS[l][1]
        stick_breaking(qb, kb, vb, obT, sbt, beside)
        _, gates = carve((4096,), (2 * KC, SEQ))
        gate_projection(l, gates)
        merge(l, oaT, obT, gates)
        output_projection(l)

        hf_tok, index, gate, small, rest = carve((TT, D), (TT, PEER_HEADS, TOPK),
                                                 (TT, PEER_HEADS, TOPK), (128,), (8576,))
        modulated_features(x_tok, adacol[:, l, 32:40], lambda c: adacol[:, l, 24 + c:25 + c],
                           rest[:, 0:2048].rearrange("p (c t) -> p c t", t=SEQ))
        index = index.bitcast(U32)
        pqT = rest[:, 0:2048].rearrange("p (h t) -> p h t", h=PEER_HEADS)
        keys = rest[:, 2048:3072].rearrange("p (h t) -> p h t", h=PEER_HEADS)
        keysT = rest[:, 3072:4096].rearrange("p (h t) -> p h t", h=PEER_HEADS)
        sc = rest[:, 4096:8192].rearrange("p (t half n) -> p t half n", t=TT, half=2)
        best, bestf, pos, p12, sel = [y_tok[:, 0, k * 256:(k + 1) * 256] for k in range(4)] \
            + [y_tok[:, 1, 0:256]]
        best, bestf, pos = [x.rearrange("p (n k) -> p n k", k=TOPK) for x in (best, bestf, pos)]
        p12, sel = [x.rearrange("p (z h k) -> p z h k", z=2, k=TOPK) for x in (p12, sel)]
        pos, p12 = pos.bitcast(U32), p12.bitcast(U32)
        cand = rest[:, 0:2048].rearrange("p (h n) -> p h n", h=PEER_HEADS)
        eq = rest[:, 2048:4096].rearrange("p (h n) -> p h n", h=PEER_HEADS)
        peer_queries(l, hf_tok, pqT, keys, keysT, sc)
        peer_select(l, sc, best, bestf, cand, pos, p12, eq, sel, index, gate)
        grow = rest[:, 0:GR * D].rearrange("p (r n) -> p r n", r=GR)
        acts = rest[:, GR * D:GR * D + 256]
        flat_index = index.rearrange("p t h k -> p (t h k)")

        begin_parts(f"context_{l}", 2048 + D_FF * TT, F32)
        experts = Experts(l, hf_tok, flat_index, gate, grow, acts, small)
        if l == 0:
            context_ffn("z00", 0, 0, 0, experts, (1, 5, 3, 1))
            context_conv(experts)
            context_ffn("z01", 0, 6, 4, experts, (1, 5, 3, 1))
        else:
            context_ffn("z10", 1, 0, 0, experts, (1, 5, 3, 1))
            h, kz = carve((KC, SEQ), (TT, 2 * NKV, HD), of=parts)
            context_norm_in(1, 3, 2, h, experts, 1)
            context_keys(h, kz, context_v[:], context_kT[:], experts, 1)
            experts.alone(HEADS // 2 - experts.done)
            experts.weigh()
        experts.alone(HEADS - experts.done)
        experts.end()
        peer_end(l, hf_tok)

    left = ffn("x00", None, 0, 0, 0)
    left = conv(left)
    left = ffn("x01", left, 0, 6, 4)
    left = ffn("x10", left, 1, 0, 0)
    begin_stretch("attention", 12288, 0)
    enter(left, 1, 3, 2)
    qk, rot, vx, qkT, cos, sin, tmp = carve((TT, 24, HD), (TT, 24, HD), (TT, 256), (12, SEQ),
                                            (TT, 2, 16), (TT, 2, 16), (24 * 32,))
    queries_and_keys(qk, rot, vx, qkT, cos, sin, tmp)
    scores, pT, band, sink = carve((3, TT, 512), (4, SEQ), (TT, 512), (NQ,))
    window_attention(qkT, context_kT[:], vx, context_v[:], scores, pT, band, sink)
    project_out("attn_o", hT, row=(mod_cols(1, 5, 0), gain_cols(1, 3), 1.0))
    ffn("x11", 2, 1, 6, 4, last=True)

    with nc.Block() as block:
        @block.sync
        def _(sp):
            sp.dma_start(out[0].rearrange("(t p) d -> p t d", p=P), x_tok[:]).then_inc(stored.sem, 16)
            sp.wait_ge(stored.sem, 16)


def constants():
    i = np.arange(P)
    s, t = i[:, None], i[None, :]
    levels = [s == t] + [(s // (2 * m) == t // (2 * m)) & (s % (2 * m) < m) & (t % (2 * m) >= m)
                         for m in LEVELS]
    tok = np.arange(SEQ)
    grid_w, quarter = 64, HD // 4
    freq = (np.float32(10000.0) ** (-np.arange(quarter, dtype=np.float32) / np.float32(quarter)))
    ang = np.stack([(tok // grid_w).astype(np.float32)[:, None] * freq,
                    (tok % grid_w).astype(np.float32)[:, None] * freq], axis=1)
    table = lambda f: np.ascontiguousarray(
        f(ang).astype(np.float32).reshape(TT, P, 2, quarter).transpose(1, 0, 2, 3))
    band = np.zeros((P, TT, 512), np.float32)
    q = tok.reshape(TT, P).T
    band[:, :, 0:SEQ] = np.where(np.abs(tok[None, None, :] - q[:, :, None]) <= 128, 0.0, NEG)
    f = np.float32
    return {
        "k_ident": (s == t).astype(f),
        "k_tri": (s >= t).astype(f),
        "k_before": (s < t).astype(f),
        "k_before_neg": np.where(s < t, 0.0, NEG).astype(f),
        "k_levels": np.ascontiguousarray(np.stack(levels, 1).astype(np.uint32)),
        "k_iota16": np.tile(np.arange(TOPK, dtype=f), (P, 1)),
        "k_cos": table(np.cos),
        "k_sin": table(np.sin),
        "k_band": band,
    }


_INS = ["x", "c", "w_ada", "b_ada", "w_in", "lb_logits", "hg_norm_g", "w_up_a", "w_up_b", "w_o",
        "w_pq", "sub_keys", "peer_u", "peer_v", "ln_g", "ln_b", "c_2", "ctx_2", "c_ctx_2",
        "w_mod_2", "b_mod_2", "norm_g_2", "ffn_w_gu_2", "ffn_w_down_2", "conv_w_in_2", "conv_w_2",
        "conv_w_out_2", "attn_w_qkv_2", "attn_w_o_2", "attn_sink_2"]


def kernel(**inputs):
    import concourse.bacc as bacc
    from concourse.bass_utils import run_bass_kernel_spmd

    nc = bacc.Bacc("TRN2", target_bir_lowering=False, num_devices=1)
    arrays, aps = {}, {}
    for name, value in [(n, inputs[n]) for n in _INS] + list(constants().items()):
        value = np.ascontiguousarray(value)
        arrays[f"in_{name}"] = value
        aps[name] = nc.dram_tensor(f"in_{name}", value.shape, mybir.dt.from_np(value.dtype),
                                   kind="ExternalInput").ap()
    out = nc.dram_tensor("out", (1, SEQ, D), F32, kind="ExternalOutput").ap()
    build(nc, aps, out)
    r = run_bass_kernel_spmd(nc, [arrays], core_ids=[0])
    return r.results[0]["out"]
```
